# Optimizing a Trainium2 kernel written in Bass

```python
import math
import jax, jax.numpy as jnp
from jax import lax
import numpy as np

D_MODEL = 2048
BATCH = 1
SEQ = 256
DEPTH = 2

D_FOURIER = D_MODEL // 2
FOURIER_GROUPS = 8
FOURIER_GROUP_DIM = D_FOURIER // FOURIER_GROUPS
V_HEAD_DIM = 128
D_ATTN = D_MODEL // 2
N_HEADS = D_ATTN // V_HEAD_DIM
QK_NOPE_DIM = 128
QK_ROPE_DIM = 64
QK_HEAD_DIM = QK_NOPE_DIM + QK_ROPE_DIM
Q_LORA_RANK = D_MODEL // 4
KV_LORA_RANK = D_MODEL // 8
D_MIX = D_FOURIER + D_ATTN
IN_SPLITS = (D_FOURIER, D_FOURIER, Q_LORA_RANK, KV_LORA_RANK, QK_ROPE_DIM, D_ATTN)
D_IN = sum(IN_SPLITS)
ROPE_THETA = 10000.0
Q_BLOCK = 128
NORM_EPS = 1e-6
DEEPNORM_ALPHA = (2 * DEPTH) ** 0.25
DEEPNORM_BETA = (8 * DEPTH) ** -0.25


def _layernorm(x, g=None, b=None):
    xf = x.astype(jnp.float32)
    mu = jnp.mean(xf, axis=-1, keepdims=True)
    var = jnp.mean(jnp.square(xf - mu), axis=-1, keepdims=True)
    y = (xf - mu) * lax.rsqrt(var + NORM_EPS)
    if g is not None:
        y = y * g.astype(jnp.float32) + b.astype(jnp.float32)
    return y.astype(x.dtype)

def _rmsnorm(x, g):
    xf = x.astype(jnp.float32)
    y = xf * lax.rsqrt(jnp.mean(jnp.square(xf), axis=-1, keepdims=True) + NORM_EPS)
    return (y * g.astype(jnp.float32)).astype(x.dtype)

def _rope_tables(positions, dtype):
    inv_freq = ROPE_THETA ** (-jnp.arange(0, QK_ROPE_DIM, 2, dtype=jnp.float32) / QK_ROPE_DIM)
    ang = positions.astype(jnp.float32)[..., None] * inv_freq
    return jnp.cos(ang).astype(dtype), jnp.sin(ang).astype(dtype)

def _apply_rope(x, cos, sin):
    x1, x2 = jnp.split(x, 2, axis=-1)
    return jnp.concatenate([x1 * cos - x2 * sin, x2 * cos + x1 * sin], axis=-1)

def _fourier_mix(u, w_fmix):
    B, S, _ = u.shape
    ug = u.reshape(B, S, FOURIER_GROUPS, FOURIER_GROUP_DIM).astype(jnp.float32)
    f = jnp.real(jnp.fft.fftn(ug, axes=(1, 3), norm="ortho")).astype(u.dtype)
    y = jnp.einsum("bsgc,gcd->bsgd", f, w_fmix)
    return y.reshape(B, S, D_FOURIER)

def _mla_attention(q_nope, q_rope, k_nope, k_rope, v):
    B, S, H, _ = q_nope.shape
    nb = S // Q_BLOCK
    scale = 1.0 / math.sqrt(QK_HEAD_DIM)
    qn = q_nope.reshape(B, nb, Q_BLOCK, H, QK_NOPE_DIM).transpose(1, 0, 2, 3, 4)
    qr = q_rope.reshape(B, nb, Q_BLOCK, H, QK_ROPE_DIM).transpose(1, 0, 2, 3, 4)

    def block(args):
        qn_b, qr_b = args
        s = (jnp.einsum("bqhd,bkhd->bhqk", qn_b, k_nope)
             + jnp.einsum("bqhr,bkr->bhqk", qr_b, k_rope)).astype(jnp.float32) * scale
        p = jax.nn.softmax(s, axis=-1).astype(v.dtype)
        return jnp.einsum("bhqk,bkhd->bqhd", p, v)

    o = lax.map(block, (qn, qr))
    return o.transpose(1, 0, 2, 3, 4).reshape(B, S, H * V_HEAD_DIM)

def first_inputs(seed: int = 0) -> dict:
    key = jax.random.key(seed)
    ks = jax.random.split(key, 16)
    f32 = jnp.float32
    x = jax.random.normal(ks[0], (BATCH, SEQ, D_MODEL), f32)
    c = jax.random.normal(ks[1], (BATCH, D_MODEL), f32)
    offs = jax.random.randint(ks[2], (BATCH, 1), 0, SEQ, dtype=jnp.int32)
    positions = (jnp.arange(SEQ, dtype=jnp.int32)[None, :] + offs).astype(jnp.int32)
    w_ada = jax.random.normal(ks[3], (DEPTH, D_MODEL, 3 * D_MODEL), f32) * D_MODEL ** -0.5
    b_ada = 0.02 * jax.random.normal(ks[4], (DEPTH, 3 * D_MODEL), f32)
    w_in = jax.random.normal(ks[5], (DEPTH, D_MODEL, D_IN), f32) * D_MODEL ** -0.5
    q_norm = 1.0 + 0.02 * jax.random.normal(ks[6], (DEPTH, Q_LORA_RANK), f32)
    w_q_b = jax.random.normal(ks[7], (DEPTH, Q_LORA_RANK, N_HEADS * QK_HEAD_DIM), f32) * Q_LORA_RANK ** -0.5
    kv_norm = 1.0 + 0.02 * jax.random.normal(ks[8], (DEPTH, KV_LORA_RANK), f32)
    w_kv_b = jax.random.normal(ks[9], (DEPTH, KV_LORA_RANK, N_HEADS * (QK_NOPE_DIM + V_HEAD_DIM)), f32) * KV_LORA_RANK ** -0.5
    w_fmix = jax.random.normal(ks[10], (DEPTH, FOURIER_GROUPS, FOURIER_GROUP_DIM, FOURIER_GROUP_DIM), f32) * FOURIER_GROUP_DIM ** -0.5
    w_out = jax.random.normal(ks[11], (DEPTH, D_MIX, D_MODEL), f32) * (D_MIX ** -0.5 * DEEPNORM_BETA)
    ln_g = 1.0 + 0.02 * jax.random.normal(ks[12], (DEPTH, D_MODEL), f32)
    ln_b = 0.02 * jax.random.normal(ks[13], (DEPTH, D_MODEL), f32)
    return {"x": x, "c": c, "positions": positions, "w_ada": w_ada, "b_ada": b_ada,
            "w_in": w_in, "q_norm": q_norm, "w_q_b": w_q_b, "kv_norm": kv_norm,
            "w_kv_b": w_kv_b, "w_fmix": w_fmix, "w_out": w_out, "ln_g": ln_g, "ln_b": ln_b}

def first_block(x, c, positions, w_ada, b_ada, w_in, q_norm, w_q_b, kv_norm, w_kv_b,
              w_fmix, w_out, ln_g, ln_b):
    B, S, D = x.shape
    cos, sin = _rope_tables(positions, x.dtype)
    cos_q, sin_q = cos[:, :, None, :], sin[:, :, None, :]
    c_act = jax.nn.silu(c)
    split_pts = list(np.cumsum(IN_SPLITS)[:-1])
    for l in range(DEPTH):
        mod = c_act @ w_ada[l] + b_ada[l]
        shift, scale, gate = jnp.split(mod, 3, axis=-1)
        h = _layernorm(x) * (1.0 + scale[:, None, :]) + shift[:, None, :]
        p = h @ w_in[l]
        u_f, z_f, cq, ckv, k_r, z_a = jnp.split(p, split_pts, axis=-1)
        y_f = _fourier_mix(u_f, w_fmix[l]) * jax.nn.silu(z_f)
        q = (_rmsnorm(cq, q_norm[l]) @ w_q_b[l]).reshape(B, S, N_HEADS, QK_HEAD_DIM)
        q_nope, q_rope = q[..., :QK_NOPE_DIM], _apply_rope(q[..., QK_NOPE_DIM:], cos_q, sin_q)
        kv = (_rmsnorm(ckv, kv_norm[l]) @ w_kv_b[l]).reshape(B, S, N_HEADS, QK_NOPE_DIM + V_HEAD_DIM)
        k_nope, v = kv[..., :QK_NOPE_DIM], kv[..., QK_NOPE_DIM:]
        k_rope = _apply_rope(k_r, cos, sin)
        y_a = _mla_attention(q_nope, q_rope, k_nope, k_rope, v) * jax.nn.silu(z_a)
        y = jnp.concatenate([y_f, y_a], axis=-1) @ w_out[l]
        x = _layernorm(DEEPNORM_ALPHA * x + gate[:, None, :] * y, ln_g[l], ln_b[l])
    return x


DEPTH_2 = 1

N_META = 16
POOL_WIDTH = D_MODEL // 2
POOL_WINDOWS = (2, 4, 8, 16)
N_POOL_GROUPS = len(POOL_WINDOWS)
POOL_GROUP_DIM = POOL_WIDTH // N_POOL_GROUPS
CONV_WIDTH = D_MODEL // 2
CONV_KERNEL = 31
D_FF = 4 * D_MODEL
IN_COLS = POOL_WIDTH + 2 * CONV_WIDTH + 2 * D_MODEL
RMS_EPS = 1e-6
LN_EPS = 1e-5


def rms_norm(x, g):
    xf = x.astype(jnp.float32)
    y = xf * lax.rsqrt(jnp.mean(xf * xf, axis=-1, keepdims=True) + RMS_EPS)
    return (y * g.astype(jnp.float32)).astype(x.dtype)

def layer_norm(x, g, b):
    xf = x.astype(jnp.float32)
    mu = jnp.mean(xf, axis=-1, keepdims=True)
    var = jnp.mean(jnp.square(xf - mu), axis=-1, keepdims=True)
    y = (xf - mu) * lax.rsqrt(var + LN_EPS)
    return (y * g.astype(jnp.float32) + b.astype(jnp.float32)).astype(x.dtype)

def causal_multiscale_pool(z, w_grp, scale):
    B, L, _ = z.shape
    zf = z.astype(jnp.float32).reshape(B, L, N_POOL_GROUPS, POOL_GROUP_DIM)
    cs = jnp.cumsum(zf, axis=1)
    pos = jnp.arange(L)
    means = []
    for g, w in enumerate(POOL_WINDOWS):
        csg = cs[:, :, g]
        lag = jnp.pad(csg[:, : L - w], ((0, 0), (w, 0), (0, 0)))
        cnt = jnp.minimum(pos + 1, w).astype(jnp.float32)[None, :, None]
        means.append((csg - lag) / cnt)
    pooled = jnp.stack(means, axis=2)
    d = (pooled - zf).astype(z.dtype)
    y = jnp.einsum('blgc,gcd->blgd', d, w_grp).reshape(B, L, POOL_WIDTH)
    return y * scale

def conformer_conv(v, gate, w_dw, b_dw, ln_g, ln_b):
    a = v * jax.nn.sigmoid(gate)
    c = lax.conv_general_dilated(
        a, w_dw[:, None, :], window_strides=(1,),
        padding=[(CONV_KERNEL - 1, 0)],
        dimension_numbers=('NWC', 'WIO', 'NWC'),
        feature_group_count=CONV_WIDTH) + b_dw
    return jax.nn.silu(layer_norm(c, ln_g, ln_b))

def second_inputs(seed: int = 0) -> dict:
    key = jax.random.key(seed)
    ks = jax.random.split(key, 24)
    f32 = jnp.float32
    n = lambda k, shape, s: jax.random.normal(k, shape, f32) * s
    gain = lambda k, shape: 1.0 + 0.05 * jax.random.normal(k, shape, f32)
    return {
        "x": jax.random.normal(ks[0], (BATCH, SEQ, D_MODEL), f32),
        "meta": n(ks[1], (N_META, D_MODEL), 1.0),
        "g_pre_mix": gain(ks[2], (DEPTH_2, D_MODEL)),
        "w_in": n(ks[3], (DEPTH_2, D_MODEL, IN_COLS), D_MODEL ** -0.5),
        "w_pool_grp": n(ks[4], (DEPTH_2, N_POOL_GROUPS, POOL_GROUP_DIM, POOL_GROUP_DIM), POOL_GROUP_DIM ** -0.5),
        "pool_scale": gain(ks[5], (DEPTH_2, POOL_WIDTH)),
        "w_pool_out": n(ks[6], (DEPTH_2, POOL_WIDTH, D_MODEL), POOL_WIDTH ** -0.5),
        "w_dw": n(ks[7], (DEPTH_2, CONV_KERNEL, CONV_WIDTH), CONV_KERNEL ** -0.5),
        "b_dw": n(ks[8], (DEPTH_2, CONV_WIDTH), 0.02),
        "conv_ln_g": gain(ks[9], (DEPTH_2, CONV_WIDTH)),
        "conv_ln_b": n(ks[10], (DEPTH_2, CONV_WIDTH), 0.02),
        "w_conv_out": n(ks[11], (DEPTH_2, CONV_WIDTH, D_MODEL), CONV_WIDTH ** -0.5),
        "w_o": n(ks[12], (DEPTH_2, D_MODEL, D_MODEL), D_MODEL ** -0.5),
        "g_post_mix": gain(ks[13], (DEPTH_2, D_MODEL)),
        "g_pre_mlp": gain(ks[14], (DEPTH_2, D_MODEL)),
        "w_up": n(ks[15], (DEPTH_2, D_MODEL, D_FF), D_MODEL ** -0.5),
        "w_down": n(ks[16], (DEPTH_2, D_FF, D_MODEL), D_FF ** -0.5),
        "g_post_mlp": gain(ks[17], (DEPTH_2, D_MODEL)),
    }

def second_block(x, meta, g_pre_mix, w_in, w_pool_grp, pool_scale, w_pool_out,
              w_dw, b_dw, conv_ln_g, conv_ln_b, w_conv_out, w_o, g_post_mix,
              g_pre_mlp, w_up, w_down, g_post_mlp):
    B = x.shape[0]
    meta_b = jnp.broadcast_to(meta[None].astype(x.dtype), (B, N_META, D_MODEL))
    h = jnp.concatenate([meta_b, x], axis=1)
    splits = np.cumsum([POOL_WIDTH, CONV_WIDTH, CONV_WIDTH, D_MODEL]).tolist()
    for l in range(DEPTH_2):
        u = rms_norm(h, g_pre_mix[l])
        proj = u @ w_in[l]
        z_pool, v_conv, g_conv, gate_a, gate_b = jnp.split(proj, splits, axis=-1)
        y_a = causal_multiscale_pool(z_pool, w_pool_grp[l], pool_scale[l]) @ w_pool_out[l]
        y_b = conformer_conv(v_conv, g_conv, w_dw[l], b_dw[l],
                             conv_ln_g[l], conv_ln_b[l]) @ w_conv_out[l]
        m = jax.nn.sigmoid(gate_a) * y_a + jax.nn.sigmoid(gate_b) * y_b
        h = h + rms_norm(m @ w_o[l], g_post_mix[l])
        u = rms_norm(h, g_pre_mlp[l])
        f = jnp.square(jax.nn.relu(u @ w_up[l])) @ w_down[l]
        h = h + rms_norm(f, g_post_mlp[l])
    return h[:, N_META:]


def setup_inputs(seed=0):
    out = dict(first_inputs(seed))
    for name, value in second_inputs(seed + 1).items():
        if name != "x":
            out[name + "_2"] = value
    return out


def reference(
    x, c, positions, w_ada, b_ada, w_in, q_norm, w_q_b, kv_norm, w_kv_b, w_fmix, w_out, ln_g,
    ln_b, meta_2, g_pre_mix_2, w_in_2, w_pool_grp_2, pool_scale_2, w_pool_out_2, w_dw_2, b_dw_2,
    conv_ln_g_2, conv_ln_b_2, w_conv_out_2, w_o_2, g_post_mix_2, g_pre_mlp_2, w_up_2, w_down_2,
    g_post_mlp_2,
):
    x = first_block(
        x, c, positions, w_ada, b_ada, w_in, q_norm, w_q_b, kv_norm, w_kv_b, w_fmix, w_out,
        ln_g, ln_b,
    )
    return second_block(
        x, meta_2, g_pre_mix_2, w_in_2, w_pool_grp_2, pool_scale_2, w_pool_out_2, w_dw_2,
        b_dw_2, conv_ln_g_2, conv_ln_b_2, w_conv_out_2, w_o_2, g_post_mix_2, g_pre_mlp_2,
        w_up_2, w_down_2, g_post_mlp_2,
    )


_drawn_inputs = setup_inputs


def setup_inputs(seed=0):
    import zlib

    import numpy as np

    out = dict(_drawn_inputs(seed))
    spreads = {}
    factors = {'b_ada': 6.314,
     'q_norm': 8.0,
     'w_q_b': 3.469,
     'kv_norm': 8.0,
     'b_dw_2': 3.34,
     'conv_ln_b_2': 6.497}
    for name, (base, spread) in spreads.items():
        noise = np.random.default_rng([zlib.crc32(name.encode()), seed]).standard_normal(out[name].shape)
        drawn = base * np.exp(spread * noise) if base else spread * noise
        out[name] = __import__('jax').numpy.asarray(drawn.astype(out[name].dtype))
    for name, factor in factors.items():
        out[name] = (out[name] * factor).astype(out[name].dtype)
    return out
```

```python
from contextlib import ExitStack, contextmanager

import numpy as np
import concourse.bass as bass
from concourse import mybir

F32 = mybir.dt.float32
F32R = mybir.dt.float32r
I32 = mybir.dt.int32
ALU = mybir.AluOpType
ACT = mybir.ActivationFunctionType
AX = mybir.AxisListType

P = 128
T = 256
META = 16
TM = T + META
D = 2048
KT = D // P
DEPTH = 2
HEADS = 8
GROUPS = 8
ROPE = 64
QT = 512 // P
CT = 256 // P
LAT = QT + CT + 1
CONV = 1024 // P
TAPS = 31
WINDOWS = (2, 4, 8, 16)
FF_BLOCKS = 8192 // D
ALPHA = (2 * DEPTH) ** 0.25
SM_SCALE = 1.0 / float(np.sqrt(192.0))

CH = 16 * P
HALF = CH // 2
RAW = 3

L_DFT = LAT
L_FMIX = LAT + 1
L_FOUR = LAT + 2
L_HEAD = L_FOUR + 2 * GROUPS
L_OUT = L_HEAD + 2 * HEADS
PER_LAYER = L_OUT + KT
B2_CONV = DEPTH * PER_LAYER
B2_POOL = B2_CONV + 2 * CONV
B2_GRP = B2_POOL + CONV
B2_GATE = B2_GRP + 1
B2_WO = B2_GATE + 3 * KT
B2_FF = B2_WO + KT
CHUNKS = B2_FF + 2 * KT * FF_BLOCKS
ADA = 3 * DEPTH * KT

VECTORS = (("c", KT), ("b_ada", 3 * DEPTH * KT), ("q_norm", DEPTH * QT), ("kv_norm", DEPTH * CT),
           ("ln_g", DEPTH * KT), ("ln_b", DEPTH * KT), ("g_pre_mix", KT), ("pool_scale", CONV),
           ("w_dw", TAPS * CONV), ("b_dw", CONV), ("conv_ln_g", CONV), ("conv_ln_b", CONV),
           ("g_post_mix", KT), ("g_pre_mlp", KT), ("g_post_mlp", KT))
COL = {}
NV = 0
for _name, _n in VECTORS:
    COL[_name] = NV
    NV += _n
NC_ = 2 * P + 3


class Chain:

    def __init__(self, eng, sem):
        self.eng, self.sem, self.n, self.i, self.per = eng, sem, 0, None, 0

    def link(self, ins):
        self.n += 1
        ins.then_inc(self.sem, 1)
        self.eng.wait_ge(self.sem, self.n if self.i is None else self.i * self.per + self.n)

    @contextmanager
    def loop(self, start, end, per):
        base = self.n
        with self.eng.Fori(start, end) as i:
            self.i, self.per, self.n = i, per, base - start * per
            yield i
            assert self.n == base - start * per + per, (self.n - base + start * per, per)
        self.i, self.n = None, base + per * (end - start)


def build(nc, stream, ada, vectors, consts, positions, x, meta, out):
    with ExitStack() as ctx:
        def sb(name, cols, dt=F32):
            return ctx.enter_context(nc.sbuf_tensor(name, [P, cols], dt))

        def sem(name):
            return ctx.enter_context(nc.semaphore(name))

        raw = sb("raw", RAW * CH)
        w_hi = sb("w_hi", 2 * CH, F32R)
        w_lo = sb("w_lo", 2 * CH, F32R)
        area = sb("area", 3 * CH)
        X = sb("X", KT * T)
        a_hi = sb("a_hi", KT * TM, F32R)
        a_lo = sb("a_lo", KT * TM, F32R)
        y_hi = sb("y_hi", KT * T, F32R)
        y_lo = sb("y_lo", KT * T, F32R)
        lat_hi = sb("lat_hi", (QT + CT) * T, F32R)
        lat_lo = sb("lat_lo", (QT + CT) * T, F32R)
        st = sb("st", 14 * T, F32R)
        kr_hi = sb("kr_hi", T, F32R)
        kr_lo = sb("kr_lo", T, F32R)
        rope = sb("rope", T)
        sc = sb("sc", 4 * T)
        rs = sb("rs", 2 * T)
        mu = sb("mu", T)
        zs = sb("zs", T)
        th = sb("th", TM)
        vec = sb("vec", NV)
        con = sb("con", NC_)
        mod = sb("mod", ADA)
        ones = sb("ones", P)
        csil = sb("csil", 2 * KT)
        mt = sb("mt", KT * META)
        stat = sb("stat", 8)
        pos = th[:, 0:T].bitcast(I32)

        ps = ctx.enter_context(nc.psum_tensor("ps", [P, 8 * 512], F32))

        def bank(b, a=0, n=T):
            return ps[:, b * 512 + a:b * 512 + a + n]

        def lat_ps(m):
            return bank(4 + m % 3, m // 3 * T)

        def v(name, i, n=1):
            return vec[:, bass.ds(COL[name] + i, n)]

        ident, pairs = con[:, 0:P], con[:, P:2 * P]
        ada_ring = area[:, 0:2 * CH]
        ada_acc = area[:, 2 * CH:3 * CH]
        dft_hi, dft_lo = st[:, 0:4 * T], st[:, 4 * T:8 * T]
        u_hi, u_lo = st[:, 8 * T:9 * T], st[:, 9 * T:10 * T]
        t_hi, t_lo = st[:, 10 * T:12 * T], st[:, 12 * T:14 * T]
        qn_hi, qn_lo, qr_hi, qr_lo = (st[:, i * T:(i + 1) * T] for i in range(4))
        kn_hi, kn_lo, vv_hi, vv_lo = (st[:, i * T:(i + 1) * T] for i in range(4, 8))
        pt_hi, pt_lo = st[:, 8 * T:10 * T], st[:, 10 * T:12 * T]
        cw_hi, cw_lo = y_hi[:, 8 * T:16 * T], y_lo[:, 8 * T:16 * T]
        conv_out = area[:, 0:CONV * T]
        conv_sq = area[:, CONV * T:2 * CONV * T]
        wide = area[:, 0:KT * T]
        pad = area[:, 2 * CH:2 * CH + TAPS - 1 - META + TM]
        pool_z, pool_a, pool_b = (area[:, 2 * CH + at:2 * CH + at + TM] for at in (512, 1024, 1536))

        def a_tile(t, k, lo=META, n=T):
            return t[:, bass.ds(k * TM + lo, n)]

        landed = [sem("landed0"), sem("landed1")]
        hi_ready, lo_ready = sem("hi_ready"), sem("lo_ready")
        weights_used = sem("weights_used")
        ada_landed = [sem("ada_landed0"), sem("ada_landed1")]
        ada_step = sem("ada_step")
        ada_clear = sem("ada_clear")
        ada_summed = sem("ada_summed")
        mod_ready = sem("mod_ready")
        small = sem("small")
        ones_set, c_tanh, c_ready = sem("ones_set"), sem("c_tanh"), sem("c_ready")
        rope_arg, rope_sin = sem("rope_arg"), sem("rope_sin")
        dve = sem("dve")
        ln_mean = sem("ln_mean")
        ln_cent, ln_sq, ln_acc = sem("ln_cent"), sem("ln_sq"), sem("ln_acc")
        ln_var, ln_std = sem("ln_var"), sem("ln_std")
        ln_y, ln_hi, ln_lo = sem("ln_y"), sem("ln_hi"), sem("ln_lo")
        x_norm = sem("x_norm")
        x_back = sem("x_back")
        lat_sq, lat_acc, lat_stat = sem("lat_sq"), sem("lat_acc"), sem("lat_stat")
        lat_y, lat_h, lat_l = sem("lat_y"), sem("lat_h"), sem("lat_l")
        cw_h, cw_l = sem("cw_h"), sem("cw_l")
        kr_rot, kr_sum, kr_h, kr_l = sem("kr_rot"), sem("kr_sum"), sem("kr_h"), sem("kr_l")
        u_h, u_l = sem("u_h"), sem("u_l")
        t_ps, t_h, t_l, yf_ps = sem("t_ps"), sem("t_h"), sem("t_l"), sem("yf_ps")
        z_tanh, z_ready = sem("z_tanh"), sem("z_ready")
        y_mul, y_h, y_l = sem("y_mul"), sem("y_h"), sem("y_l")
        q_h, q_l, qr_rot = sem("q_h"), sem("q_l"), sem("qr_rot")
        v_h, v_l = sem("v_h"), sem("v_l")
        s_ps, s_max, s_exp, p_ready = sem("s_ps"), sem("s_max"), sem("s_exp"), sem("p_ready")
        pt_ps, pt_h, pt_l, o_ps = sem("pt_ps"), sem("pt_h"), sem("pt_l"), sem("o_ps")
        g_tmp, g_mul = sem("g_tmp"), sem("g_mul")
        m_sq, m_acc = sem("m_sq"), sem("m_acc")
        am_y, am_h, am_l = sem("am_y"), sem("am_h"), sem("am_l")
        cv_tanh, cv_in, cv_done = sem("cv_tanh"), sem("cv_in"), sem("cv_done")
        pl_in, pl_sum, pl_h, pl_l = sem("pl_in"), sem("pl_sum"), sem("pl_h"), sem("pl_l")
        gp_h, gp_l = sem("gp_h"), sem("gp_l")
        cm_ps, cm_cent, cm_sq, cm_acc = sem("cm_ps"), sem("cm_cent"), sem("cm_sq"), sem("cm_acc")
        cn_y, cn_tanh, cn_mul, cn_h, cn_l = (sem(n) for n in ("cn_y", "cn_tanh", "cn_mul", "cn_h", "cn_l"))
        gt_tanh, gt_done = sem("gt_tanh"), sem("gt_done")
        mm_h, mm_l = sem("mm_h"), sem("mm_l")
        wo_out, wo_sq, wo_acc, wo_stat = sem("wo_out"), sem("wo_sq"), sem("wo_acc"), sem("wo_stat")
        h_new, h_hi, h_sq, h_lo, h_acc, h_stat = (sem(n) for n in ("h_new", "h_hi", "h_sq", "h_lo", "h_acc", "h_stat"))
        f_relu, f_sq, f_hi, f_lo, f_acc = (sem(n) for n in ("f_relu", "f_sq", "f_hi", "f_lo", "f_acc"))
        f_osq, f_osum = sem("f_osq"), sem("f_osum")
        y_out, stored = sem("y_out"), sem("stored")

        SMALL = 5 * 16
        NORM = {n: i for i, n in enumerate(("meta", "pre0", "lat0", "post0", "pre1", "lat1", "post1",
                                            "mix", "conv", "wo", "out"))}
        block = ctx.enter_context(nc.Block())

        @block.sync
        def _(sp):
            sp.dma_start(vec[:, :], vectors).then_inc(small, 16)
            sp.dma_start(con[:, :], consts).then_inc(small, 16)
            sp.dma_start(pos, positions).then_inc(small, 16)
            sp.dma_start(X[:, :], x).then_inc(small, 16)
            sp.dma_start(mt[:, :], meta).then_inc(small, 16)

            def load(g, par, waits):
                if waits:
                    split_before = sp.snap(sp.to_reg(2 * g - 2 * RAW + 2))
                    landed_before = sp.snap(sp.to_reg(8 * (g - par)))
                    sp.wait_ge(lo_ready, split_before)
                    sp.wait_ge(landed[par], landed_before)
                sp.dma_start(raw[:, bass.ds((g % RAW) * CH, CH)],
                             stream[bass.ds(g, 1)].rearrange("a p n -> (a p) n")).then_inc(landed[par], 16)

            load(0, 0, False)
            load(1, 1, False)
            sp.wait_ge(landed[0], 16)
            load(2, 0, False)
            sp.wait_ge(landed[1], 16)
            sp.wait_ge(lo_ready, 2)
            load(3, 1, False)
            with sp.Fori(2, CHUNKS // 2) as i:
                for par in range(2):
                    load(2 * i + par, par, True)
            sp.wait_ge(lo_ready, 2 * (CHUNKS - RAW))
            sp.wait_ge(landed[0], 8 * (CHUNKS - 1))
            load(CHUNKS - 1, 0, False)
            for q in range(4):
                sp.wait_ge(y_out, 4 * q + 4)
                sp.dma_start(out[:, q * 4 * T:(q + 1) * 4 * T],
                             X[:, q * 4 * T:(q + 1) * 4 * T]).then_inc(stored, 16)
            sp.wait_ge(stored, 4 * 16)

        @block.gpsimd
        def _(pool):
            for a in range(2):
                pool.dma_start(ada_ring[:, a * CH:(a + 1) * CH], ada[a]).then_inc(ada_landed[a], 16)
            with pool.Fori(1, ADA // 2) as i:
                for par in range(2):
                    pool.wait_ge(ada_step, 2 * i + par - 1)
                    pool.dma_start(ada_ring[:, par * CH:(par + 1) * CH],
                                   ada[bass.ds(2 * i + par, 1)].rearrange("a p n -> (a p) n"))\
                        .then_inc(ada_landed[par], 16)

        @block.tensor
        def _(pe):
            def mm3(o, w, a, first, last):
                pe.matmul(o, w[1], a[0], start=first, stop=False)
                pe.matmul(o, w[0], a[1], start=False, stop=False)
                return pe.matmul(o, w[0], a[0], start=False, stop=last)

            def wb(par, k, n=P):
                at = par * CH + k * P
                return w_hi[:, at:at + n], w_lo[:, at:at + n]

            def a_ops(k):
                return a_tile(a_hi, k), a_tile(a_lo, k)

            def am_ops(k):
                return a_tile(a_hi, k, 0, TM), a_tile(a_lo, k, 0, TM)

            def y_ops(k):
                return y_hi[:, k * T:(k + 1) * T], y_lo[:, k * T:(k + 1) * T]

            def half(g, h):
                pe.wait_ge(lo_ready, 2 * g + h + 1)

            def blocks(par, o, ops, ks, first, last, w0=0):
                for k in ks:
                    r = mm3(o, wb(par, w0 + k), ops(k), first and k == ks[0], last and k == ks[-1])
                return r

            def chunk(g, par, o, ops):
                half(g, 0)
                blocks(par, o, ops, range(8), True, False)
                half(g, 1)
                blocks(par, o, ops, range(8, 16), False, True).then_inc(weights_used, 1)

            def ada_sum(r):
                pe.wait_ge(ada_step, KT * (r + 1))
                if r:
                    pe.wait_ge(mod_ready, r)
                for m in range(KT):
                    o = pe.matmul(bank(7, m, 1), ada_acc[:, m * P:(m + 1) * P], ones[:, 0:1],
                                  start=True, stop=True)
                o.then_inc(ada_summed, 1)

            def mean():
                for k in range(KT):
                    o = pe.matmul(bank(6), ones[:, :], X[:, k * T:(k + 1) * T], start=k == 0, stop=k == KT - 1)
                o.then_inc(ln_mean, 1)

            def squares(n):
                for i in range(KT // 2):
                    pe.wait_ge(ln_sq, 8 * n + i + 1)
                    for j in range(2):
                        at = (i % 2) * 2 * T + j * T
                        o = pe.matmul(bank(6, T), ones[:, :], sc[:, at:at + T],
                                      start=i + j == 0, stop=i == KT // 2 - 1 and j == 1)
                    o.then_inc(ln_acc, 1)

            pe.wait_ge(small, SMALL)
            pe.wait_ge(ones_set, 1)
            pe.wait_ge(m_sq, 1)
            for k in range(KT):
                o = pe.matmul(bank(5, 0, META), ones[:, :], sc[:, k * META:(k + 1) * META],
                              start=k == 0, stop=k == KT - 1)
            o.then_inc(m_acc, 1)
            mean()
            squares(0)
            ada_sum(0)
            ada_sum(1)

            for l in range(DEPTH):
                G = l * PER_LAYER
                pe.wait_ge(ln_lo, 8 * (l + 1))
                pe.wait_ge(ln_var, NORM["pre0"] + 1)
                for m in range(LAT - 1):
                    if m >= 3:
                        pe.wait_ge(lat_sq, 6 * l + m - 2)
                    chunk(G + m, (G + m) % 2, lat_ps(m), a_ops)
                pe.wait_ge(mod_ready, 3 * l + 2)
                chunk(G + LAT - 1, (G + LAT - 1) % 2, bank(7), a_ops)
                pe.wait_ge(lat_acc, 6 * (l + 1))
                pe.matmul(bank(3, 0, 2 * T), ones[:, :], sc[:, 0:2 * T], start=True, stop=True)\
                    .then_inc(lat_stat, 1)
                pe.wait_ge(lo_ready, 2 * (G + L_DFT) + 2)
                pe.wait_ge(weights_used, G + L_DFT)
                pe.nop().then_inc(weights_used, 1)
                g = G + L_FMIX
                half(g, 0)
                half(g, 1)
                pe.wait_ge(kr_rot, l + 1)
                for j, b in enumerate((0, 1, 2, 7)):
                    o = mm3(bank(b, 0, 512), wb(g % 2, 8 + j // 2), wb(g % 2, 4 * (j % 2), 512), True, True)
                o.then_inc(weights_used, 1)
                pe.wait_ge(ln_var, NORM[f"lat{l}"] + 1)
                pe.matmul(bank(3), pairs, sc[:, 3 * T:4 * T], start=True, stop=True).then_inc(kr_sum, 1)

                def seq_dft(q, first):
                    pe.wait_ge(t_l, 8 * l + q + 1)
                    if first:
                        pe.wait_ge(cw_l, 4 * l + 3)
                    else:
                        pe.wait_ge(y_mul, 16 * l + q)
                    for j in range(4):
                        tile_, trig = j // 2, j % 2
                        at, rhs = tile_ * T + trig * P, (2 * trig + tile_) * T
                        o = mm3(bank(2), (t_hi[:, at:at + P], t_lo[:, at:at + P]),
                                (dft_hi[:, rhs:rhs + T], dft_lo[:, rhs:rhs + T]), j == 0, j == 3)
                    o.then_inc(yf_ps, 1)

                def group(q, first, second=False):
                    g = G + L_FOUR + 2 * q
                    g0 = G + L_FOUR
                    if first:
                        pe.wait_ge(cw_l, 4 * l + 1)
                    chunk(g, g0 % 2, bank(0), a_ops)
                    if first:
                        pe.wait_ge(cw_l, 4 * l + 2)
                    else:
                        seq_dft(q - 1, second)
                        pe.wait_ge(z_ready, 16 * l + q)
                    chunk(g + 1, (g0 + 1) % 2, bank(1), a_ops)
                    pe.wait_ge(u_l, 8 * l + q + 1)
                    if first:
                        pe.wait_ge(cw_l, 4 * (l + 1))
                        pe.wait_ge(kr_l, l + 1)
                    for j in range(2):
                        o = mm3(bank(3, j * T), (u_hi[:, j * P:(j + 1) * P], u_lo[:, j * P:(j + 1) * P]),
                                (cw_hi[:, bass.ds(q * T, T)], cw_lo[:, bass.ds(q * T, T)]), True, True)
                    o.then_inc(t_ps, 1)

                group(0, True)
                group(1, False, True)
                with pe.Fori(2, GROUPS // 2) as q:
                    group(q, False)
                ada_sum(2 if l == 0 else 5)
                with pe.Fori(GROUPS // 2, GROUPS) as q:
                    group(q, False)
                seq_dft(GROUPS - 1, False)

                def project(h, first):
                    g = G + L_HEAD + 2 * h
                    par = (G + L_HEAD) % 2
                    half(g, 0)
                    if first:
                        pe.wait_ge(lat_l, 6 * (l + 1))
                        pe.wait_ge(z_ready, 16 * l + GROUPS)

                    def lat(k):
                        return lat_hi[:, k * T:(k + 1) * T], lat_lo[:, k * T:(k + 1) * T]
                    blocks(par, bank(0), lat, range(QT), True, True)
                    blocks(par, bank(0, T), lat, range(QT), True, True, QT)
                    half(g, 1)
                    if not first:
                        pe.wait_ge(v_l, 8 * l + h)
                    for k in range(CT):
                        mm3(bank(1), wb(par, 8 + k), lat(QT + k), k == 0, k == CT - 1)
                    for tt in range(2):
                        for k in range(CT):
                            o = mm3(bank(1, T + tt * P, P),
                                    tuple(t[:, tt * P:(tt + 1) * P] for t in lat(QT + k)),
                                    wb(par, 10 + k), k == 0, k == CT - 1)
                    o.then_inc(weights_used, 1)

                def turn(h):
                    pe.wait_ge(p_ready, 8 * l + h + 1)
                    for qt in range(2):
                        for kt in range(2):
                            o = pe.transpose(bank(3, kt * T + qt * P, P),
                                             sc[:, qt * T + kt * P:qt * T + kt * P + P], ident)
                    o.then_inc(pt_ps, 1)

                def attend(h, first=False):
                    pe.wait_ge(pt_l, 8 * l + h + 1)
                    pe.wait_ge(v_l, 8 * l + h + 1)
                    if not first:
                        pe.wait_ge(y_mul, 16 * l + GROUPS + h)
                    for k in range(2):
                        o = mm3(bank(4), (vv_hi[:, k * P:(k + 1) * P], vv_lo[:, k * P:(k + 1) * P]),
                                (pt_hi[:, k * T:(k + 1) * T], pt_lo[:, k * T:(k + 1) * T]), k == 0, k == 1)
                    o.then_inc(o_ps, 1)

                def head(h, first, second=False):
                    g = G + L_HEAD + 2 * h
                    par = (G + L_HEAD + 1) % 2
                    project(h, first)
                    half(g + 1, 0)
                    if first:
                        pe.wait_ge(y_mul, 16 * l + GROUPS)
                    else:
                        pe.wait_ge(z_ready, 16 * l + GROUPS + h)
                    blocks(par, bank(2), a_ops, range(8), True, False)
                    if not first:
                        turn(h - 1)
                    half(g + 1, 1)
                    blocks(par, bank(2), a_ops, range(8, 16), False, True).then_inc(weights_used, 1)
                    if not first:
                        attend(h - 1, second)
                    pe.wait_ge(q_l, 3 * (8 * l + h) + 3)
                    for qt in range(2):
                        s = slice(qt * P, (qt + 1) * P)
                        mm3(bank(5, qt * T), (qn_hi[:, s], qn_lo[:, s]), (kn_hi, kn_lo), True, False)
                        o = mm3(bank(5, qt * T), (qr_hi[:, s], qr_lo[:, s]), (kr_hi[:, :], kr_lo[:, :]),
                                False, True)
                    o.then_inc(s_ps, 1)

                head(0, True)
                head(1, False, True)
                with pe.Fori(2, HEADS // 2) as h:
                    head(h, False)
                if l == 0:
                    ada_sum(3)
                with pe.Fori(HEADS // 2, HEADS) as h:
                    head(h, False)

                g = G + L_OUT
                half(g, 0)
                pe.wait_ge(y_l, 16 * l + 15)
                blocks(g % 2, bank(0), y_ops, range(8), True, False)
                turn(HEADS - 1)
                half(g, 1)
                blocks(g % 2, bank(0), y_ops, range(8, 12), False, False)
                attend(HEADS - 1)
                blocks(g % 2, bank(0), y_ops, range(12, 15), False, False)
                pe.wait_ge(y_l, 16 * (l + 1))
                blocks(g % 2, bank(0), y_ops, range(15, 16), False, True).then_inc(weights_used, 1)
                chunk(g + 1, (g + 1) % 2, bank(1), y_ops)
                with pe.Fori(1, KT // 2) as i:
                    for b in range(2):
                        pe.wait_ge(g_tmp, 16 * l + 2 * i + b - 1)
                        chunk(g + 2 * i + b, (g + b) % 2, bank(b), y_ops)
                if l == 0:
                    ada_sum(4)
                pe.wait_ge(g_mul, 16 * (l + 1))
                mean()
                squares(2 * l + 1)
                if l == 0:
                    pe.wait_ge(x_norm, 1)
                    mean()
                    squares(2)

            squares(4)
            pe.wait_ge(ln_lo, 8 * 3)
            pe.wait_ge(am_l, 1)

            def conv_tile(j, first):
                if not first:
                    pe.wait_ge(cv_in, j)
                for b in range(2):
                    chunk(B2_CONV + 2 * j + b, (B2_CONV + b) % 2, bank(b, 0, TM), am_ops)

            conv_tile(0, True)
            with pe.Fori(1, CONV) as j:
                conv_tile(j, False)
            pe.wait_ge(cv_in, CONV)
            for b in range(2):
                chunk(B2_POOL + b, (B2_POOL + b) % 2, bank(b, 0, TM), am_ops)
            with pe.Fori(1, CONV // 2) as i:
                for b in range(2):
                    pe.wait_ge(pl_in, 2 * i + b - 1)
                    chunk(B2_POOL + 2 * i + b, (B2_POOL + b) % 2, bank(b, 0, TM), am_ops)
            pe.wait_ge(cv_done, CONV)
            for k in range(CONV):
                o = pe.matmul(bank(6), ones[:, :], conv_out[:, k * T:(k + 1) * T], start=k == 0, stop=k == CONV - 1)
            o.then_inc(cm_ps, 1)
            half(B2_GRP, 0)
            half(B2_GRP, 1)
            pe.wait_ge(pl_l, CONV)
            for m in range(CONV):
                for k in range(2):
                    o = mm3(bank(2 + m // 2, (m % 2) * T), wb(B2_GRP % 2, 2 * m + k), y_ops(2 * (m // 2) + k),
                            k == 0, k == 1)
            o.then_inc(weights_used, 1)
            for k in range(CONV):
                pe.wait_ge(cm_sq, k // 2 + 1)
                o = pe.matmul(bank(6, T), ones[:, :], conv_sq[:, k * T:(k + 1) * T], start=k == 0, stop=k == CONV - 1)
            o.then_inc(cm_acc, 1)

            def gate_tile(m, b, first):
                g, g0 = B2_GATE + 3 * m, B2_GATE + 3 * b
                if not first:
                    pe.wait_ge(gt_tanh, 2 * m - 1)
                chunk(g, g0 % 2, bank(0), a_ops)
                if not first:
                    pe.wait_ge(gt_tanh, 2 * m)
                chunk(g + 1, (g0 + 1) % 2, bank(1), a_ops)
                half(g + 2, 0)
                if first:
                    pe.wait_ge(gp_l, CONV)
                else:
                    pe.wait_ge(gt_done, m)
                for k in range(CONV):
                    mm3(bank(2), wb((g0 + 2) % 2, k), y_ops(CONV + k), k == 0, k == CONV - 1)
                half(g + 2, 1)
                if first:
                    pe.wait_ge(cn_l, CONV)
                for k in range(CONV):
                    o = mm3(bank(3), wb((g0 + 2) % 2, CONV + k), y_ops(k), k == 0, k == CONV - 1)
                o.then_inc(weights_used, 1)

            pe.wait_ge(pl_in, CONV)
            gate_tile(0, 0, True)
            gate_tile(1, 1, False)
            with pe.Fori(1, KT // 2) as i:
                for b in range(2):
                    gate_tile(2 * i + b, b, False)
            pe.wait_ge(mm_l, 4)
            for b in range(2):
                chunk(B2_WO + b, (B2_WO + b) % 2, bank(b), a_ops)
            with pe.Fori(1, KT // 2) as i:
                for b in range(2):
                    pe.wait_ge(wo_sq, 2 * i + b - 1)
                    chunk(B2_WO + 2 * i + b, (B2_WO + b) % 2, bank(b), a_ops)
            pe.wait_ge(wo_acc, KT)
            pe.matmul(bank(6), ones[:, :], mu[:, :], start=True, stop=True).then_inc(wo_stat, 1)

            def up(f, i, b, first):
                if not first:
                    pe.wait_ge(f_relu, 16 * f + 2 * i + b - 1)
                chunk(B2_FF + 32 * f + 2 * i + b, (B2_FF + b) % 2, bank(b), a_ops)

            def down(f, i, b, first):
                if not first:
                    pe.wait_ge(f_acc, 16 * f + 2 * i + b - 1)
                chunk(B2_FF + 32 * f + KT + 2 * i + b, (B2_FF + b) % 2, bank(2 + b), y_ops)

            pe.wait_ge(h_lo, KT)
            for b in range(2):
                up(0, 0, b, True)
            with pe.Fori(1, KT // 2) as i:
                for b in range(2):
                    up(0, i, b, False)
            pe.wait_ge(h_acc, KT)
            pe.matmul(bank(6, T), ones[:, :], mu[:, :], start=True, stop=True).then_inc(h_stat, 1)
            pe.wait_ge(f_lo, 16)
            for b in range(2):
                down(0, 0, b, True)
            with pe.Fori(1, KT // 2) as i:
                for b in range(2):
                    down(0, i, b, False)
            with pe.Fori(1, FF_BLOCKS) as f:
                with pe.Fori(0, KT // 2) as i:
                    for b in range(2):
                        up(f, i, b, False)
                with pe.Fori(0, KT // 2) as i:
                    pe.wait_ge(f_lo, 16 * f + 16)
                    for b in range(2):
                        down(f, i, b, False)
            for i in range(KT // 2):
                pe.wait_ge(f_osq, i + 1)
                for j in range(2):
                    at = (i % 2) * 2 * T + j * T
                    o = pe.matmul(bank(6), ones[:, :], sc[:, at:at + T],
                                  start=i + j == 0, stop=i == KT // 2 - 1 and j == 1)
                o.then_inc(f_osum, 1)

        @block.scalar
        def _(ac):
            def split(g, par, dft=False):
                ac.wait_ge(landed[par], 8 * (g - par) + 16)
                if not (isinstance(g, int) and g < 2):
                    ac.wait_ge(weights_used, g - 1)
                n = HALF // 2 if dft else HALF
                for h in range(2):
                    to = dft_hi[:, h * n:(h + 1) * n] if dft else w_hi[:, par * CH + h * n:par * CH + (h + 1) * n]
                    ac.copy(to, raw[:, bass.ds((g % RAW) * CH + h * n, n)]).then_inc(hi_ready, 1)

            def after(g, base):
                split(g + 2, base % 2)

            def rstd(name, n=T):
                ac.wait_ge(ln_var, NORM[name] + 1)
                ac.activation(rs[:, 0:n], rs[:, 0:n], ACT.Sqrt).then_inc(ln_std, 1)

            def square_x(n, waits):
                for i in range(KT // 2):
                    if waits:
                        ac.wait_ge(ln_cent, 8 * n + i + 1)
                    if i >= 2:
                        ac.wait_ge(ln_acc, 8 * n + i - 1)
                    ac.activation(sc[:, (i % 2) * 2 * T:(i % 2 + 1) * 2 * T], X[:, 2 * i * T:(2 * i + 2) * T],
                                  ACT.Square).then_inc(ln_sq, 1)

            def split_input(n):
                with ac.Fori(0, KT // 2) as i:
                    ac.wait_ge(ln_y, i + (8 * n + 1))
                    to = a_hi[:, bass.ds(i * 2 * TM, 2 * TM)].rearrange("p (k t) -> p k t", k=2)[:, :, META:TM]
                    frm = sc[:, bass.ds((i % 2) * 2 * T, 2 * T)].rearrange("p (k t) -> p k t", k=2)
                    ac.copy(to, frm).then_inc(ln_hi, 1)

            split(0, 0)
            split(1, 1)
            ac.wait_ge(small, SMALL)
            ac.activation(csil[:, 0:KT], v("c", 0, KT), ACT.Tanh, scale=0.5).then_inc(c_tanh, 1)
            ac.wait_ge(rope_arg, 1)
            ac.activation(rope[:, :], zs[:, :], ACT.Sin).then_inc(rope_sin, 1)
            rstd("meta", META)
            square_x(0, True)
            rstd("pre0")
            split_input(0)

            for l in range(DEPTH):
                G = l * PER_LAYER
                if l == 0:
                    ac.wait_ge(ln_hi, 8)
                    ac.wait_ge(ln_lo, 8)
                    ac.dma_start(X[:, :], x).then_inc(x_back, 16)
                for m in range(LAT):
                    ac.wait_ge(weights_used, G + m + 1)
                    if m < QT + CT:
                        if m:
                            ac.wait_ge(lat_acc, 6 * l + m)
                        ac.activation(sc[:, 2 * T:3 * T], lat_ps(m),
                                      ACT.Square).then_inc(lat_sq, 1)
                    split(G + m + 2, (G + m) % 2, dft=m + 2 == L_DFT)
                ac.wait_ge(weights_used, G + L_DFT + 1)
                after(G + L_DFT, G + L_DFT)
                ac.wait_ge(weights_used, G + L_FMIX + 1)

                def cw(j):
                    b, trig, g4 = (0, 1, 2, 7)[j], j // 2, j % 2
                    to = cw_hi[:, g4 * 4 * T:(g4 + 1) * 4 * T].rearrange("p (g c) -> p g c", g=4)
                    ac.copy(to[:, :, trig * P:(trig + 1) * P],
                            bank(b, 0, 512).rearrange("p (g c) -> p g c", g=4)).then_inc(cw_h, 1)

                cw(0)
                cw(1)
                after(G + L_FMIX, G + L_FMIX)
                cw(2)
                cw(3)
                rstd(f"lat{l}", 2 * T)
                ac.wait_ge(kr_sum, l + 1)
                ac.copy(kr_hi[:, :], bank(3)).then_inc(kr_h, 1)
                for m in range(QT + CT):
                    ac.wait_ge(lat_y, 6 * l + m + 1)
                    ac.copy(lat_hi[:, m * T:(m + 1) * T], sc[:, (m % 2) * T:(m % 2 + 1) * T]).then_inc(lat_h, 1)

                def y_part(t):
                    ac.wait_ge(y_mul, 16 * l + t + 1)
                    ac.copy(y_hi[:, bass.ds(t * T, T)], sc[:, 2 * T:3 * T]).then_inc(y_h, 1)

                def group(q, first):
                    g, g0 = G + L_FOUR + 2 * q, G + L_FOUR
                    ac.wait_ge(weights_used, g + 1)
                    ac.copy(u_hi, bank(0)).then_inc(u_h, 1)
                    after(g, g0)
                    if not first:
                        y_part(q - 1)
                    ac.wait_ge(weights_used, g + 2)
                    ac.activation(th[:, 0:T], bank(1), ACT.Tanh, scale=0.5).then_inc(z_tanh, 1)
                    after(g + 1, g0 + 1)
                    ac.wait_ge(t_ps, 8 * l + q + 1)
                    ac.copy(t_hi, bank(3, 0, 2 * T)).then_inc(t_h, 1)

                group(0, True)
                with ac.Fori(1, GROUPS) as q:
                    group(q, False)
                y_part(GROUPS - 1)

                def turned(h):
                    ac.wait_ge(pt_ps, 8 * l + h + 1)
                    ac.copy(pt_hi, bank(3, 0, 2 * T)).then_inc(pt_h, 1)

                def head(h, first):
                    g, g0 = G + L_HEAD + 2 * h, G + L_HEAD
                    ac.wait_ge(weights_used, g + 1)
                    ac.copy(qn_hi, bank(0)).then_inc(q_h, 1)
                    ac.copy(kn_hi, bank(1)).then_inc(q_h, 1)
                    ac.wait_ge(qr_rot, 8 * l + h + 1)
                    ac.copy(qr_hi, sc[:, 3 * T:4 * T]).then_inc(q_h, 1)
                    after(g, g0)
                    if not first:
                        turned(h - 1)
                    ac.wait_ge(weights_used, g + 2)
                    if not first:
                        ac.wait_ge(z_ready, 16 * l + GROUPS + h)
                    ac.activation(th[:, 0:T], bank(2), ACT.Tanh, scale=0.5).then_inc(z_tanh, 1)
                    if not first:
                        ac.wait_ge(o_ps, 8 * l + h)
                    ac.wait_ge(q_l, 3 * (8 * l + h) + 2)
                    ac.copy(vv_hi, bank(1, T)).then_inc(v_h, 1)
                    if not first:
                        y_part(GROUPS + h - 1)
                    ac.wait_ge(s_max, 8 * l + h + 1)
                    for qt in range(2):
                        ac.activation(sc[:, qt * T:(qt + 1) * T], bank(5, qt * T), ACT.Exp,
                                      bias=stat[:, 2 + qt:3 + qt], scale=SM_SCALE,
                                      accum_out=stat[:, 4 + qt:5 + qt]).then_inc(s_exp, 1)
                    after(g + 1, g0 + 1)

                head(0, True)
                with ac.Fori(1, HEADS) as h:
                    head(h, False)

                def out_tile(i, b, first):
                    g = G + L_OUT
                    m = 2 * i + b
                    ac.wait_ge(weights_used, m + (g + 1))
                    if not first:
                        ac.wait_ge(g_mul, m + (16 * l - 1))
                    ac.activation(sc[:, b * T:(b + 1) * T], bank(b), ACT.Copy,
                                  scale=mod[:, bass.ds(m + (3 * l + 2) * KT, 1)]).then_inc(g_tmp, 1)
                    after(m + g, g + b)

                turned(HEADS - 1)
                y_part(2 * HEADS - 1)
                ac.wait_ge(mod_ready, 3 * l + 3)
                for b in range(2):
                    out_tile(0, b, True)
                with ac.Fori(1, KT // 2) as i:
                    for b in range(2):
                        out_tile(i, b, False)
                square_x(2 * l + 1, True)
                rstd(f"post{l}")
                if l == 0:
                    for i in range(KT // 2):
                        ac.wait_ge(ln_cent, 8 * 2 + i + 1)
                        s = slice((i % 2) * 2 * T, (i % 2 + 1) * 2 * T)
                        ac.activation(sc[:, s], sc[:, s], ACT.Square).then_inc(ln_sq, 1)
                    rstd("pre1")
                    split_input(1)

            ac.wait_ge(x_norm, 2)
            square_x(4, False)
            rstd("mix")
            split_input(2)
            ac.wait_ge(am_y, 1)
            ac.copy(a_hi[:, :].rearrange("p (k t) -> p k t", k=KT)[:, :, 0:META],
                    mt[:, :].rearrange("p (k t) -> p k t", k=KT)).then_inc(am_h, 1)

            with ac.Fori(0, CONV) as j:
                g = B2_CONV + 2 * j
                ac.wait_ge(weights_used, g + 1)
                after(g, B2_CONV)
                ac.wait_ge(weights_used, g + 2)
                ac.activation(th[:, :], bank(1, 0, TM), ACT.Tanh, scale=0.5).then_inc(cv_tanh, 1)
                after(g + 1, B2_CONV + 1)
            for j in range(CONV):
                ac.wait_ge(weights_used, B2_POOL + j + 1)
                if j:
                    ac.wait_ge(pl_sum, j)
                ac.copy(pool_z, bank(j % 2, 0, TM)).then_inc(pl_in, 1)
                after(B2_POOL + j, B2_POOL + j)
                ac.wait_ge(pl_sum, j + 1)
                ac.copy(y_hi[:, j * T:(j + 1) * T], zs[:, :]).then_inc(pl_h, 1)
            ac.wait_ge(weights_used, B2_GRP + 1)
            for i, m in enumerate((0, 2, 4, 6, 1, 3, 5, 7)):
                if m % 2:
                    ac.wait_ge(gp_l, i - 3)
                ac.activation(y_hi[:, (CONV + m) * T:(CONV + m + 1) * T], bank(2 + m // 2, (m % 2) * T), ACT.Copy,
                              scale=v("pool_scale", m)).then_inc(gp_h, 1)
            after(B2_GRP, B2_GRP)
            for i in range(CONV // 2):
                ac.wait_ge(cm_cent, i + 1)
                s = slice(2 * i * T, (2 * i + 2) * T)
                ac.activation(conv_sq[:, s], conv_out[:, s], ACT.Square).then_inc(cm_sq, 1)
            rstd("conv")

            def gate_first(m, b):
                g, g0 = B2_GATE + 3 * m, B2_GATE + 3 * b
                ac.wait_ge(weights_used, g + 1)
                if not (isinstance(m, int) and m == 0):
                    ac.wait_ge(gt_done, m)
                ac.activation(sc[:, 0:T], bank(0), ACT.Tanh, scale=0.5).then_inc(gt_tanh, 1)
                after(g, g0)

            def gate_rest(m, b):
                g, g0 = B2_GATE + 3 * m, B2_GATE + 3 * b
                ac.wait_ge(weights_used, g + 2)
                ac.activation(sc[:, T:2 * T], bank(1), ACT.Tanh, scale=0.5).then_inc(gt_tanh, 1)
                after(g + 1, g0 + 1)
                ac.wait_ge(weights_used, g + 3)
                after(g + 2, g0 + 2)

            gate_first(0, 0)
            for k in range(CONV):
                ac.wait_ge(cn_y, k + 1)
                ac.activation(th[:, 0:T], conv_out[:, k * T:(k + 1) * T], ACT.Tanh, scale=0.5).then_inc(cn_tanh, 1)
                ac.wait_ge(cn_mul, k + 1)
                ac.activation(y_hi[:, k * T:(k + 1) * T], zs[:, :], ACT.Copy, scale=0.5).then_inc(cn_h, 1)
            gate_rest(0, 0)
            gate_first(1, 1)
            gate_rest(1, 1)
            with ac.Fori(1, KT // 2) as i:
                for b in range(2):
                    gate_first(2 * i + b, b)
                    gate_rest(2 * i + b, b)
            for i in range(4):
                ac.wait_ge(gt_done, KT)
                to = a_hi[:, i * 4 * TM:(i + 1) * 4 * TM].rearrange("p (k t) -> p k t", k=4)[:, :, META:TM]
                ac.activation(to, wide[:, i * 4 * T:(i + 1) * 4 * T].rearrange("p (k t) -> p k t", k=4),
                              ACT.Copy, scale=0.5).then_inc(mm_h, 1)

            def wo_tile(i, b, first):
                m = 2 * i + b
                ac.wait_ge(weights_used, m + (B2_WO + 1))
                ac.copy(wide[:, bass.ds(m * T, T)], bank(b)).then_inc(wo_out, 1)
                if not first:
                    ac.wait_ge(wo_acc, m - 1)
                ac.activation(sc[:, b * T:(b + 1) * T], bank(b), ACT.Square).then_inc(wo_sq, 1)
                after(m + B2_WO, B2_WO + b)

            for b in range(2):
                wo_tile(0, b, True)
            with ac.Fori(1, KT // 2) as i:
                for b in range(2):
                    wo_tile(i, b, False)
            rstd("wo")
            def new_h(m, b, first):
                if not first:
                    ac.wait_ge(h_acc, m - 1)
                ac.wait_ge(h_new, m + 1)
                ac.activation(a_tile(a_hi, m), X[:, bass.ds(m * T, T)], ACT.Copy,
                              scale=v("g_pre_mlp", m)).then_inc(h_hi, 1)
                ac.activation(sc[:, (2 + b) * T:(3 + b) * T], X[:, bass.ds(m * T, T)], ACT.Square).then_inc(h_sq, 1)

            for b in range(2):
                new_h(b, b, True)
            with ac.Fori(1, KT // 2) as i:
                for b in range(2):
                    new_h(2 * i + b, b, False)

            def up(f, i, b, first):
                m = 16 * f + 2 * i + b
                g = B2_FF + 32 * f + 2 * i + b
                ac.wait_ge(weights_used, g + 1)
                if not first:
                    ac.wait_ge(f_lo, m - 1)
                ac.activation(sc[:, b * T:(b + 1) * T], bank(b), ACT.Relu).then_inc(f_relu, 1)
                ac.wait_ge(f_relu, m + 1)
                ac.activation(y_hi[:, bass.ds((2 * i + b) * T, T)], sc[:, b * T:(b + 1) * T], ACT.Square)\
                    .then_inc(f_hi, 1)
                after(g, B2_FF + b)

            for b in range(2):
                up(0, 0, b, True)
            with ac.Fori(1, KT // 2) as i:
                for b in range(2):
                    up(0, i, b, False)
            with ac.Fori(0, KT // 2) as i:
                for b in range(2):
                    g = B2_FF + KT + 2 * i + b
                    ac.wait_ge(weights_used, g + 1)
                    after(g, B2_FF + b)
            with ac.Fori(1, FF_BLOCKS - 1) as f:
                with ac.Fori(0, KT // 2) as i:
                    for b in range(2):
                        up(f, i, b, False)
                with ac.Fori(0, KT // 2) as i:
                    for b in range(2):
                        g = B2_FF + KT + 32 * f + 2 * i + b
                        ac.wait_ge(weights_used, g + 1)
                        after(g, B2_FF + b)
            f = FF_BLOCKS - 1
            with ac.Fori(0, KT // 2) as i:
                for b in range(2):
                    up(f, i, b, False)
            with ac.Fori(0, KT // 2 - 1) as i:
                for b in range(2):
                    g = B2_FF + KT + 32 * f + 2 * i + b
                    ac.wait_ge(weights_used, g + 1)
                    after(g, B2_FF + b)
            for i in range(KT // 2):
                ac.wait_ge(f_acc, 16 * (FF_BLOCKS - 1) + 2 * i + 2)
                if i >= 2:
                    ac.wait_ge(f_osum, i - 1)
                ac.activation(sc[:, (i % 2) * 2 * T:(i % 2 + 1) * 2 * T], wide[:, 2 * i * T:(2 * i + 2) * T],
                              ACT.Square).then_inc(f_osq, 1)
            ac.wait_ge(ln_var, NORM["out"] + 1)
            ac.activation(rs[:, T:2 * T], rs[:, T:2 * T], ACT.Sqrt).then_inc(ln_std, 1)

        @block.vector
        def _(ve):
            own = Chain(ve, dve)

            def split(g, par, dft=False):
                n = HALF // 2 if dft else HALF
                for h in range(2):
                    ve.wait_ge(hi_ready, 2 * g + h + 1)
                    if dft:
                        to, hi = dft_lo[:, h * n:(h + 1) * n], dft_hi[:, h * n:(h + 1) * n]
                    else:
                        s = slice(par * CH + h * n, par * CH + (h + 1) * n)
                        to, hi = w_lo[:, s], w_hi[:, s]
                    ve.tensor_tensor(to, raw[:, bass.ds((g % RAW) * CH + h * n, n)], hi.bitcast(F32),
                                     ALU.subtract).then_inc(lo_ready, 1)

            def after(g, base):
                split(g + 2, base % 2)

            def sub_hi(out_, exact, hi):
                return ve.tensor_tensor(out_, exact, hi.bitcast(F32), ALU.subtract)

            def over_tokens(t, k):
                return t.unsqueeze(1).to_broadcast([P, k, T])

            def tiles(t, k):
                return t.rearrange("p (k t) -> p k t", k=k)

            def add_ada(a, par):
                ve.wait_ge(ada_landed[par], 8 * (a - par) + 16)
                if not (isinstance(a, int) and a == 0):
                    ve.wait_ge(ada_step, a)
                ve.scalar_tensor_tensor(out=ada_acc, in0=ada_ring[:, par * CH:(par + 1) * CH],
                                        scalar=csil[:, bass.ds(KT + a % KT, 1)], in1=ada_acc,
                                        op0=ALU.mult, op1=ALU.add).then_inc(ada_step, 1)

            def clear_ada(r):
                if r:
                    ve.wait_ge(ada_summed, r)
                ve.memset(ada_acc, 0.0).then_inc(ada_clear, 1)
                ve.wait_ge(ada_clear, r + 1)

            def read_mod(r):
                ve.wait_ge(ada_summed, r + 1)
                ve.scalar_tensor_tensor(out=mod[:, r * KT:(r + 1) * KT], in0=bank(7, 0, KT),
                                        scalar=1.0 if r % 3 == 1 else 0.0, in1=v("b_ada", r * KT, KT),
                                        op0=ALU.add, op1=ALU.add).then_inc(mod_ready, 1)
                if r + 1 < 3 * DEPTH:
                    clear_ada(r + 1)

            def rstd(name, parts, eps):
                for part, total, count in parts:
                    o = ve.tensor_scalar(part, total, 1.0 / count, eps, ALU.mult, ALU.add)
                    if part is not parts[-1][0]:
                        own.link(o)
                o.then_inc(ln_var, 1)
                ve.wait_ge(ln_std, NORM[name] + 1)
                whole = rs[:, 0:T * len(parts)] if name != "meta" else parts[0][0]
                own.link(ve.reciprocal(whole, whole))

            def centre(n, in_place):
                ve.wait_ge(ln_mean, n + 1)
                own.link(ve.tensor_scalar(mu[:, :], bank(6), 1.0 / D, None, ALU.mult))
                for i in range(KT // 2):
                    frm = X[:, 2 * i * T:(2 * i + 2) * T]
                    if not in_place and i >= 2:
                        ve.wait_ge(ln_acc, 8 * n + i - 1)
                    to = frm if in_place else sc[:, (i % 2) * 2 * T:(i % 2 + 1) * 2 * T]
                    ve.tensor_tensor(tiles(to, 2), tiles(frm, 2), over_tokens(mu[:, :], 2), ALU.subtract)\
                        .then_inc(ln_cent, 1)
                ve.wait_ge(ln_acc, 8 * (n + 1))

            def split_input(n, terms, affine, links):
                def make(i):
                    buf = sc[:, bass.ds((i % 2) * 2 * T, 2 * T)]
                    frm = X[:, bass.ds(i * 2 * T, 2 * T)]
                    for row, op in terms:
                        own.link(ve.tensor_tensor(tiles(buf, 2), tiles(frm, 2), over_tokens(row, 2), op))
                        frm = buf
                    for j in range(2):
                        src = buf if terms else frm
                        ins = affine(sc[:, bass.ds((i % 2) * 2 * T + j * T, T)],
                                     sc[:, bass.ds((i % 2) * 2 * T + j * T, T)] if terms
                                     else X[:, bass.ds(i * 2 * T + j * T, T)], 2 * i + j)
                        own.link(ins)
                    ve.sem_inc(ln_y, 1)

                def finish(i):
                    ve.wait_ge(ln_hi, i + (8 * n + 1))
                    to, hi = (tiles(t[:, bass.ds(i * 2 * TM, 2 * TM)], 2)[:, :, META:TM] for t in (a_lo, a_hi))
                    sub_hi(to, tiles(sc[:, bass.ds((i % 2) * 2 * T, 2 * T)], 2), hi).then_inc(ln_lo, 1)

                make(0)
                with own.loop(1, KT // 2, links) as i:
                    make(i)
                    finish(i - 1)
                    ve.wait_ge(ln_lo, i + 8 * n)
                finish(KT // 2 - 1)

            ve.memset(ones[:, :], 1.0).then_inc(ones_set, 1)
            clear_ada(0)
            split(0, 0)
            split(1, 1)
            ve.wait_ge(small, SMALL)
            ve.tensor_tensor(sc[:, 0:KT * META], mt[:, :], mt[:, :], ALU.mult).then_inc(m_sq, 1)
            two_pi = 2.0 * np.pi
            c1 = float(np.float32(6.28125))
            c2 = float(np.float32(np.float32((two_pi - c1) * 2 ** 20).astype(np.int64) / 2 ** 20))
            c2 = float(np.round((two_pi - c1) * 2.0 ** 17) / 2.0 ** 17)
            c3 = float(np.float32(two_pi - c1 - c2))
            freq, phase, sign = (con[:, 2 * P + i:2 * P + i + 1] for i in range(3))
            magic = 1.5 * 2.0 ** 23
            ang, turns_ = zs, mu
            own.link(ve.tensor_copy(ang[:, :], pos))
            own.link(ve.tensor_scalar(ang[:, :], ang[:, :], freq, None, ALU.mult))
            own.link(ve.tensor_scalar(sc[:, T:2 * T], ang[:, :], phase, 1.0 / two_pi, ALU.add, ALU.mult))
            own.link(ve.tensor_scalar(turns_[:, :], sc[:, T:2 * T], magic, None, ALU.add))
            own.link(ve.tensor_scalar(turns_[:, :], turns_[:, :], magic, None, ALU.subtract))
            for c in (c1, c2, c3):
                own.link(ve.scalar_tensor_tensor(out=ang[:, :], in0=turns_[:, :], scalar=-c, in1=ang[:, :],
                                                 op0=ALU.mult, op1=ALU.add))
            own.link(ve.tensor_scalar(ang[:, :], ang[:, :], phase, None, ALU.add))
            ve.tensor_scalar(ang[:, :], ang[:, :], float(np.float32(3.1415925)), float(np.float32(-3.1415925)),
                             ALU.min, ALU.max).then_inc(rope_arg, 1)
            ve.wait_ge(c_tanh, 1)
            own.link(ve.scalar_tensor_tensor(out=csil[:, KT:2 * KT], in0=csil[:, 0:KT], scalar=1.0,
                                             in1=v("c", 0, KT), op0=ALU.add, op1=ALU.mult))
            own.link(ve.tensor_scalar(csil[:, KT:2 * KT], csil[:, KT:2 * KT], 0.5, None, ALU.mult))
            ve.wait_ge(rope_sin, 1)
            own.link(ve.tensor_scalar(rope[:, :], rope[:, :], sign, None, ALU.mult))
            ve.wait_ge(m_acc, 1)
            rstd("meta", [(rs[:, 0:META], bank(5, 0, META), D)], 1e-6)
            own.link(ve.tensor_tensor(mt[:, :].rearrange("p (k t) -> p k t", k=KT),
                                      mt[:, :].rearrange("p (k t) -> p k t", k=KT),
                                      rs[:, 0:META].unsqueeze(1).to_broadcast([P, KT, META]), ALU.mult))
            ve.tensor_tensor(mt[:, :].rearrange("p (k t) -> p k t", k=KT),
                             mt[:, :].rearrange("p (k t) -> p k t", k=KT),
                             v("g_pre_mix", 0, KT).unsqueeze(2).to_broadcast([P, KT, META]), ALU.mult)\
                .then_inc(am_y, 1)
            centre(0, True)
            rstd("pre0", [(rs[:, 0:T], bank(6, T), D)], 1e-6)
            ve.wait_ge(ln_cent, 8)
            for i in range(4):
                s = X[:, i * 4 * T:(i + 1) * 4 * T]
                own.link(ve.tensor_tensor(tiles(s, 4), tiles(s, 4), over_tokens(rs[:, 0:T], 4), ALU.mult))
            for r in range(2):
                with ve.Fori(0, KT // 2) as i:
                    for par in range(2):
                        add_ada(2 * i + (KT * r + par), par)
                read_mod(r)

            def modulate(l):
                def affine(o, frm, m):
                    return ve.tensor_scalar(o, frm, mod[:, bass.ds(m + (3 * l + 1) * KT, 1)],
                                            mod[:, bass.ds(m + 3 * l * KT, 1)], ALU.mult, ALU.add)
                return affine

            split_input(0, (), modulate(0), 2)

            for l in range(DEPTH):
                G = l * PER_LAYER
                A = (2 + 3 * l) * KT
                for m in range(LAT):
                    if m < QT + CT:
                        ve.wait_ge(lat_sq, 6 * l + m + 1)
                        acc = sc[:, 0:T] if m < QT else sc[:, T:2 * T]
                        if m:
                            ve.wait_ge(lat_acc, 6 * l + m)
                        if m in (0, QT):
                            ve.tensor_copy(acc, sc[:, 2 * T:3 * T]).then_inc(lat_acc, 1)
                        else:
                            ve.tensor_tensor(acc, acc, sc[:, 2 * T:3 * T], ALU.add).then_inc(lat_acc, 1)
                    else:
                        ve.wait_ge(weights_used, G + m + 1)
                        ve.tensor_tensor(sc[:, 3 * T:4 * T], bank(7), rope[:, :], ALU.mult).then_inc(kr_rot, 1)
                    split(G + m + 2, (G + m) % 2, dft=m + 2 == L_DFT)
                    add_ada(A + m, (A + m) % 2)
                after(G + L_DFT, G + L_DFT)
                add_ada(A + LAT, (A + LAT) % 2)
                ve.wait_ge(lat_stat, l + 1)
                rs_parts = [(rs[:, 0:T], bank(3), QT * P), (rs[:, T:2 * T], bank(3, T), CT * P)]

                def cw(j):
                    b, trig, g4 = (0, 1, 2, 7)[j], j // 2, j % 2
                    to, hi = (t[:, g4 * 4 * T:(g4 + 1) * 4 * T].rearrange("p (g c) -> p g c", g=4)
                              [:, :, trig * P:(trig + 1) * P] for t in (cw_lo, cw_hi))
                    ve.wait_ge(cw_h, 4 * l + j + 1)
                    sub_hi(to, bank(b, 0, 512).rearrange("p (g c) -> p g c", g=4), hi).then_inc(cw_l, 1)

                cw(0)
                cw(1)
                after(G + L_FMIX, G + L_FMIX)
                cw(2)
                cw(3)
                rstd(f"lat{l}", rs_parts, 1e-6)
                ve.wait_ge(kr_h, l + 1)
                sub_hi(kr_lo[:, :], bank(3), kr_hi[:, :]).then_inc(kr_l, 1)
                for m in range(QT + CT):
                    gain = v("q_norm", l * QT + m) if m < QT else v("kv_norm", l * CT + m - QT)
                    row = rs[:, 0:T] if m < QT else rs[:, T:2 * T]
                    ve.scalar_tensor_tensor(out=sc[:, (m % 2) * T:(m % 2 + 1) * T],
                                            in0=lat_ps(m), scalar=gain,
                                            in1=row, op0=ALU.mult, op1=ALU.mult).then_inc(lat_y, 1)
                    ve.wait_ge(lat_h, 6 * l + m + 1)
                    s = slice(m * T, (m + 1) * T)
                    sub_hi(lat_lo[:, s], sc[:, (m % 2) * T:(m % 2 + 1) * T], lat_hi[:, s]).then_inc(lat_l, 1)

                def y_tile(t, o):
                    ve.scalar_tensor_tensor(out=sc[:, 2 * T:3 * T], in0=o, scalar=0.5, in1=zs[:, :],
                                            op0=ALU.mult, op1=ALU.mult).then_inc(y_mul, 1)

                def y_rest(t):
                    ve.wait_ge(y_h, 16 * l + t + 1)
                    sub_hi(y_lo[:, bass.ds(t * T, T)], sc[:, 2 * T:3 * T], y_hi[:, bass.ds(t * T, T)])\
                        .then_inc(y_l, 1)

                def gate(t, b):
                    ve.wait_ge(z_tanh, 16 * l + t + 1)
                    ve.scalar_tensor_tensor(out=zs[:, :], in0=th[:, 0:T], scalar=1.0, in1=bank(b),
                                            op0=ALU.add, op1=ALU.mult).then_inc(z_ready, 1)

                def group(q, first, with_ada):
                    g, g0 = G + L_FOUR + 2 * q, G + L_FOUR
                    ve.wait_ge(u_h, 8 * l + q + 1)
                    sub_hi(u_lo, bank(0), u_hi).then_inc(u_l, 1)
                    after(g, g0)
                    if not first:
                        ve.wait_ge(yf_ps, 8 * l + q)
                        ve.wait_ge(z_ready, 16 * l + q)
                        y_tile(q - 1, bank(2))
                        y_rest(q - 1)
                    if with_ada:
                        add_ada(2 * q + (A + GROUPS), 0)
                    gate(q, 1)
                    after(g + 1, g0 + 1)
                    if with_ada:
                        add_ada(2 * q + (A + GROUPS + 1), 1)
                    ve.wait_ge(t_h, 8 * l + q + 1)
                    sub_hi(t_lo, bank(3, 0, 2 * T), t_hi).then_inc(t_l, 1)

                group(0, True, True)
                with ve.Fori(1, GROUPS // 2) as q:
                    group(q, False, True)
                read_mod(3 * l + 2)
                with ve.Fori(GROUPS // 2, GROUPS) as q:
                    group(q, False, l == 0)
                ve.wait_ge(yf_ps, 8 * (l + 1))
                ve.wait_ge(z_ready, 16 * l + GROUPS)
                y_tile(GROUPS - 1, bank(2))
                y_rest(GROUPS - 1)

                def turned(h):
                    ve.wait_ge(pt_h, 8 * l + h + 1)
                    sub_hi(pt_lo, bank(3, 0, 2 * T), pt_hi).then_inc(pt_l, 1)

                def head(h, first, with_ada):
                    g, g0 = G + L_HEAD + 2 * h, G + L_HEAD
                    ve.wait_ge(q_h, 3 * (8 * l + h) + 1)
                    ve.tensor_tensor(sc[:, 3 * T:4 * T], bank(0, T), rope[:, :], ALU.mult).then_inc(qr_rot, 1)
                    sub_hi(qn_lo, bank(0), qn_hi).then_inc(q_l, 1)
                    ve.wait_ge(q_h, 3 * (8 * l + h) + 2)
                    sub_hi(kn_lo, bank(1), kn_hi).then_inc(q_l, 1)
                    ve.wait_ge(q_h, 3 * (8 * l + h) + 3)
                    sub_hi(qr_lo, sc[:, 3 * T:4 * T], qr_hi).then_inc(q_l, 1)
                    after(g, g0)
                    if with_ada:
                        add_ada(2 * h + (A + 3 * GROUPS), 0)
                    if not first:
                        turned(h - 1)
                        ve.wait_ge(o_ps, 8 * l + h)
                        ve.wait_ge(z_ready, 16 * l + GROUPS + h)
                        y_tile(GROUPS + h - 1, bank(4))
                        ve.wait_ge(y_mul, 16 * l + GROUPS + h)
                    gate(GROUPS + h, 2)
                    ve.wait_ge(v_h, 8 * l + h + 1)
                    sub_hi(vv_lo, bank(1, T), vv_hi).then_inc(v_l, 1)
                    if not first:
                        y_rest(GROUPS + h - 1)
                    ve.wait_ge(s_ps, 8 * l + h + 1)
                    own.link(ve.tensor_reduce(stat[:, 0:2], bank(5, 0, 2 * T).rearrange("p (q k) -> p q k", q=2),
                                              AX.X, ALU.max))
                    ve.tensor_scalar(stat[:, 2:4], stat[:, 0:2], -SM_SCALE, None, ALU.mult).then_inc(s_max, 1)
                    ve.wait_ge(s_exp, 2 * (8 * l + h) + 2)
                    own.link(ve.reciprocal(stat[:, 6:8], stat[:, 4:6]))
                    for qt in range(2):
                        s = sc[:, qt * T:(qt + 1) * T]
                        o = ve.tensor_scalar(s, s, stat[:, 6 + qt:7 + qt], None, ALU.mult)
                        if qt == 0:
                            own.link(o)
                    o.then_inc(p_ready, 1)
                    after(g + 1, g0 + 1)
                    if with_ada:
                        add_ada(2 * h + (A + 3 * GROUPS + 1), 1)

                head(0, True, l == 0)
                with own.loop(1, HEADS // 2, 3) as h:
                    head(h, False, l == 0)
                if l == 0:
                    read_mod(3)
                with own.loop(HEADS // 2, HEADS, 3) as h:
                    head(h, False, False)

                def out_tile(i, b):
                    g = G + L_OUT
                    m = 2 * i + b
                    ve.wait_ge(g_tmp, m + (16 * l + 1))
                    xm = X[:, bass.ds(m * T, T)]
                    ve.scalar_tensor_tensor(out=xm, in0=xm, scalar=ALPHA, in1=sc[:, b * T:(b + 1) * T],
                                            op0=ALU.mult, op1=ALU.add).then_inc(g_mul, 1)
                    after(m + g, g + b)
                    if l == 0:
                        add_ada(m + (A + 2 * KT), b)

                turned(HEADS - 1)
                ve.wait_ge(o_ps, 8 * (l + 1))
                ve.wait_ge(z_ready, 16 * (l + 1))
                y_tile(2 * HEADS - 1, bank(4))
                y_rest(2 * HEADS - 1)
                if l == 0:
                    ve.wait_ge(x_back, 16)
                with ve.Fori(0, KT // 2) as i:
                    for b in range(2):
                        out_tile(i, b)
                if l == 0:
                    read_mod(4)
                ve.wait_ge(g_mul, 16 * (l + 1))
                centre(2 * l + 1, True)
                rstd(f"post{l}", [(rs[:, 0:T], bank(6, T), D)], 1e-6)
                ve.wait_ge(ln_cent, 8 * (2 * l + 2))
                for i in range(4):
                    s = X[:, i * 4 * T:(i + 1) * 4 * T]
                    own.link(ve.tensor_tensor(tiles(s, 4), tiles(s, 4), over_tokens(rs[:, 0:T], 4), ALU.mult))
                for m in range(KT):
                    s = X[:, m * T:(m + 1) * T]
                    o = ve.tensor_scalar(s, s, v("ln_g", l * KT + m), v("ln_b", l * KT + m), ALU.mult, ALU.add)
                    if m < KT - 1:
                        own.link(o)
                o.then_inc(x_norm, 1)
                ve.wait_ge(x_norm, l + 1)
                if l == 0:
                    centre(2, False)
                    rstd("pre1", [(rs[:, 0:T], bank(6, T), D)], 1e-6)
                    split_input(1, ((mu[:, :], ALU.subtract), (rs[:, 0:T], ALU.mult)), modulate(1), 4)

            ve.wait_ge(ln_acc, 8 * 4 + 8)
            rstd("mix", [(rs[:, 0:T], bank(6, T), D)], 1e-6)

            def pre_mix(o, frm, m):
                return ve.tensor_scalar(o, frm, v("g_pre_mix", m), None, ALU.mult)

            split_input(2, ((rs[:, 0:T], ALU.mult),), pre_mix, 3)
            ve.wait_ge(am_h, 1)
            lo3, hi3 = (t[:, :].rearrange("p (k t) -> p k t", k=KT)[:, :, 0:META] for t in (a_lo, a_hi))
            sub_hi(lo3, mt[:, :].rearrange("p (k t) -> p k t", k=KT), hi3).then_inc(am_l, 1)

            ahead = TAPS - 1 - META
            ve.wait_ge(ada_summed, 3 * DEPTH)
            own.link(ve.memset(pad[:, 0:ahead], 0.0))

            def taps(j, lo, hi):
                acc = conv_out[:, bass.ds(j * T, T)]
                for k in range(lo, hi):
                    w = v("w_dw", j * TAPS + k)
                    if k == 0:
                        own.link(ve.tensor_scalar(acc, pad[:, 0:T], w, None, ALU.mult))
                    else:
                        own.link(ve.scalar_tensor_tensor(out=acc, in0=pad[:, k:k + T], scalar=w, in1=acc,
                                                         op0=ALU.mult, op1=ALU.add))

            after(B2_CONV, B2_CONV)
            with own.loop(0, CONV, TAPS) as j:
                g = B2_CONV + 2 * j
                ve.wait_ge(cv_tanh, j + 1)
                ve.scalar_tensor_tensor(out=pad[:, ahead:ahead + TM], in0=th[:, :], scalar=1.0, in1=bank(0, 0, TM),
                                        op0=ALU.add, op1=ALU.mult).then_inc(cv_in, 1)
                after(g + 1, B2_CONV + 1)
                ve.wait_ge(cv_in, j + 1)
                taps(j, 0, TAPS // 2)
                after(g + 2, B2_CONV)
                taps(j, TAPS // 2, TAPS)
                acc = conv_out[:, bass.ds(j * T, T)]
                ve.tensor_scalar(acc, acc, 0.5, v("b_dw", j), ALU.mult, ALU.add).then_inc(cv_done, 1)
            for j in range(CONV):
                if j:
                    after(B2_POOL + j, B2_POOL + j)
                ve.wait_ge(pl_in, j + 1)
                w = WINDOWS[j // 2]
                src, n, bufs = pool_z, 1, (pool_a, pool_b)
                while n < w:
                    to, first = bufs[0], 2 * n - 1
                    own.link(ve.tensor_tensor(to[:, first:TM], src[:, first:TM], src[:, first - n:TM - n], ALU.add))
                    src, n, bufs = to, 2 * n, bufs[::-1]
                ve.scalar_tensor_tensor(out=zs[:, :], in0=src[:, META:TM], scalar=1.0 / w, in1=pool_z[:, META:TM],
                                        op0=ALU.mult, op1=ALU.subtract).then_inc(pl_sum, 1)
                ve.wait_ge(pl_h, j + 1)
                s = slice(j * T, (j + 1) * T)
                sub_hi(y_lo[:, s], zs[:, :], y_hi[:, s]).then_inc(pl_l, 1)
            for i, m in enumerate((0, 2, 4, 6, 1, 3, 5, 7)):
                ve.wait_ge(gp_h, i + 1)
                s = slice((CONV + m) * T, (CONV + m + 1) * T)
                ve.scalar_tensor_tensor(out=y_lo[:, s], in0=bank(2 + m // 2, (m % 2) * T), scalar=v("pool_scale", m),
                                        in1=y_hi[:, s].bitcast(F32), op0=ALU.mult, op1=ALU.subtract).then_inc(gp_l, 1)
            after(B2_GRP, B2_GRP)
            ve.wait_ge(cm_ps, 1)
            own.link(ve.tensor_scalar(mu[:, :], bank(6), 1.0 / (CONV * P), None, ALU.mult))
            for i in range(CONV // 2):
                s = tiles(conv_out[:, 2 * i * T:(2 * i + 2) * T], 2)
                ve.tensor_tensor(s, s, over_tokens(mu[:, :], 2), ALU.subtract).then_inc(cm_cent, 1)
            ve.wait_ge(cm_cent, CONV // 2)
            ve.wait_ge(cm_acc, 1)
            rstd("conv", [(rs[:, 0:T], bank(6, T), CONV * P)], 1e-5)
            after(B2_GATE, B2_GATE)
            for k in range(CONV):
                c = conv_out[:, k * T:(k + 1) * T]
                own.link(ve.tensor_tensor(c, c, rs[:, 0:T], ALU.mult))
                ve.tensor_scalar(c, c, v("conv_ln_g", k), v("conv_ln_b", k), ALU.mult, ALU.add).then_inc(cn_y, 1)
                ve.wait_ge(cn_tanh, k + 1)
                ve.scalar_tensor_tensor(out=zs[:, :], in0=th[:, 0:T], scalar=1.0, in1=c, op0=ALU.add,
                                        op1=ALU.mult).then_inc(cn_mul, 1)
                ve.wait_ge(cn_h, k + 1)
                s = slice(k * T, (k + 1) * T)
                ve.scalar_tensor_tensor(out=y_lo[:, s], in0=zs[:, :], scalar=0.5, in1=y_hi[:, s].bitcast(F32),
                                        op0=ALU.mult, op1=ALU.subtract).then_inc(cn_l, 1)

            def gate_rest(m, b):
                g, g0 = B2_GATE + 3 * m, B2_GATE + 3 * b
                after(g + 1, g0 + 1)
                ve.wait_ge(weights_used, g + 3)
                own.link(ve.scalar_tensor_tensor(out=sc[:, 2 * T:3 * T], in0=sc[:, 0:T], scalar=1.0, in1=bank(2),
                                                 op0=ALU.add, op1=ALU.mult))
                own.link(ve.scalar_tensor_tensor(out=sc[:, 3 * T:4 * T], in0=sc[:, T:2 * T], scalar=1.0, in1=bank(3),
                                                 op0=ALU.add, op1=ALU.mult))
                ve.tensor_tensor(wide[:, bass.ds(m * T, T)], sc[:, 2 * T:3 * T], sc[:, 3 * T:4 * T], ALU.add)\
                    .then_inc(gt_done, 1)
                after(g + 2, g0 + 2)

            gate_rest(0, 0)
            after(B2_GATE + 3, B2_GATE + 3)
            gate_rest(1, 1)
            with own.loop(1, KT // 2, 4) as i:
                for b in range(2):
                    ve.wait_ge(gt_tanh, 2 * (2 * i + b) + 1)
                    after(B2_GATE + 3 * (2 * i + b), B2_GATE + 3 * b)
                    gate_rest(2 * i + b, b)
            ve.wait_ge(gt_done, KT)
            for i in range(4):
                ve.wait_ge(mm_h, i + 1)
                to, hi = (t[:, i * 4 * TM:(i + 1) * 4 * TM].rearrange("p (k t) -> p k t", k=4)[:, :, META:TM]
                          for t in (a_lo, a_hi))
                ve.scalar_tensor_tensor(out=to, in0=tiles(wide[:, i * 4 * T:(i + 1) * 4 * T], 4), scalar=0.5,
                                        in1=hi.bitcast(F32), op0=ALU.mult, op1=ALU.subtract).then_inc(mm_l, 1)

            def wo_tile(i, b, first):
                m = 2 * i + b
                ve.wait_ge(wo_sq, m + 1)
                s = sc[:, b * T:(b + 1) * T]
                if first and b == 0:
                    ve.tensor_copy(mu[:, :], s).then_inc(wo_acc, 1)
                else:
                    ve.wait_ge(wo_acc, m)
                    ve.tensor_tensor(mu[:, :], mu[:, :], s, ALU.add).then_inc(wo_acc, 1)
                after(m + B2_WO, B2_WO + b)

            for b in range(2):
                wo_tile(0, b, True)
            with ve.Fori(1, KT // 2) as i:
                for b in range(2):
                    wo_tile(i, b, False)
            ve.wait_ge(wo_stat, 1)
            ve.wait_ge(wo_out, KT)
            rstd("wo", [(rs[:, 0:T], bank(6), D)], 1e-6)

            def new_h(m, par):
                buf = sc[:, par * T:(par + 1) * T]
                xm = X[:, bass.ds(m * T, T)]
                own.link(ve.scalar_tensor_tensor(out=buf, in0=wide[:, bass.ds(m * T, T)],
                                                 scalar=v("g_post_mix", m), in1=rs[:, 0:T],
                                                 op0=ALU.mult, op1=ALU.mult))
                ve.tensor_tensor(xm, xm, buf, ALU.add).then_inc(h_new, 1)

            def rest_h(m, par, first):
                ve.wait_ge(h_hi, m + 1)
                ve.wait_ge(h_new, m + 1)
                ve.scalar_tensor_tensor(out=a_tile(a_lo, m), in0=X[:, bass.ds(m * T, T)], scalar=v("g_pre_mlp", m),
                                        in1=a_tile(a_hi, m).bitcast(F32), op0=ALU.mult, op1=ALU.subtract)\
                    .then_inc(h_lo, 1)
                ve.wait_ge(h_sq, m + 1)
                s = sc[:, (2 + par) * T:(3 + par) * T]
                if first:
                    ve.tensor_copy(mu[:, :], s).then_inc(h_acc, 1)
                else:
                    ve.wait_ge(h_acc, m)
                    ve.tensor_tensor(mu[:, :], mu[:, :], s, ALU.add).then_inc(h_acc, 1)

            new_h(0, 0)
            new_h(1, 1)
            rest_h(0, 0, True)
            with own.loop(1, KT // 2, 2) as i:
                for b in range(2):
                    new_h(2 * i + b, b)
                    rest_h(2 * i + b - 1, 1 - b, False)
            rest_h(KT - 1, 1, False)

            def up(f, i, b):
                m = 16 * f + 2 * i + b
                g = B2_FF + 32 * f + 2 * i + b
                r, s = sc[:, b * T:(b + 1) * T], sc[:, (2 + b) * T:(3 + b) * T]
                ve.wait_ge(f_relu, m + 1)
                ve.tensor_tensor(s, r, r, ALU.mult).then_inc(f_sq, 1)
                ve.wait_ge(f_sq, m + 1)
                ve.wait_ge(f_hi, m + 1)
                at = bass.ds((2 * i + b) * T, T)
                sub_hi(y_lo[:, at], s, y_hi[:, at]).then_inc(f_lo, 1)
                after(g, B2_FF + b)

            def down(f, i, b, last=False):
                m = 16 * f + 2 * i + b
                g = B2_FF + KT + 32 * f + 2 * i + b
                ve.wait_ge(weights_used, g + 1)
                o = wide[:, bass.ds((2 * i + b) * T, T)]
                if isinstance(f, int) and f == 0:
                    ve.tensor_copy(o, bank(2 + b)).then_inc(f_acc, 1)
                else:
                    ve.wait_ge(f_acc, m - 15)
                    ve.tensor_tensor(o, o, bank(2 + b), ALU.add).then_inc(f_acc, 1)
                if not last:
                    after(g, B2_FF + b)

            with ve.Fori(0, KT // 2) as i:
                for b in range(2):
                    up(0, i, b)
            ve.wait_ge(h_stat, 1)
            own.link(ve.tensor_scalar(rs[:, 0:T], bank(6, T), 1.0 / D, 1e-6, ALU.mult, ALU.add))
            own.link(ve.reciprocal(rs[:, 0:T], rs[:, 0:T]))
            with ve.Fori(0, KT // 2) as i:
                for b in range(2):
                    down(0, i, b)
            with ve.Fori(1, FF_BLOCKS - 1) as f:
                with ve.Fori(0, KT // 2) as i:
                    for b in range(2):
                        up(f, i, b)
                with ve.Fori(0, KT // 2) as i:
                    for b in range(2):
                        down(f, i, b)
            f = FF_BLOCKS - 1
            with ve.Fori(0, KT // 2) as i:
                for b in range(2):
                    up(f, i, b)
            with ve.Fori(0, KT // 2 - 1) as i:
                for b in range(2):
                    down(f, i, b)
            for b in range(2):
                down(f, KT // 2 - 1, b, True)
            ve.wait_ge(f_osum, KT // 2)
            own.link(ve.tensor_tensor(mu[:, :], rs[:, 0:T], rs[:, 0:T], ALU.mult))
            own.link(ve.scalar_tensor_tensor(out=rs[:, T:2 * T], in0=bank(6), scalar=1.0 / D, in1=mu[:, :],
                                             op0=ALU.mult, op1=ALU.mult))
            ve.tensor_scalar(rs[:, T:2 * T], rs[:, T:2 * T], 1e-6, None, ALU.add).then_inc(ln_var, 1)
            ve.wait_ge(ln_std, NORM["out"] + 1)
            own.link(ve.reciprocal(rs[:, T:2 * T], rs[:, T:2 * T]))
            own.link(ve.tensor_tensor(rs[:, 0:T], rs[:, 0:T], rs[:, T:2 * T], ALU.mult))
            ve.wait_ge(f_acc, 16 * FF_BLOCKS)
            for m in range(KT):
                s = slice(m * T, (m + 1) * T)
                t = sc[:, (m % 4) * T:(m % 4 + 1) * T]
                own.link(ve.scalar_tensor_tensor(out=t, in0=wide[:, s], scalar=v("g_post_mlp", m),
                                                 in1=rs[:, 0:T], op0=ALU.mult, op1=ALU.mult))
                ve.tensor_tensor(X[:, s], X[:, s], t, ALU.add).then_inc(y_out, 1)


def by_tile(w):
    k, n = w.shape
    return w.reshape(k // P, P, n // P, P).transpose(2, 1, 0, 3).reshape(n // P, P, k)


def padded(chunks):
    out = np.zeros((chunks.shape[0], P, CH), np.float32)
    out[:, :, :chunks.shape[2]] = chunks
    return out


def columns(a):
    return np.asarray(a).reshape(-1, P).T


def swap_halves(w):
    h = ROPE // 2
    return np.concatenate([w[..., h:], w[..., :h]], axis=-1)


def dft(n):
    k = np.outer(np.arange(n), np.arange(n)) % n
    return (np.cos(2 * np.pi * k / n) / np.sqrt(n)), (np.sin(2 * np.pi * k / n) / np.sqrt(n))


def weight_stream(i):
    parts = []
    cos_s, sin_s = dft(T)
    cos_c, sin_c = dft(P)
    seq = np.concatenate([t.reshape(2, P, T).transpose(1, 0, 2).reshape(P, 2 * T) for t in (cos_s, -sin_s)], axis=1)
    seq = seq.astype(np.float32)
    chan = np.concatenate([cos_c, sin_c], axis=1).astype(np.float32)
    for l in range(DEPTH):
        w = np.asarray(i["w_in"][l])
        u, z, cq, ckv, kr, za = np.split(w, np.cumsum([1024, 1024, 512, 256, ROPE]), axis=1)
        parts.append(by_tile(np.concatenate([cq, ckv, kr, swap_halves(kr)], axis=1)))
        parts.append(padded(seq[None]))
        fm = np.asarray(i["w_fmix"][l]).transpose(1, 0, 2).reshape(P, GROUPS * P)
        parts.append(padded(np.concatenate([fm, chan], axis=1)[None]))
        parts.append(np.stack([by_tile(u), by_tile(z)], axis=1).reshape(2 * GROUPS, P, CH))
        wq = np.asarray(i["w_q_b"][l]).reshape(QT, P, HEADS, P + ROPE)
        wkv = np.asarray(i["w_kv_b"][l]).reshape(CT, P, HEADS, 2, P)
        nope, rp = wq[..., :P], wq[..., P:]
        rp = np.concatenate([rp, swap_halves(rp)], axis=-1)
        head = np.concatenate([nope, rp, wkv[:, :, :, 0], wkv[:, :, :, 1]], axis=0)
        head = head.transpose(2, 1, 0, 3).reshape(HEADS, P, 12 * P)
        parts.append(np.stack([padded(head), by_tile(za)], axis=1).reshape(2 * HEADS, P, CH))
        parts.append(by_tile(np.asarray(i["w_out"][l])))
    w = by_tile(np.asarray(i["w_in_2"][0]))
    z, val, gat, ga, gb = np.split(w, np.cumsum([CONV, CONV, CONV, KT]), axis=0)
    parts.append(np.stack([val, gat], axis=1).reshape(2 * CONV, P, CH))
    parts.append(z)
    grp = np.asarray(i["w_pool_grp_2"][0]).reshape(4, 2, P, 2, P)
    parts.append(grp.transpose(2, 0, 3, 1, 4).reshape(1, P, CH))
    po, co = (np.asarray(i[n][0]).reshape(CONV, P, KT, P).transpose(2, 1, 0, 3).reshape(KT, P, HALF)
              for n in ("w_pool_out_2", "w_conv_out_2"))
    parts.append(np.stack([ga, gb, np.concatenate([po, co], axis=2)], axis=1).reshape(3 * KT, P, CH))
    parts.append(by_tile(np.asarray(i["w_o_2"][0])))
    up = by_tile(np.asarray(i["w_up_2"][0])).reshape(FF_BLOCKS, KT, P, CH)
    down = np.asarray(i["w_down_2"][0]).reshape(FF_BLOCKS, KT, P, KT, P).transpose(0, 3, 2, 1, 4)
    parts.append(np.concatenate([up, down.reshape(FF_BLOCKS, KT, P, CH)], axis=1).reshape(-1, P, CH))
    return np.concatenate(parts, axis=0)


def kernel(**i):
    import concourse.bacc as bacc
    from concourse.bass_utils import run_bass_kernel_spmd

    def f32(name):
        return np.asarray(i[name])

    stream = weight_stream(i)
    assert stream.shape == (CHUNKS, P, CH), stream.shape
    ada = f32("w_ada").reshape(DEPTH, KT, P, 3, D).transpose(0, 3, 1, 2, 4).reshape(ADA, P, D)
    taps = f32("w_dw_2")[0].reshape(TAPS, CONV, P).transpose(1, 0, 2)
    named = {"c": f32("c"), "b_ada": f32("b_ada"), "q_norm": f32("q_norm"), "kv_norm": f32("kv_norm"),
             "ln_g": f32("ln_g"), "ln_b": f32("ln_b"), "g_pre_mix": f32("g_pre_mix_2"),
             "pool_scale": f32("pool_scale_2"), "w_dw": taps, "b_dw": f32("b_dw_2"),
             "conv_ln_g": f32("conv_ln_g_2"), "conv_ln_b": f32("conv_ln_b_2"),
             "g_post_mix": f32("g_post_mix_2"), "g_pre_mlp": f32("g_pre_mlp_2"), "g_post_mlp": f32("g_post_mlp_2")}
    vectors = np.concatenate([columns(named[n]) for n, _ in VECTORS], axis=1)
    p = np.arange(P)
    freq = np.float32(10000.0) ** (-np.arange(0, ROPE, 2, dtype=np.float32) / np.float32(ROPE))
    consts = np.concatenate([
        np.eye(P), (p[:, None] % ROPE == p[None] % ROPE), freq[p % (ROPE // 2)][:, None],
        np.where(p < ROPE, np.pi / 2, 0.0)[:, None],
        np.where((p >= ROPE) & (p < ROPE + ROPE // 2), -1.0, 1.0)[:, None]], axis=1).astype(np.float32)
    positions = np.ascontiguousarray(np.broadcast_to(np.asarray(i["positions"]).astype(np.int32), (P, T)))
    x = f32("x")[0].reshape(T, KT, P).transpose(2, 1, 0).reshape(P, KT * T)
    meta = f32("meta_2").reshape(META, KT, P).transpose(2, 1, 0).reshape(P, KT * META)
    arrays = {"stream": stream, "ada": ada, "vectors": vectors, "consts": consts, "positions": positions,
              "x": x, "meta": meta}
    nc = bacc.Bacc("TRN2", target_bir_lowering=False, num_devices=1)
    aps = {}
    for name, a in arrays.items():
        arrays[name] = a = np.ascontiguousarray(a)
        aps[name] = nc.dram_tensor(f"in_{name}", a.shape, mybir.dt.from_np(a.dtype), kind="ExternalInput").ap()
    out = nc.dram_tensor("out", (P, KT * T), F32, kind="ExternalOutput").ap()
    build(nc, **aps, out=out)
    r = run_bass_kernel_spmd(nc, [{f"in_{n}": a for n, a in arrays.items()}], core_ids=[0])
    y = np.asarray(r.results[0]["out"])
    return y.reshape(P, KT, T).transpose(2, 1, 0).reshape(1, T, D)
```

```python
from contextlib import ExitStack, contextmanager

import numpy as np
import concourse.bass as bass
from concourse import mybir

F32 = mybir.dt.float32
F32R = mybir.dt.float32r
I32 = mybir.dt.int32
ALU = mybir.AluOpType
ACT = mybir.ActivationFunctionType
AX = mybir.AxisListType

P = 128
T = 256
META = 16
TM = T + META
D = 2048
KT = D // P
DEPTH = 2
HEADS = 8
GROUPS = 8
ROPE = 64
QT = 512 // P
CT = 256 // P
LAT = QT + CT + 1
CONV = 1024 // P
TAPS = 31
WINDOWS = (2, 4, 8, 16)
FF_BLOCKS = 8192 // D
ALPHA = (2 * DEPTH) ** 0.25
SM_SCALE = 1.0 / float(np.sqrt(192.0))

CH = 16 * P
HALF = CH // 2
RAW = 3

L_DFT = LAT
L_FMIX = LAT + 1
L_FOUR = LAT + 2
L_HEAD = L_FOUR + 2 * GROUPS
L_OUT = L_HEAD + 2 * HEADS
PER_LAYER = L_OUT + KT
B2_MIX = DEPTH * PER_LAYER
MIX = 5
B2_GRP = B2_MIX + MIX * CONV
B2_GATE = B2_GRP + 1
B2_WO = B2_GATE + 2 * KT
B2_FF = B2_WO + KT
CHUNKS = B2_FF + 2 * KT * FF_BLOCKS
ADA = 3 * DEPTH * KT
ADA0 = 2 * KT

VECTORS = (("c", KT), ("b_ada", 3 * DEPTH * KT), ("q_norm", DEPTH * QT), ("kv_norm", DEPTH * CT),
           ("ln_g", DEPTH * KT), ("ln_b", DEPTH * KT), ("g_pre_mix", KT), ("pool_scale", CONV),
           ("w_dw", TAPS * CONV), ("b_dw", CONV), ("conv_ln_g", CONV), ("conv_ln_b", CONV),
           ("g_post_mix", KT), ("g_pre_mlp", KT), ("g_post_mlp", KT))
COL = {}
NV = 0
for _name, _n in VECTORS:
    COL[_name] = NV
    NV += _n
NC_ = 2 * P + 3


class Chain:

    def __init__(self, eng, sem):
        self.eng, self.sem, self.n, self.i, self.per = eng, sem, 0, None, 0

    def link(self, ins, lag=0):
        self.n += 1
        ins.then_inc(self.sem, 1)
        n = self.n - lag
        self.eng.wait_ge(self.sem, n if self.i is None else self.i * self.per + n)

    @contextmanager
    def loop(self, start, end, per):
        base = self.n
        with self.eng.Fori(start, end) as i:
            self.i, self.per, self.n = i, per, base - start * per
            yield i
            assert self.n == base - start * per + per, (self.n - base + start * per, per)
        self.i, self.n = None, base + per * (end - start)


def build(nc, stream, ada0, ada, vectors, consts, positions, x, meta, out):
    with ExitStack() as ctx:
        def sb(name, cols, dt=F32):
            return ctx.enter_context(nc.sbuf_tensor(name, [P, cols], dt))

        def sem(name):
            return ctx.enter_context(nc.semaphore(name))

        raw = sb("raw", RAW * CH)
        w_hi = sb("w_hi", 2 * CH, F32R)
        w_lo = sb("w_lo", 2 * CH, F32R)
        area = sb("area", 3 * CH)
        X = sb("X", KT * T)
        a_hi = sb("a_hi", KT * TM, F32R)
        a_lo = sb("a_lo", KT * TM, F32R)
        y_hi = sb("y_hi", KT * T, F32R)
        y_lo = sb("y_lo", KT * T, F32R)
        lat_hi = sb("lat_hi", (QT + CT) * T, F32R)
        lat_lo = sb("lat_lo", (QT + CT) * T, F32R)
        st = sb("st", 14 * T, F32R)
        kr_hi = sb("kr_hi", T, F32R)
        kr_lo = sb("kr_lo", T, F32R)
        rope = sb("rope", T)
        sc = sb("sc", 4 * T)
        rs = sb("rs", 2 * T)
        mu = sb("mu", T)
        zs = sb("zs", T)
        th = sb("th", TM)
        vec = sb("vec", NV)
        con = sb("con", NC_)
        mod = sb("mod", ADA)
        ones = sb("ones", P)
        csil = sb("csil", 2 * KT)
        row = sb("row", 512)
        mt = sb("mt", KT * META)
        stat = sb("stat", 8)
        pos = th[:, 0:T].bitcast(I32)

        ps = ctx.enter_context(nc.psum_tensor("ps", [P, 8 * 512], F32))

        def bank(b, a=0, n=T):
            return ps[:, b * 512 + a:b * 512 + a + n]

        def two_tiles(t, i):
            return t[:, i * 2 * TM:(i + 1) * 2 * TM].rearrange("p (k t) -> p k t", k=2)[:, :, META:TM]

        def lat_ps(m):
            return bank(4 + m % 3, m // 3 * T)

        def grp_ps(m):
            return bank((0, 1, 5, 7)[m // 2], (m % 2) * T)

        def v(name, i, n=1):
            return vec[:, bass.ds(COL[name] + i, n)]

        ident, pairs = con[:, 0:P], con[:, P:2 * P]
        ada_ring = area[:, 0:2 * CH]
        ada_acc = area[:, 2 * CH:3 * CH]
        dft_hi, dft_lo = st[:, 0:4 * T], st[:, 4 * T:8 * T]
        u_hi, u_lo = st[:, 8 * T:9 * T], st[:, 9 * T:10 * T]
        t_hi, t_lo = st[:, 10 * T:12 * T], st[:, 12 * T:14 * T]
        qn_hi, qn_lo, qr_hi, qr_lo = (st[:, i * T:(i + 1) * T] for i in range(4))
        kn_hi, kn_lo, vv_hi, vv_lo = (st[:, i * T:(i + 1) * T] for i in range(4, 8))
        pt_hi, pt_lo = st[:, 8 * T:10 * T], st[:, 10 * T:12 * T]
        cw_hi, cw_lo = y_hi[:, 8 * T:16 * T], y_lo[:, 8 * T:16 * T]
        wide = area[:, 0:KT * T]
        conv_out = area[:, KT * T:(KT + CONV) * T]
        pad = rs[:, 0:TAPS - 1 - META + TM]
        pool_z, pool_a, pool_b = (sc[:, at:at + TM] for at in (0, TM, 2 * TM))

        def a_tile(t, k, lo=META, n=T):
            return t[:, bass.ds(k * TM + lo, n)]

        landed = [sem("landed0"), sem("landed1")]
        hi_ready, lo_ready = sem("hi_ready"), sem("lo_ready")
        weights_used = sem("weights_used")
        ada0_landed = [sem(f"ada0_landed{i}") for i in range(4)]
        ada0_used = sem("ada0_used")
        row_in = sem("row_in")
        col_ps, col_in = sem("col_ps"), sem("col_in")
        ada_landed = [sem("ada_landed0"), sem("ada_landed1")]
        ada_step = sem("ada_step")
        ada_clear = sem("ada_clear")
        ada_summed = sem("ada_summed")
        mod_ready = sem("mod_ready")
        vec_in = sem("vec_in")
        x_in = sem("x_in")
        small = sem("small")
        ones_set, c_tanh, c_ready = sem("ones_set"), sem("c_tanh"), sem("c_ready")
        rope_arg, rope_sin = sem("rope_arg"), sem("rope_sin")
        dve = sem("dve")
        ln_mean = sem("ln_mean")
        ln_cent, ln_sq, ln_acc = sem("ln_cent"), sem("ln_sq"), sem("ln_acc")
        ln_var, ln_std = sem("ln_var"), sem("ln_std")
        ln_y, ln_hi, ln_lo = sem("ln_y"), sem("ln_hi"), sem("ln_lo")
        x_sum, x_fold = sem("x_sum"), sem("x_fold")
        x_stat = sem("x_stat")
        x_norm = sem("x_norm")
        x_back = sem("x_back")
        lat_sq, lat_acc, lat_stat = sem("lat_sq"), sem("lat_acc"), sem("lat_stat")
        lat_y, lat_h, lat_l = sem("lat_y"), sem("lat_h"), sem("lat_l")
        cw_h, cw_l = sem("cw_h"), sem("cw_l")
        kr_rot, kr_sum, kr_h, kr_l = sem("kr_rot"), sem("kr_sum"), sem("kr_h"), sem("kr_l")
        u_h, u_l = sem("u_h"), sem("u_l")
        t_ps, t_h, t_l, yf_ps = sem("t_ps"), sem("t_h"), sem("t_l"), sem("yf_ps")
        z_tanh, z_ready = sem("z_tanh"), sem("z_ready")
        y_mul, y_h, y_l = sem("y_mul"), sem("y_h"), sem("y_l")
        q_h, q_l, qr_rot = sem("q_h"), sem("q_l"), sem("qr_rot")
        v_h, v_l = sem("v_h"), sem("v_l")
        s_ps, s_max, s_exp, p_ready = sem("s_ps"), sem("s_max"), sem("s_exp"), sem("p_ready")
        pt_ps, pt_h, pt_l, o_ps = sem("pt_ps"), sem("pt_h"), sem("pt_l"), sem("o_ps")
        g_tmp, g_mul = sem("g_tmp"), sem("g_mul")
        m_sq, m_acc = sem("m_sq"), sem("m_acc")
        am_y, am_h, am_l = sem("am_y"), sem("am_h"), sem("am_l")
        cv_tanh, cv_in, cv_done = sem("cv_tanh"), sem("cv_in"), sem("cv_done")
        pl_in, pl_sum, pl_h, pl_l = sem("pl_in"), sem("pl_sum"), sem("pl_h"), sem("pl_l")
        gp_h, gp_l = sem("gp_h"), sem("gp_l")
        cm_sum = sem("cm_sum")
        cm_fold = sem("cm_fold")
        cm_ps, cm_cent, cm_sq, cm_acc = sem("cm_ps"), sem("cm_cent"), sem("cm_sq"), sem("cm_acc")
        cn_y, cn_tanh, cn_mul, cn_h, cn_l = (sem(n) for n in ("cn_y", "cn_tanh", "cn_mul", "cn_h", "cn_l"))
        gt_tanh, gt_done = sem("gt_tanh"), sem("gt_done")
        mm_h, mm_l = sem("mm_h"), sem("mm_l")
        wo_out, wo_sq, wo_acc, wo_stat = sem("wo_out"), sem("wo_sq"), sem("wo_acc"), sem("wo_stat")
        h_new, h_hi, h_sq, h_lo, h_acc, h_stat = (sem(n) for n in ("h_new", "h_hi", "h_sq", "h_lo", "h_acc", "h_stat"))
        f_relu, f_sq, f_hi, f_lo, f_acc = (sem(n) for n in ("f_relu", "f_sq", "f_hi", "f_lo", "f_acc"))
        f_osq, f_osum = sem("f_osq"), sem("f_osum")
        y_out, stored = sem("y_out"), sem("stored")

        SMALL = 3 * 16
        NORM = {n: i for i, n in enumerate(("pre0", "meta", "lat0", "post0", "pre1", "lat1", "post1",
                                            "mix", "conv", "wo", "out"))}
        block = ctx.enter_context(nc.Block())

        @block.sync
        def _(sp):
            ada0_slot = [area[:, i * CH:(i + 1) * CH] for i in range(3)] + [raw[:, 2 * CH:3 * CH]]
            sp.dma_start(vec[:, :], vectors).then_inc(vec_in, 16)
            for s in range(4):
                sp.dma_start(ada0_slot[s], ada0[s]).then_inc(ada0_landed[s], 16)
            sp.dma_start(X[:, :], x).then_inc(x_in, 16)
            sp.dma_start(con[:, :], consts).then_inc(small, 16)
            sp.dma_start(pos, positions).then_inc(small, 16)
            sp.dma_start(mt[:, :], meta).then_inc(small, 16)

            def load(g, par, waits):
                if waits:
                    split_before = sp.snap(sp.to_reg(2 * g - 2 * RAW + 2))
                    landed_before = sp.snap(sp.to_reg(8 * (g - par)))
                    sp.wait_ge(lo_ready, split_before)
                    sp.wait_ge(landed[par], landed_before)
                sp.dma_start(raw[:, bass.ds((g % RAW) * CH, CH)],
                             stream[bass.ds(g, 1)].rearrange("a p n -> (a p) n")).then_inc(landed[par], 16)

            load(0, 0, False)
            load(1, 1, False)
            with sp.Fori(1, ADA0 // 4) as i:
                for s in range(4):
                    sp.wait_ge(ada0_used, 4 * i + s - 3)
                    sp.dma_start(ada0_slot[s], ada0[bass.ds(4 * i + s, 1)].rearrange("a p n -> (a p) n"))\
                        .then_inc(ada0_landed[s], 16)
            sp.wait_ge(landed[0], 16)
            sp.wait_ge(ada0_used, ADA0)
            load(2, 0, False)
            sp.wait_ge(landed[1], 16)
            sp.wait_ge(lo_ready, 2)
            load(3, 1, False)
            with sp.Fori(2, CHUNKS // 2) as i:
                for par in range(2):
                    load(2 * i + par, par, True)
            sp.wait_ge(lo_ready, 2 * (CHUNKS - RAW))
            sp.wait_ge(landed[0], 8 * (CHUNKS - 1))
            load(CHUNKS - 1, 0, False)
            for q in range(4):
                sp.wait_ge(y_out, 4 * q + 4)
                sp.dma_start(out[:, q * 4 * T:(q + 1) * 4 * T],
                             X[:, q * 4 * T:(q + 1) * 4 * T]).then_inc(stored, 16)
            sp.wait_ge(stored, 4 * 16)

        @block.gpsimd
        def _(pool):
            pool.wait_ge(ada0_used, ADA0)
            for a in range(2):
                pool.dma_start(ada_ring[:, a * CH:(a + 1) * CH], ada[a]).then_inc(ada_landed[a], 16)
            with pool.Fori(1, (ADA - ADA0) // 2) as i:
                for par in range(2):
                    pool.wait_ge(ada_step, 2 * i + par - 1)
                    pool.dma_start(ada_ring[:, par * CH:(par + 1) * CH],
                                   ada[bass.ds(2 * i + par, 1)].rearrange("a p n -> (a p) n"))\
                        .then_inc(ada_landed[par], 16)

        @block.tensor
        def _(pe):
            def mm3(o, w, a, first, last):
                pe.matmul(o, w[1], a[0], start=first, stop=False)
                pe.matmul(o, w[0], a[1], start=False, stop=False)
                return pe.matmul(o, w[0], a[0], start=False, stop=last)

            def wb(par, k, n=P):
                at = par * CH + k * P
                return w_hi[:, at:at + n], w_lo[:, at:at + n]

            def a_ops(k):
                return a_tile(a_hi, k), a_tile(a_lo, k)

            def am_ops(k):
                return a_tile(a_hi, k, 0, TM), a_tile(a_lo, k, 0, TM)

            def y_ops(k):
                return y_hi[:, k * T:(k + 1) * T], y_lo[:, k * T:(k + 1) * T]

            def half(g, h):
                pe.wait_ge(lo_ready, 2 * g + h + 1)

            def blocks(par, o, ops, ks, first, last, w0=0):
                for k in ks:
                    r = mm3(o, wb(par, w0 + k), ops(k), first and k == ks[0], last and k == ks[-1])
                return r

            def chunk(g, par, o, ops):
                half(g, 0)
                blocks(par, o, ops, range(8), True, False)
                half(g, 1)
                blocks(par, o, ops, range(8, 16), False, True).then_inc(weights_used, 1)

            def first_chunk(g, o, ops, n):
                for k in range(KT):
                    if k % 8 == 0:
                        half(g, k // 8)
                    if k % 2 == 0:
                        pe.wait_ge(ln_lo, 8 * n + k // 2 + 1)
                    r = mm3(o, wb(g % 2, k), ops(k), k == 0, k == KT - 1)
                r.then_inc(weights_used, 1)

            def ada_sum(r):
                pe.wait_ge(ada_step, KT * (r - 1))
                if r > 2:
                    pe.wait_ge(mod_ready, r - 2)
                for m in range(KT):
                    o = pe.matmul(bank(7, m, 1), ada_acc[:, m * P:(m + 1) * P], ones[:, 0:1],
                                  start=True, stop=True)
                o.then_inc(ada_summed, 1)

            def mean():
                for k in range(KT):
                    o = pe.matmul(bank(6), ones[:, :], X[:, k * T:(k + 1) * T], start=k == 0, stop=k == KT - 1)
                o.then_inc(ln_mean, 1)

            def squares(n):
                for i in range(KT // 2):
                    pe.wait_ge(ln_sq, 8 * n + i + 1)
                    for j in range(2):
                        at = (i % 2) * 2 * T + j * T
                        o = pe.matmul(bank(6, T), ones[:, :], sc[:, at:at + T],
                                      start=i + j == 0, stop=i == KT // 2 - 1 and j == 1)
                    o.then_inc(ln_acc, 1)

            def ada_row(r):
                if r >= 2:
                    pe.wait_ge(row_in, r - 1)
                for s in range(4):
                    pe.wait_ge(ada0_landed[s], 16 * r + 16)
                    w = (ada_ring[:, s * CH:(s + 1) * CH] if s < 2 else ada_acc if s == 2
                         else raw[:, 2 * CH:3 * CH])
                    for k in range(4):
                        o = pe.matmul(ps[0:1, (1 + r % 2) * 512:(2 + r % 2) * 512],
                                      csil[:, KT + 4 * s + k:KT + 4 * s + k + 1], w[:, k * 512:(k + 1) * 512],
                                      start=s + k == 0, stop=s + k == 6)
                    o.then_inc(ada0_used, 1)

            def turn_row(r):
                pe.wait_ge(row_in, r + 1)
                if r >= 4:
                    pe.wait_ge(col_in, r // 2 - 1)
                for t in range(4):
                    o = pe.matmul(bank((3, 7)[r // 2 % 2], 4 * (r % 2) + t, 1), row[0:1, t * P:(t + 1) * P],
                                  ones[0:1, 0:1], start=True, stop=True)
                o.then_inc(col_ps, 1)

            pe.wait_ge(c_ready, 1)
            for r in range(ADA0 // 4):
                ada_row(r)
                if r:
                    turn_row(r - 1)
                if r == 0:
                    pe.wait_ge(x_sum, 1)
                    pe.matmul(bank(6), ones[:, :], mu[:, :], start=True, stop=True).then_inc(ln_mean, 1)
                if r == 1:
                    pe.wait_ge(x_fold, 1)
                    pe.matmul(bank(6, T), ones[:, :], sc[:, 0:T], start=True, stop=True).then_inc(x_stat, 1)
                    pe.wait_ge(m_sq, 1)
                    pe.matmul(bank(5, 0, META), ones[:, :], zs[:, 0:META], start=True, stop=True)\
                        .then_inc(m_acc, 1)
            turn_row(ADA0 // 4 - 1)

            for l in range(DEPTH):
                G = l * PER_LAYER
                pe.wait_ge(ln_var, NORM["meta"] + 1)
                for m in range(LAT - 1):
                    if m >= 3:
                        pe.wait_ge(lat_sq, 6 * l + m - 2)
                    if m:
                        chunk(G + m, (G + m) % 2, lat_ps(m), a_ops)
                    else:
                        first_chunk(G, lat_ps(0), a_ops, l)
                if l:
                    pe.wait_ge(mod_ready, 3)
                chunk(G + LAT - 1, (G + LAT - 1) % 2, bank(7), a_ops)
                pe.wait_ge(lat_acc, 6 * (l + 1))
                pe.matmul(bank(3, 0, 2 * T), ones[:, :], sc[:, 0:2 * T], start=True, stop=True)\
                    .then_inc(lat_stat, 1)
                pe.wait_ge(lo_ready, 2 * (G + L_DFT) + 2)
                pe.wait_ge(weights_used, G + L_DFT)
                pe.nop().then_inc(weights_used, 1)
                g = G + L_FMIX
                half(g, 0)
                half(g, 1)
                pe.wait_ge(kr_rot, l + 1)
                for j, b in enumerate((0, 1, 2, 7)):
                    o = mm3(bank(b, 0, 512), wb(g % 2, 8 + j // 2), wb(g % 2, 4 * (j % 2), 512), True, True)
                o.then_inc(weights_used, 1)
                pe.wait_ge(ln_var, NORM[f"lat{l}"] + 1)
                pe.matmul(bank(3), pairs, sc[:, 3 * T:4 * T], start=True, stop=True).then_inc(kr_sum, 1)

                def seq_dft(q, first):
                    pe.wait_ge(t_l, 8 * l + q + 1)
                    if first:
                        pe.wait_ge(cw_l, 4 * l + 3)
                    else:
                        pe.wait_ge(y_mul, 16 * l + q)
                    for j in range(4):
                        tile_, trig = j // 2, j % 2
                        at, rhs = tile_ * T + trig * P, (2 * trig + tile_) * T
                        o = mm3(bank(2), (t_hi[:, at:at + P], t_lo[:, at:at + P]),
                                (dft_hi[:, rhs:rhs + T], dft_lo[:, rhs:rhs + T]), j == 0, j == 3)
                    o.then_inc(yf_ps, 1)

                def group(q, first, second=False):
                    g = G + L_FOUR + 2 * q
                    g0 = G + L_FOUR
                    if first:
                        pe.wait_ge(cw_l, 4 * l + 1)
                    chunk(g, g0 % 2, bank(0), a_ops)
                    if first:
                        pe.wait_ge(cw_l, 4 * l + 2)
                    else:
                        seq_dft(q - 1, second)
                        pe.wait_ge(z_ready, 16 * l + q)
                    chunk(g + 1, (g0 + 1) % 2, bank(1), a_ops)
                    pe.wait_ge(u_l, 8 * l + q + 1)
                    if first:
                        pe.wait_ge(cw_l, 4 * (l + 1))
                        pe.wait_ge(kr_l, l + 1)
                    for j in range(2):
                        o = mm3(bank(3, j * T), (u_hi[:, j * P:(j + 1) * P], u_lo[:, j * P:(j + 1) * P]),
                                (cw_hi[:, bass.ds(q * T, T)], cw_lo[:, bass.ds(q * T, T)]), True, True)
                    o.then_inc(t_ps, 1)

                group(0, True)
                group(1, False, True)
                with pe.Fori(2, GROUPS // 2) as q:
                    group(q, False)
                ada_sum(2 if l == 0 else 5)
                with pe.Fori(GROUPS // 2, GROUPS) as q:
                    group(q, False)
                seq_dft(GROUPS - 1, False)

                def project(h, first):
                    g = G + L_HEAD + 2 * h
                    par = (G + L_HEAD) % 2
                    half(g, 0)
                    if first:
                        pe.wait_ge(lat_l, 6 * (l + 1))
                        pe.wait_ge(z_ready, 16 * l + GROUPS)

                    def lat(k):
                        return lat_hi[:, k * T:(k + 1) * T], lat_lo[:, k * T:(k + 1) * T]
                    blocks(par, bank(0), lat, range(QT), True, True)
                    blocks(par, bank(0, T), lat, range(QT), True, True, QT)
                    half(g, 1)
                    if not first:
                        pe.wait_ge(v_l, 8 * l + h)
                    for k in range(CT):
                        mm3(bank(1), wb(par, 8 + k), lat(QT + k), k == 0, k == CT - 1)
                    for tt in range(2):
                        for k in range(CT):
                            o = mm3(bank(1, T + tt * P, P),
                                    tuple(t[:, tt * P:(tt + 1) * P] for t in lat(QT + k)),
                                    wb(par, 10 + k), k == 0, k == CT - 1)
                    o.then_inc(weights_used, 1)

                def turn(h):
                    pe.wait_ge(p_ready, 8 * l + h + 1)
                    for qt in range(2):
                        for kt in range(2):
                            o = pe.transpose(bank(3, kt * T + qt * P, P),
                                             sc[:, qt * T + kt * P:qt * T + kt * P + P], ident)
                    o.then_inc(pt_ps, 1)

                def attend(h, first=False):
                    pe.wait_ge(pt_l, 8 * l + h + 1)
                    pe.wait_ge(v_l, 8 * l + h + 1)
                    if not first:
                        pe.wait_ge(y_mul, 16 * l + GROUPS + h)
                    for k in range(2):
                        o = mm3(bank(4), (vv_hi[:, k * P:(k + 1) * P], vv_lo[:, k * P:(k + 1) * P]),
                                (pt_hi[:, k * T:(k + 1) * T], pt_lo[:, k * T:(k + 1) * T]), k == 0, k == 1)
                    o.then_inc(o_ps, 1)

                def head(h, first, second=False):
                    g = G + L_HEAD + 2 * h
                    par = (G + L_HEAD + 1) % 2
                    project(h, first)
                    half(g + 1, 0)
                    if first:
                        pe.wait_ge(y_mul, 16 * l + GROUPS)
                    else:
                        pe.wait_ge(z_ready, 16 * l + GROUPS + h)
                    blocks(par, bank(2), a_ops, range(8), True, False)
                    if not first:
                        turn(h - 1)
                    half(g + 1, 1)
                    blocks(par, bank(2), a_ops, range(8, 16), False, True).then_inc(weights_used, 1)
                    if not first:
                        attend(h - 1, second)
                    pe.wait_ge(q_l, 3 * (8 * l + h) + 3)
                    for qt in range(2):
                        s = slice(qt * P, (qt + 1) * P)
                        mm3(bank(5, qt * T), (qn_hi[:, s], qn_lo[:, s]), (kn_hi, kn_lo), True, False)
                        o = mm3(bank(5, qt * T), (qr_hi[:, s], qr_lo[:, s]), (kr_hi[:, :], kr_lo[:, :]),
                                False, True)
                    o.then_inc(s_ps, 1)

                head(0, True)
                head(1, False, True)
                with pe.Fori(2, HEADS // 2) as h:
                    head(h, False)
                if l == 0:
                    ada_sum(3)
                with pe.Fori(HEADS // 2, HEADS) as h:
                    head(h, False)

                g = G + L_OUT
                half(g, 0)
                pe.wait_ge(y_l, 16 * l + 15)
                blocks(g % 2, bank(0), y_ops, range(8), True, False)
                turn(HEADS - 1)
                half(g, 1)
                blocks(g % 2, bank(0), y_ops, range(8, 12), False, False)
                attend(HEADS - 1)
                blocks(g % 2, bank(0), y_ops, range(12, 15), False, False)
                pe.wait_ge(y_l, 16 * (l + 1))
                blocks(g % 2, bank(0), y_ops, range(15, 16), False, True).then_inc(weights_used, 1)
                chunk(g + 1, (g + 1) % 2, bank(1), y_ops)
                with pe.Fori(1, KT // 2) as i:
                    for b in range(2):
                        pe.wait_ge(g_tmp, 16 * l + 2 * i + b - 1)
                        chunk(g + 2 * i + b, (g + b) % 2, bank(b), y_ops)
                if l == 0:
                    ada_sum(4)
                pe.wait_ge(g_mul, 16 * (l + 1))
                mean()
                squares(2 * l + 1)
                if l == 0:
                    pe.wait_ge(x_norm, 1)
                    mean()
                    squares(2)

            squares(4)
            pe.wait_ge(am_l, 1)

            def mix_tile(j, par, first):
                g = B2_MIX + MIX * j
                p0 = B2_MIX + par
                if first and par == 0:
                    first_chunk(g, bank(0, 0, TM), am_ops, 2)
                else:
                    pe.wait_ge(cv_in, j)
                    chunk(g, p0 % 2, bank(0, 0, TM), am_ops)
                chunk(g + 1, (p0 + 1) % 2, bank(1, 0, TM), am_ops)
                if not (first and par == 0):
                    pe.wait_ge(pl_in, j)
                chunk(g + 2, p0 % 2, bank(2, 0, TM), am_ops)
                for b in range(2):
                    if not (first and par == 0):
                        pe.wait_ge(gt_tanh, 2 * j + b - 1)
                    chunk(g + 3 + b, (p0 + 1 + b) % 2, bank(3 + b), a_ops)

            for par in range(2):
                mix_tile(par, par, True)
            with pe.Fori(1, CONV // 2) as i:
                for par in range(2):
                    mix_tile(2 * i + par, par, False)
            half(B2_GRP, 0)
            half(B2_GRP, 1)
            pe.wait_ge(cv_in, CONV)
            pe.wait_ge(pl_l, CONV)
            for m in range(CONV):
                for k in range(2):
                    o = mm3(grp_ps(m), wb(B2_GRP % 2, 2 * m + k), y_ops(2 * (m // 2) + k), k == 0, k == 1)
            o.then_inc(weights_used, 1)
            for k in range(CONV):
                pe.wait_ge(cv_done, k + 1)
                o = pe.matmul(bank(6), ones[:, :], conv_out[:, k * T:(k + 1) * T], start=k == 0, stop=k == CONV - 1)
            o.then_inc(cm_ps, 1)

            def gate_b(i, b):
                g, g0 = B2_GATE + 4 * i + b, B2_GATE + b
                pe.wait_ge(gt_tanh, KT + 2 * i + b - 1)
                chunk(g, g0 % 2, bank(3 + b), a_ops)

            def branches(i, b, first):
                g, g0 = B2_GATE + 4 * i + 2 + b, B2_GATE + b
                half(g, 0)
                if first:
                    pe.wait_ge(gp_l, CONV)
                else:
                    pe.wait_ge(gt_done, 2 * i + b - 1)
                for k in range(CONV):
                    mm3(bank((0, 2)[b]), wb(g0 % 2, k), y_ops(CONV + k), k == 0, k == CONV - 1)
                half(g, 1)
                if first:
                    pe.wait_ge(cn_l, CONV)
                for k in range(CONV):
                    o = mm3(bank((1, 5)[b]), wb(g0 % 2, CONV + k), y_ops(k), k == 0, k == CONV - 1)
                o.then_inc(weights_used, 1)

            gate_b(0, 0)
            pe.wait_ge(cm_fold, 1)
            pe.matmul(bank(6, T), ones[:, :], zs[:, :], start=True, stop=True).then_inc(cm_acc, 1)
            gate_b(0, 1)
            branches(0, 0, True)
            branches(0, 1, True)
            with pe.Fori(1, KT // 2) as i:
                for b in range(2):
                    gate_b(i, b)
                for b in range(2):
                    branches(i, b, False)
            pe.wait_ge(gt_done, KT)
            for k in range(KT):
                if k % 8 == 0:
                    half(B2_WO, k // 8)
                if k % 2 == 0:
                    pe.wait_ge(mm_l, k // 2 + 1)
                o = mm3(bank(0), wb(B2_WO % 2, k), a_ops(k), k == 0, k == KT - 1)
            o.then_inc(weights_used, 1)
            chunk(B2_WO + 1, (B2_WO + 1) % 2, bank(1), a_ops)
            with pe.Fori(1, KT // 2) as i:
                for b in range(2):
                    pe.wait_ge(wo_sq, 2 * i + b - 1)
                    chunk(B2_WO + 2 * i + b, (B2_WO + b) % 2, bank(b), a_ops)
            pe.wait_ge(wo_acc, KT)
            pe.matmul(bank(6), ones[:, :], mu[:, :], start=True, stop=True).then_inc(wo_stat, 1)

            def up(f, i, b, first):
                if not first:
                    pe.wait_ge(f_relu, 16 * f + 2 * i + b - 1)
                chunk(B2_FF + 32 * f + 2 * i + b, (B2_FF + b) % 2, bank(b), a_ops)

            def down(f, i, b, first):
                if not first:
                    pe.wait_ge(f_acc, 16 * f + 2 * i + b - 1)
                chunk(B2_FF + 32 * f + KT + 2 * i + b, (B2_FF + b) % 2, bank(2 + b), y_ops)

            pe.wait_ge(h_lo, KT)
            for b in range(2):
                up(0, 0, b, True)
            with pe.Fori(1, KT // 2) as i:
                for b in range(2):
                    up(0, i, b, False)
            pe.wait_ge(h_acc, KT)
            pe.matmul(bank(6, T), ones[:, :], mu[:, :], start=True, stop=True).then_inc(h_stat, 1)
            pe.wait_ge(f_lo, 16)
            for b in range(2):
                down(0, 0, b, True)
            with pe.Fori(1, KT // 2) as i:
                for b in range(2):
                    down(0, i, b, False)
            with pe.Fori(1, FF_BLOCKS) as f:
                with pe.Fori(0, KT // 2) as i:
                    for b in range(2):
                        up(f, i, b, False)
                with pe.Fori(0, KT // 2) as i:
                    pe.wait_ge(f_lo, 16 * f + 16)
                    for b in range(2):
                        down(f, i, b, False)
            for i in range(KT // 2):
                pe.wait_ge(f_osq, i + 1)
                for j in range(2):
                    at = (i % 2) * 2 * T + j * T
                    o = pe.matmul(bank(6), ones[:, :], sc[:, at:at + T],
                                  start=i + j == 0, stop=i == KT // 2 - 1 and j == 1)
                o.then_inc(f_osum, 1)

        @block.scalar
        def _(ac):
            def split(g, par, dft=False):
                ac.wait_ge(landed[par], 8 * (g - par) + 16)
                if not (isinstance(g, int) and g < 2):
                    ac.wait_ge(weights_used, g - 1)
                n = HALF // 2 if dft else HALF
                for h in range(2):
                    to = dft_hi[:, h * n:(h + 1) * n] if dft else w_hi[:, par * CH + h * n:par * CH + (h + 1) * n]
                    ac.copy(to, raw[:, bass.ds((g % RAW) * CH + h * n, n)]).then_inc(hi_ready, 1)

            def after(g, base):
                split(g + 2, base % 2)

            def rstd(name, n=T):
                ac.wait_ge(ln_var, NORM[name] + 1)
                ac.activation(rs[:, 0:n], rs[:, 0:n], ACT.Sqrt).then_inc(ln_std, 1)

            def square_x(n, waits):
                for i in range(KT // 2):
                    if waits:
                        ac.wait_ge(ln_cent, 8 * n + i + 1)
                    if i >= 2:
                        ac.wait_ge(ln_acc, 8 * n + i - 1)
                    ac.activation(sc[:, (i % 2) * 2 * T:(i % 2 + 1) * 2 * T], X[:, 2 * i * T:(2 * i + 2) * T],
                                  ACT.Square).then_inc(ln_sq, 1)

            def split_input(n):
                with ac.Fori(0, KT // 2) as i:
                    ac.wait_ge(ln_y, i + (8 * n + 1))
                    to = a_hi[:, bass.ds(i * 2 * TM, 2 * TM)].rearrange("p (k t) -> p k t", k=2)[:, :, META:TM]
                    frm = sc[:, bass.ds((i % 2) * 2 * T, 2 * T)].rearrange("p (k t) -> p k t", k=2)
                    ac.copy(to, frm).then_inc(ln_hi, 1)

            ac.wait_ge(vec_in, 16)
            ac.activation(csil[:, 0:KT], v("c", 0, KT), ACT.Tanh, scale=0.5).then_inc(c_tanh, 1)

            def take_row(r):
                ac.wait_ge(ada0_used, 4 * r + 4)
                if r:
                    ac.wait_ge(col_ps, r)
                ac.copy(row[0:1, :], ps[0:1, (1 + r % 2) * 512:(2 + r % 2) * 512]).then_inc(row_in, 1)

            take_row(0)
            square_x(0, True)
            take_row(1)
            rstd("pre0")
            rstd("meta", META)
            ac.wait_ge(rope_arg, 1)
            ac.activation(rope[:, :], zs[:, :], ACT.Sin).then_inc(rope_sin, 1)
            split(0, 0)
            split(1, 1)
            for r in range(2, ADA0 // 4 + 2, 2):
                for q in (r, r + 1):
                    if q == r + 1:
                        for i in (r - 2, r - 1):
                            ac.wait_ge(ln_y, i + 1)
                            ac.copy(two_tiles(a_hi, i), sc[:, (i % 2) * 2 * T:(i % 2 + 1) * 2 * T]
                                    .rearrange("p (k t) -> p k t", k=2)).then_inc(ln_hi, 1)
                    if q < ADA0 // 4:
                        take_row(q)

            for l in range(DEPTH):
                G = l * PER_LAYER
                if l == 0:
                    ac.wait_ge(ln_hi, 8)
                    ac.wait_ge(ln_lo, 8)
                    ac.dma_start(X[:, :], x).then_inc(x_back, 16)
                for m in range(LAT):
                    ac.wait_ge(weights_used, G + m + 1)
                    if m < QT + CT:
                        if m:
                            ac.wait_ge(lat_acc, 6 * l + m)
                        ac.activation(sc[:, 2 * T:3 * T], lat_ps(m),
                                      ACT.Square).then_inc(lat_sq, 1)
                    split(G + m + 2, (G + m) % 2, dft=m + 2 == L_DFT)
                ac.wait_ge(weights_used, G + L_DFT + 1)
                after(G + L_DFT, G + L_DFT)
                ac.wait_ge(weights_used, G + L_FMIX + 1)

                def cw(j):
                    b, trig, g4 = (0, 1, 2, 7)[j], j // 2, j % 2
                    to = cw_hi[:, g4 * 4 * T:(g4 + 1) * 4 * T].rearrange("p (g c) -> p g c", g=4)
                    ac.copy(to[:, :, trig * P:(trig + 1) * P],
                            bank(b, 0, 512).rearrange("p (g c) -> p g c", g=4)).then_inc(cw_h, 1)

                cw(0)
                cw(1)
                after(G + L_FMIX, G + L_FMIX)
                cw(2)
                cw(3)
                rstd(f"lat{l}", 2 * T)
                ac.wait_ge(kr_sum, l + 1)
                ac.copy(kr_hi[:, :], bank(3)).then_inc(kr_h, 1)
                for m in range(QT + CT):
                    ac.wait_ge(lat_y, 6 * l + m + 1)
                    ac.copy(lat_hi[:, m * T:(m + 1) * T], sc[:, (m % 2) * T:(m % 2 + 1) * T]).then_inc(lat_h, 1)

                def y_part(t):
                    ac.wait_ge(y_mul, 16 * l + t + 1)
                    ac.copy(y_hi[:, bass.ds(t * T, T)], sc[:, 2 * T:3 * T]).then_inc(y_h, 1)

                def group(q, first):
                    g, g0 = G + L_FOUR + 2 * q, G + L_FOUR
                    ac.wait_ge(weights_used, g + 1)
                    ac.copy(u_hi, bank(0)).then_inc(u_h, 1)
                    after(g, g0)
                    if not first:
                        y_part(q - 1)
                    ac.wait_ge(weights_used, g + 2)
                    ac.activation(th[:, 0:T], bank(1), ACT.Tanh, scale=0.5).then_inc(z_tanh, 1)
                    after(g + 1, g0 + 1)
                    ac.wait_ge(t_ps, 8 * l + q + 1)
                    ac.copy(t_hi, bank(3, 0, 2 * T)).then_inc(t_h, 1)

                group(0, True)
                with ac.Fori(1, GROUPS) as q:
                    group(q, False)
                y_part(GROUPS - 1)

                def turned(h):
                    ac.wait_ge(pt_ps, 8 * l + h + 1)
                    ac.copy(pt_hi, bank(3, 0, 2 * T)).then_inc(pt_h, 1)

                def head(h, first):
                    g, g0 = G + L_HEAD + 2 * h, G + L_HEAD
                    ac.wait_ge(weights_used, g + 1)
                    ac.copy(qn_hi, bank(0)).then_inc(q_h, 1)
                    ac.copy(kn_hi, bank(1)).then_inc(q_h, 1)
                    ac.wait_ge(qr_rot, 8 * l + h + 1)
                    ac.copy(qr_hi, sc[:, 3 * T:4 * T]).then_inc(q_h, 1)
                    after(g, g0)
                    if not first:
                        turned(h - 1)
                    ac.wait_ge(weights_used, g + 2)
                    if not first:
                        ac.wait_ge(z_ready, 16 * l + GROUPS + h)
                    ac.activation(th[:, 0:T], bank(2), ACT.Tanh, scale=0.5).then_inc(z_tanh, 1)
                    if not first:
                        ac.wait_ge(o_ps, 8 * l + h)
                    ac.wait_ge(q_l, 3 * (8 * l + h) + 2)
                    ac.copy(vv_hi, bank(1, T)).then_inc(v_h, 1)
                    if not first:
                        y_part(GROUPS + h - 1)
                    ac.wait_ge(s_max, 8 * l + h + 1)
                    for qt in range(2):
                        ac.activation(sc[:, qt * T:(qt + 1) * T], bank(5, qt * T), ACT.Exp,
                                      bias=stat[:, 2 + qt:3 + qt], scale=SM_SCALE,
                                      accum_out=stat[:, 4 + qt:5 + qt]).then_inc(s_exp, 1)
                    after(g + 1, g0 + 1)

                head(0, True)
                with ac.Fori(1, HEADS) as h:
                    head(h, False)

                def out_tile(i, b, first):
                    g = G + L_OUT
                    m = 2 * i + b
                    ac.wait_ge(weights_used, m + (g + 1))
                    if not first:
                        ac.wait_ge(g_mul, m + (16 * l - 1))
                    ac.activation(sc[:, b * T:(b + 1) * T], bank(b), ACT.Copy,
                                  scale=mod[:, bass.ds(m + (3 * l + 2) * KT, 1)]).then_inc(g_tmp, 1)
                    after(m + g, g + b)

                turned(HEADS - 1)
                y_part(2 * HEADS - 1)
                ac.wait_ge(mod_ready, 3 * l + 1)
                for b in range(2):
                    out_tile(0, b, True)
                with ac.Fori(1, KT // 2) as i:
                    for b in range(2):
                        out_tile(i, b, False)
                square_x(2 * l + 1, True)
                rstd(f"post{l}")
                if l == 0:
                    for i in range(KT // 2):
                        ac.wait_ge(ln_cent, 8 * 2 + i + 1)
                        s = slice((i % 2) * 2 * T, (i % 2 + 1) * 2 * T)
                        ac.activation(sc[:, s], sc[:, s], ACT.Square).then_inc(ln_sq, 1)
                    rstd("pre1")
                    split_input(1)

            ac.wait_ge(x_norm, 2)
            square_x(4, False)
            rstd("mix")
            split_input(2)
            ac.wait_ge(am_y, 1)
            ac.copy(a_hi[:, :].rearrange("p (k t) -> p k t", k=KT)[:, :, 0:META],
                    mt[:, :].rearrange("p (k t) -> p k t", k=KT)).then_inc(am_h, 1)

            def mix_tile(j, par, first):
                g, p0 = B2_MIX + MIX * j, B2_MIX + par
                ac.wait_ge(weights_used, g + 1)
                after(g, p0)
                ac.wait_ge(weights_used, g + 2)
                ac.activation(th[:, :], bank(1, 0, TM), ACT.Tanh, scale=0.5).then_inc(cv_tanh, 1)
                after(g + 1, p0 + 1)
                ac.wait_ge(weights_used, g + 3)
                if not first:
                    ac.wait_ge(pl_sum, j)
                ac.copy(pool_z, bank(2, 0, TM)).then_inc(pl_in, 1)
                after(g + 2, p0)
                for b in range(2):
                    ac.wait_ge(weights_used, g + 4 + b)
                    ac.activation(wide[:, bass.ds((2 * j + b) * T, T)], bank(3 + b), ACT.Tanh, scale=0.5)\
                        .then_inc(gt_tanh, 1)
                    if b == 0:
                        after(g + 3, p0 + 1)
                        ac.wait_ge(pl_sum, j + 1)
                        ac.copy(y_hi[:, bass.ds(j * T, T)], zs[:, :]).then_inc(pl_h, 1)
                    else:
                        after(g + 4, p0)

            mix_tile(0, 0, True)
            mix_tile(1, 1, False)
            with ac.Fori(1, CONV // 2) as i:
                for par in range(2):
                    mix_tile(2 * i + par, par, False)
            ac.wait_ge(weights_used, B2_GRP + 1)
            for i, m in enumerate((0, 2, 4, 6, 1, 3, 5, 7)):
                if m % 2:
                    ac.wait_ge(gp_l, i - 3)
                ac.activation(y_hi[:, (CONV + m) * T:(CONV + m + 1) * T], grp_ps(m), ACT.Copy,
                              scale=v("pool_scale", m)).then_inc(gp_h, 1)
            after(B2_GRP, B2_GRP)
            for i in range(CONV // 2):
                ac.wait_ge(cm_cent, i + 1)
                if i >= 2:
                    ac.wait_ge(cm_sum, i - 1)
                ac.activation(sc[:, (i % 2) * 2 * T:(i % 2 + 1) * 2 * T], conv_out[:, 2 * i * T:(2 * i + 2) * T],
                              ACT.Square).then_inc(cm_sq, 1)

            def gate_b(i, b, first=False):
                g, g0 = B2_GATE + 4 * i + b, B2_GATE + b
                ac.wait_ge(weights_used, g + 1)
                if not first:
                    ac.wait_ge(gt_done, 2 * i)
                ac.activation(sc[:, b * T:(b + 1) * T], bank(3 + b), ACT.Tanh, scale=0.5).then_inc(gt_tanh, 1)
                after(g, g0)

            def branches(i, b):
                g, g0 = B2_GATE + 4 * i + 2 + b, B2_GATE + b
                ac.wait_ge(weights_used, g + 1)
                after(g, g0)

            ac.wait_ge(cm_fold, 1)
            gate_b(0, 0, True)
            rstd("conv")
            for k in range(CONV):
                ac.wait_ge(cn_y, k + 1)
                ac.activation(th[:, 0:T], conv_out[:, k * T:(k + 1) * T], ACT.Tanh, scale=0.5).then_inc(cn_tanh, 1)
                ac.wait_ge(cn_mul, k + 1)
                ac.activation(y_hi[:, k * T:(k + 1) * T], zs[:, :], ACT.Copy, scale=0.5).then_inc(cn_h, 1)
                if k == 0:
                    gate_b(0, 1, True)
            branches(0, 0)
            branches(0, 1)
            with ac.Fori(1, KT // 2 - 1) as i:
                for b in range(2):
                    gate_b(i, b)
                for b in range(2):
                    branches(i, b)
            last = KT // 2 - 1
            for b in range(2):
                gate_b(last, b)
            for i in range(KT // 2):
                if i == 3:
                    branches(last, 0)
                if i == last:
                    branches(last, 1)
                ac.wait_ge(gt_done, 2 * i + 2)
                to = a_hi[:, i * 2 * TM:(i + 1) * 2 * TM].rearrange("p (k t) -> p k t", k=2)[:, :, META:TM]
                ac.activation(to, wide[:, i * 2 * T:(i + 1) * 2 * T].rearrange("p (k t) -> p k t", k=2),
                              ACT.Copy, scale=0.5).then_inc(mm_h, 1)

            def wo_tile(i, b, first):
                m = 2 * i + b
                ac.wait_ge(weights_used, m + (B2_WO + 1))
                ac.copy(wide[:, bass.ds(m * T, T)], bank(b)).then_inc(wo_out, 1)
                if not first:
                    ac.wait_ge(wo_acc, m - 1)
                ac.activation(sc[:, b * T:(b + 1) * T], bank(b), ACT.Square).then_inc(wo_sq, 1)
                after(m + B2_WO, B2_WO + b)

            for b in range(2):
                wo_tile(0, b, True)
            with ac.Fori(1, KT // 2) as i:
                for b in range(2):
                    wo_tile(i, b, False)
            rstd("wo")
            def new_h(m, b, first):
                if not first:
                    ac.wait_ge(h_acc, m - 1)
                ac.wait_ge(h_new, m + 1)
                ac.activation(a_tile(a_hi, m), X[:, bass.ds(m * T, T)], ACT.Copy,
                              scale=v("g_pre_mlp", m)).then_inc(h_hi, 1)
                ac.activation(sc[:, (2 + b) * T:(3 + b) * T], X[:, bass.ds(m * T, T)], ACT.Square).then_inc(h_sq, 1)

            for b in range(2):
                new_h(b, b, True)
            with ac.Fori(1, KT // 2) as i:
                for b in range(2):
                    new_h(2 * i + b, b, False)

            def up(f, i, b, first):
                m = 16 * f + 2 * i + b
                g = B2_FF + 32 * f + 2 * i + b
                ac.wait_ge(weights_used, g + 1)
                if not first:
                    ac.wait_ge(f_lo, m - 1)
                ac.activation(sc[:, b * T:(b + 1) * T], bank(b), ACT.Relu).then_inc(f_relu, 1)
                ac.wait_ge(f_relu, m + 1)
                ac.activation(y_hi[:, bass.ds((2 * i + b) * T, T)], sc[:, b * T:(b + 1) * T], ACT.Square)\
                    .then_inc(f_hi, 1)
                after(g, B2_FF + b)

            for b in range(2):
                up(0, 0, b, True)
            with ac.Fori(1, KT // 2) as i:
                for b in range(2):
                    up(0, i, b, False)
            with ac.Fori(0, KT // 2) as i:
                for b in range(2):
                    g = B2_FF + KT + 2 * i + b
                    ac.wait_ge(weights_used, g + 1)
                    after(g, B2_FF + b)
            with ac.Fori(1, FF_BLOCKS - 1) as f:
                with ac.Fori(0, KT // 2) as i:
                    for b in range(2):
                        up(f, i, b, False)
                with ac.Fori(0, KT // 2) as i:
                    for b in range(2):
                        g = B2_FF + KT + 32 * f + 2 * i + b
                        ac.wait_ge(weights_used, g + 1)
                        after(g, B2_FF + b)
            f = FF_BLOCKS - 1
            with ac.Fori(0, KT // 2) as i:
                for b in range(2):
                    up(f, i, b, False)
            with ac.Fori(0, KT // 2 - 1) as i:
                for b in range(2):
                    g = B2_FF + KT + 32 * f + 2 * i + b
                    ac.wait_ge(weights_used, g + 1)
                    after(g, B2_FF + b)
            for i in range(KT // 2):
                ac.wait_ge(f_acc, 16 * (FF_BLOCKS - 1) + 2 * i + 2)
                if i >= 2:
                    ac.wait_ge(f_osum, i - 1)
                ac.activation(sc[:, (i % 2) * 2 * T:(i % 2 + 1) * 2 * T], wide[:, 2 * i * T:(2 * i + 2) * T],
                              ACT.Square).then_inc(f_osq, 1)
            ac.wait_ge(ln_var, NORM["out"] + 1)
            ac.activation(rs[:, T:2 * T], rs[:, T:2 * T], ACT.Sqrt).then_inc(ln_std, 1)

        @block.vector
        def _(ve):
            own = Chain(ve, dve)

            def split(g, par, dft=False):
                n = HALF // 2 if dft else HALF
                for h in range(2):
                    ve.wait_ge(hi_ready, 2 * g + h + 1)
                    if dft:
                        to, hi = dft_lo[:, h * n:(h + 1) * n], dft_hi[:, h * n:(h + 1) * n]
                    else:
                        s = slice(par * CH + h * n, par * CH + (h + 1) * n)
                        to, hi = w_lo[:, s], w_hi[:, s]
                    ve.tensor_tensor(to, raw[:, bass.ds((g % RAW) * CH + h * n, n)], hi.bitcast(F32),
                                     ALU.subtract).then_inc(lo_ready, 1)

            def after(g, base):
                split(g + 2, base % 2)

            def sub_hi(out_, exact, hi):
                return ve.tensor_tensor(out_, exact, hi.bitcast(F32), ALU.subtract)

            def over_tokens(t, k):
                return t.unsqueeze(1).to_broadcast([P, k, T])

            def tiles(t, k):
                return t.rearrange("p (k t) -> p k t", k=k)

            def add_ada(a, par):
                ve.wait_ge(ada_landed[par], 8 * (a - par) + (16 - 8 * ADA0))
                if not (isinstance(a, int) and a == ADA0):
                    ve.wait_ge(ada_step, a - ADA0)
                ve.scalar_tensor_tensor(out=ada_acc, in0=ada_ring[:, par * CH:(par + 1) * CH],
                                        scalar=csil[:, bass.ds(KT + a % KT, 1)], in1=ada_acc,
                                        op0=ALU.mult, op1=ALU.add).then_inc(ada_step, 1)

            def clear_ada(r):
                if r > 2:
                    ve.wait_ge(ada_summed, r - 2)
                ve.memset(ada_acc, 0.0).then_inc(ada_clear, 1)
                ve.wait_ge(ada_clear, r - 1)

            def read_mod(r):
                ve.wait_ge(ada_summed, r - 1)
                ve.scalar_tensor_tensor(out=mod[:, r * KT:(r + 1) * KT], in0=bank(7, 0, KT),
                                        scalar=1.0 if r % 3 == 1 else 0.0, in1=v("b_ada", r * KT, KT),
                                        op0=ALU.add, op1=ALU.add).then_inc(mod_ready, 1)
                if r + 1 < 3 * DEPTH:
                    clear_ada(r + 1)

            def rstd(name, parts, eps):
                for part, total, count in parts:
                    o = ve.tensor_scalar(part, total, 1.0 / count, eps, ALU.mult, ALU.add)
                    if part is not parts[-1][0]:
                        own.link(o)
                o.then_inc(ln_var, 1)
                ve.wait_ge(ln_std, NORM[name] + 1)
                whole = rs[:, 0:T * len(parts)] if name != "meta" else parts[0][0]
                own.link(ve.reciprocal(whole, whole))

            def centre(n, in_place):
                ve.wait_ge(ln_mean, n + 1)
                own.link(ve.tensor_scalar(mu[:, :], bank(6), 1.0 / D, None, ALU.mult))
                for i in range(KT // 2):
                    frm = X[:, 2 * i * T:(2 * i + 2) * T]
                    if not in_place and i >= 2:
                        ve.wait_ge(ln_acc, 8 * n + i - 1)
                    to = frm if in_place else sc[:, (i % 2) * 2 * T:(i % 2 + 1) * 2 * T]
                    ve.tensor_tensor(tiles(to, 2), tiles(frm, 2), over_tokens(mu[:, :], 2), ALU.subtract)\
                        .then_inc(ln_cent, 1)
                ve.wait_ge(ln_acc, 8 * (n + 1))

            def split_input(n, terms, affine, links, before=None):
                def make(i):
                    if before:
                        before(i)
                    buf = sc[:, bass.ds((i % 2) * 2 * T, 2 * T)]
                    frm = X[:, bass.ds(i * 2 * T, 2 * T)]
                    for row, op in terms:
                        own.link(ve.tensor_tensor(tiles(buf, 2), tiles(frm, 2), over_tokens(row, 2), op))
                        frm = buf
                    for j in range(2):
                        src = buf if terms else frm
                        ins = affine(sc[:, bass.ds((i % 2) * 2 * T + j * T, T)],
                                     sc[:, bass.ds((i % 2) * 2 * T + j * T, T)] if terms
                                     else X[:, bass.ds(i * 2 * T + j * T, T)], 2 * i + j)
                        own.link(ins)
                    ve.sem_inc(ln_y, 1)

                def finish(i):
                    ve.wait_ge(ln_hi, i + (8 * n + 1))
                    to, hi = (tiles(t[:, bass.ds(i * 2 * TM, 2 * TM)], 2)[:, :, META:TM] for t in (a_lo, a_hi))
                    sub_hi(to, tiles(sc[:, bass.ds((i % 2) * 2 * T, 2 * T)], 2), hi).then_inc(ln_lo, 1)

                make(0)
                if before:
                    for i in range(1, KT // 2):
                        if i >= 2:
                            ve.wait_ge(ln_lo, i - 1)
                        make(i)
                        finish(i - 1)
                    finish(KT // 2 - 1)
                    return
                with own.loop(1, KT // 2, links) as i:
                    make(i)
                    finish(i - 1)
                    ve.wait_ge(ln_lo, i + 8 * n)
                finish(KT // 2 - 1)

            ve.memset(ones[:, :], 1.0).then_inc(ones_set, 1)
            ve.wait_ge(c_tanh, 1)
            own.link(ve.scalar_tensor_tensor(out=csil[:, KT:2 * KT], in0=csil[:, 0:KT], scalar=1.0,
                                             in1=v("c", 0, KT), op0=ALU.add, op1=ALU.mult))
            ve.tensor_scalar(csil[:, KT:2 * KT], csil[:, KT:2 * KT], 0.5, None, ALU.mult).then_inc(c_ready, 1)
            ve.wait_ge(c_ready, 1)
            ve.wait_ge(x_in, 16)
            for i in range(1, KT // 2):
                own.link(ve.tensor_tensor(sc[:, 0:2 * T], X[:, 0:2 * T] if i == 1 else sc[:, 0:2 * T],
                                          X[:, 2 * i * T:(2 * i + 2) * T], ALU.add))
            ve.tensor_tensor(mu[:, :], sc[:, 0:T], sc[:, T:2 * T], ALU.add).then_inc(x_sum, 1)
            ve.wait_ge(ln_mean, 1)
            own.link(ve.tensor_scalar(mu[:, :], bank(6), 1.0 / D, None, ALU.mult))

            def add_square(i, acc, squares_sem, acc_sem):
                ve.wait_ge(squares_sem, i + 1)
                sq = sc[:, (i % 2) * 2 * T:(i % 2 + 1) * 2 * T]
                if i:
                    ve.wait_ge(acc_sem, i)
                    ve.tensor_tensor(acc, acc, sq, ALU.add).then_inc(acc_sem, 1)
                else:
                    ve.tensor_copy(acc, sq).then_inc(acc_sem, 1)

            for i in range(KT // 2):
                s = X[:, 2 * i * T:(2 * i + 2) * T]
                ve.tensor_tensor(tiles(s, 2), tiles(s, 2), over_tokens(mu[:, :], 2), ALU.subtract)\
                    .then_inc(ln_cent, 1)
                if i:
                    add_square(i - 1, rs[:, :], ln_sq, ln_acc)
            add_square(KT // 2 - 1, rs[:, :], ln_sq, ln_acc)
            ve.wait_ge(ln_acc, 8)
            ve.tensor_tensor(sc[:, 0:T], rs[:, 0:T], rs[:, T:2 * T], ALU.add).then_inc(x_fold, 1)
            ve.wait_ge(small, SMALL)
            ve.wait_ge(x_fold, 1)
            own.link(ve.tensor_tensor(sc[:, 2 * T:2 * T + KT * META], mt[:, :], mt[:, :], ALU.mult))
            ve.tensor_reduce(zs[:, 0:META], sc[:, 2 * T:2 * T + KT * META].rearrange("p (k t) -> p t k", k=KT),
                             AX.X, ALU.add).then_inc(m_sq, 1)
            ve.wait_ge(x_stat, 1)
            rstd("pre0", [(rs[:, 0:T], bank(6, T), D)], 1e-6)
            for i in range(4):
                s = X[:, i * 4 * T:(i + 1) * 4 * T]
                own.link(ve.tensor_tensor(tiles(s, 4), tiles(s, 4), over_tokens(rs[:, 0:T], 4), ALU.mult))
            ve.wait_ge(m_acc, 1)
            rstd("meta", [(rs[:, 0:META], bank(5, 0, META), D)], 1e-6)
            own.link(ve.tensor_tensor(mt[:, :].rearrange("p (k t) -> p k t", k=KT),
                                      mt[:, :].rearrange("p (k t) -> p k t", k=KT),
                                      rs[:, 0:META].unsqueeze(1).to_broadcast([P, KT, META]), ALU.mult))
            ve.tensor_tensor(mt[:, :].rearrange("p (k t) -> p k t", k=KT),
                             mt[:, :].rearrange("p (k t) -> p k t", k=KT),
                             v("g_pre_mix", 0, KT).unsqueeze(2).to_broadcast([P, KT, META]), ALU.mult)\
                .then_inc(am_y, 1)
            two_pi = 2.0 * np.pi
            c1 = float(np.float32(6.28125))
            c2 = float(np.round((two_pi - c1) * 2.0 ** 17) / 2.0 ** 17)
            c3 = float(np.float32(two_pi - c1 - c2))
            freq, phase, sign = (con[:, 2 * P + i:2 * P + i + 1] for i in range(3))
            magic = 1.5 * 2.0 ** 23
            ang, turns_ = zs, mu
            own.link(ve.tensor_copy(ang[:, :], pos))
            own.link(ve.tensor_scalar(ang[:, :], ang[:, :], freq, None, ALU.mult))
            own.link(ve.tensor_scalar(sc[:, T:2 * T], ang[:, :], phase, 1.0 / two_pi, ALU.add, ALU.mult))
            own.link(ve.tensor_scalar(turns_[:, :], sc[:, T:2 * T], magic, None, ALU.add))
            own.link(ve.tensor_scalar(turns_[:, :], turns_[:, :], magic, None, ALU.subtract))
            for c in (c1, c2, c3):
                own.link(ve.scalar_tensor_tensor(out=ang[:, :], in0=turns_[:, :], scalar=-c, in1=ang[:, :],
                                                 op0=ALU.mult, op1=ALU.add))
            own.link(ve.tensor_scalar(ang[:, :], ang[:, :], phase, None, ALU.add))
            ve.tensor_scalar(ang[:, :], ang[:, :], float(np.float32(3.1415925)), float(np.float32(-3.1415925)),
                             ALU.min, ALU.max).then_inc(rope_arg, 1)
            ve.wait_ge(rope_sin, 1)
            own.link(ve.tensor_scalar(rope[:, :], rope[:, :], sign, None, ALU.mult))
            split(0, 0)
            split(1, 1)

            def read_mod0(i):
                if i % 2:
                    return
                ve.wait_ge(col_ps, i + 2)
                for third in range(2):
                    ve_mod = mod[:, KT * third + 2 * i:KT * third + 2 * i + 4]
                    o = ve.scalar_tensor_tensor(out=ve_mod, in0=bank((3, 7)[i // 2 % 2], 4 * third, 4),
                                                scalar=float(third), in1=v("b_ada", KT * third + 2 * i, 4),
                                                op0=ALU.add, op1=ALU.add)
                o.then_inc(col_in, 1)
                ve.wait_ge(col_in, i // 2 + 1)

            def modulate(l):
                def affine(o, frm, m):
                    return ve.tensor_scalar(o, frm, mod[:, bass.ds(m + (3 * l + 1) * KT, 1)],
                                            mod[:, bass.ds(m + 3 * l * KT, 1)], ALU.mult, ALU.add)
                return affine

            split_input(0, (), modulate(0), 2, read_mod0)
            ve.wait_ge(ada0_used, ADA0)
            clear_ada(2)

            for l in range(DEPTH):
                G = l * PER_LAYER
                A = (2 + 3 * l) * KT
                for m in range(LAT):
                    if m < QT + CT:
                        ve.wait_ge(lat_sq, 6 * l + m + 1)
                        acc = sc[:, 0:T] if m < QT else sc[:, T:2 * T]
                        if m:
                            ve.wait_ge(lat_acc, 6 * l + m)
                        if m in (0, QT):
                            ve.tensor_copy(acc, sc[:, 2 * T:3 * T]).then_inc(lat_acc, 1)
                        else:
                            ve.tensor_tensor(acc, acc, sc[:, 2 * T:3 * T], ALU.add).then_inc(lat_acc, 1)
                    else:
                        ve.wait_ge(weights_used, G + m + 1)
                        ve.tensor_tensor(sc[:, 3 * T:4 * T], bank(7), rope[:, :], ALU.mult).then_inc(kr_rot, 1)
                    split(G + m + 2, (G + m) % 2, dft=m + 2 == L_DFT)
                    add_ada(A + m, (A + m) % 2)
                after(G + L_DFT, G + L_DFT)
                add_ada(A + LAT, (A + LAT) % 2)
                ve.wait_ge(lat_stat, l + 1)
                rs_parts = [(rs[:, 0:T], bank(3), QT * P), (rs[:, T:2 * T], bank(3, T), CT * P)]

                def cw(j):
                    b, trig, g4 = (0, 1, 2, 7)[j], j // 2, j % 2
                    to, hi = (t[:, g4 * 4 * T:(g4 + 1) * 4 * T].rearrange("p (g c) -> p g c", g=4)
                              [:, :, trig * P:(trig + 1) * P] for t in (cw_lo, cw_hi))
                    ve.wait_ge(cw_h, 4 * l + j + 1)
                    sub_hi(to, bank(b, 0, 512).rearrange("p (g c) -> p g c", g=4), hi).then_inc(cw_l, 1)

                cw(0)
                cw(1)
                after(G + L_FMIX, G + L_FMIX)
                cw(2)
                cw(3)
                rstd(f"lat{l}", rs_parts, 1e-6)
                ve.wait_ge(kr_h, l + 1)
                sub_hi(kr_lo[:, :], bank(3), kr_hi[:, :]).then_inc(kr_l, 1)
                for m in range(QT + CT):
                    gain = v("q_norm", l * QT + m) if m < QT else v("kv_norm", l * CT + m - QT)
                    row = rs[:, 0:T] if m < QT else rs[:, T:2 * T]
                    ve.scalar_tensor_tensor(out=sc[:, (m % 2) * T:(m % 2 + 1) * T],
                                            in0=lat_ps(m), scalar=gain,
                                            in1=row, op0=ALU.mult, op1=ALU.mult).then_inc(lat_y, 1)
                    ve.wait_ge(lat_h, 6 * l + m + 1)
                    s = slice(m * T, (m + 1) * T)
                    sub_hi(lat_lo[:, s], sc[:, (m % 2) * T:(m % 2 + 1) * T], lat_hi[:, s]).then_inc(lat_l, 1)

                def y_tile(t, o):
                    ve.scalar_tensor_tensor(out=sc[:, 2 * T:3 * T], in0=o, scalar=0.5, in1=zs[:, :],
                                            op0=ALU.mult, op1=ALU.mult).then_inc(y_mul, 1)

                def y_rest(t):
                    ve.wait_ge(y_h, 16 * l + t + 1)
                    sub_hi(y_lo[:, bass.ds(t * T, T)], sc[:, 2 * T:3 * T], y_hi[:, bass.ds(t * T, T)])\
                        .then_inc(y_l, 1)

                def gate(t, b):
                    ve.wait_ge(z_tanh, 16 * l + t + 1)
                    ve.scalar_tensor_tensor(out=zs[:, :], in0=th[:, 0:T], scalar=1.0, in1=bank(b),
                                            op0=ALU.add, op1=ALU.mult).then_inc(z_ready, 1)

                def group(q, first, with_ada):
                    g, g0 = G + L_FOUR + 2 * q, G + L_FOUR
                    ve.wait_ge(u_h, 8 * l + q + 1)
                    sub_hi(u_lo, bank(0), u_hi).then_inc(u_l, 1)
                    after(g, g0)
                    if not first:
                        ve.wait_ge(yf_ps, 8 * l + q)
                        ve.wait_ge(z_ready, 16 * l + q)
                        y_tile(q - 1, bank(2))
                        y_rest(q - 1)
                    if with_ada:
                        add_ada(2 * q + (A + GROUPS), 0)
                    gate(q, 1)
                    after(g + 1, g0 + 1)
                    if with_ada:
                        add_ada(2 * q + (A + GROUPS + 1), 1)
                    ve.wait_ge(t_h, 8 * l + q + 1)
                    sub_hi(t_lo, bank(3, 0, 2 * T), t_hi).then_inc(t_l, 1)

                group(0, True, True)
                with ve.Fori(1, GROUPS // 2) as q:
                    group(q, False, True)
                read_mod(3 * l + 2)
                with ve.Fori(GROUPS // 2, GROUPS) as q:
                    group(q, False, l == 0)
                ve.wait_ge(yf_ps, 8 * (l + 1))
                ve.wait_ge(z_ready, 16 * l + GROUPS)
                y_tile(GROUPS - 1, bank(2))
                y_rest(GROUPS - 1)

                def turned(h):
                    ve.wait_ge(pt_h, 8 * l + h + 1)
                    sub_hi(pt_lo, bank(3, 0, 2 * T), pt_hi).then_inc(pt_l, 1)

                def head(h, first, with_ada):
                    g, g0 = G + L_HEAD + 2 * h, G + L_HEAD
                    ve.wait_ge(q_h, 3 * (8 * l + h) + 1)
                    ve.tensor_tensor(sc[:, 3 * T:4 * T], bank(0, T), rope[:, :], ALU.mult).then_inc(qr_rot, 1)
                    sub_hi(qn_lo, bank(0), qn_hi).then_inc(q_l, 1)
                    ve.wait_ge(q_h, 3 * (8 * l + h) + 2)
                    sub_hi(kn_lo, bank(1), kn_hi).then_inc(q_l, 1)
                    ve.wait_ge(q_h, 3 * (8 * l + h) + 3)
                    sub_hi(qr_lo, sc[:, 3 * T:4 * T], qr_hi).then_inc(q_l, 1)
                    after(g, g0)
                    if with_ada:
                        add_ada(2 * h + (A + 3 * GROUPS), 0)
                    if not first:
                        turned(h - 1)
                        ve.wait_ge(o_ps, 8 * l + h)
                        ve.wait_ge(z_ready, 16 * l + GROUPS + h)
                        y_tile(GROUPS + h - 1, bank(4))
                        ve.wait_ge(y_mul, 16 * l + GROUPS + h)
                    gate(GROUPS + h, 2)
                    ve.wait_ge(v_h, 8 * l + h + 1)
                    sub_hi(vv_lo, bank(1, T), vv_hi).then_inc(v_l, 1)
                    if not first:
                        y_rest(GROUPS + h - 1)
                    ve.wait_ge(s_ps, 8 * l + h + 1)
                    own.link(ve.tensor_reduce(stat[:, 0:2], bank(5, 0, 2 * T).rearrange("p (q k) -> p q k", q=2),
                                              AX.X, ALU.max))
                    ve.tensor_scalar(stat[:, 2:4], stat[:, 0:2], -SM_SCALE, None, ALU.mult).then_inc(s_max, 1)
                    ve.wait_ge(s_exp, 2 * (8 * l + h) + 2)
                    own.link(ve.reciprocal(stat[:, 6:8], stat[:, 4:6]))
                    for qt in range(2):
                        s = sc[:, qt * T:(qt + 1) * T]
                        o = ve.tensor_scalar(s, s, stat[:, 6 + qt:7 + qt], None, ALU.mult)
                        if qt == 0:
                            own.link(o)
                    o.then_inc(p_ready, 1)
                    after(g + 1, g0 + 1)
                    if with_ada:
                        add_ada(2 * h + (A + 3 * GROUPS + 1), 1)

                head(0, True, l == 0)
                with own.loop(1, HEADS // 2, 3) as h:
                    head(h, False, l == 0)
                if l == 0:
                    read_mod(3)
                with own.loop(HEADS // 2, HEADS, 3) as h:
                    head(h, False, False)

                def out_tile(i, b):
                    g = G + L_OUT
                    m = 2 * i + b
                    ve.wait_ge(g_tmp, m + (16 * l + 1))
                    xm = X[:, bass.ds(m * T, T)]
                    ve.scalar_tensor_tensor(out=xm, in0=xm, scalar=ALPHA, in1=sc[:, b * T:(b + 1) * T],
                                            op0=ALU.mult, op1=ALU.add).then_inc(g_mul, 1)
                    after(m + g, g + b)
                    if l == 0:
                        add_ada(m + (A + 2 * KT), b)

                turned(HEADS - 1)
                ve.wait_ge(o_ps, 8 * (l + 1))
                ve.wait_ge(z_ready, 16 * (l + 1))
                y_tile(2 * HEADS - 1, bank(4))
                y_rest(2 * HEADS - 1)
                if l == 0:
                    ve.wait_ge(x_back, 16)
                with ve.Fori(0, KT // 2) as i:
                    for b in range(2):
                        out_tile(i, b)
                if l == 0:
                    read_mod(4)
                ve.wait_ge(g_mul, 16 * (l + 1))
                centre(2 * l + 1, True)
                rstd(f"post{l}", [(rs[:, 0:T], bank(6, T), D)], 1e-6)
                ve.wait_ge(ln_cent, 8 * (2 * l + 2))
                for i in range(4):
                    s = X[:, i * 4 * T:(i + 1) * 4 * T]
                    own.link(ve.tensor_tensor(tiles(s, 4), tiles(s, 4), over_tokens(rs[:, 0:T], 4), ALU.mult))
                for m in range(KT):
                    s = X[:, m * T:(m + 1) * T]
                    o = ve.tensor_scalar(s, s, v("ln_g", l * KT + m), v("ln_b", l * KT + m), ALU.mult, ALU.add)
                    if m < KT - 1:
                        own.link(o)
                o.then_inc(x_norm, 1)
                ve.wait_ge(x_norm, l + 1)
                if l == 0:
                    centre(2, False)
                    rstd("pre1", [(rs[:, 0:T], bank(6, T), D)], 1e-6)
                    split_input(1, ((mu[:, :], ALU.subtract), (rs[:, 0:T], ALU.mult)), modulate(1), 4)

            ve.wait_ge(ln_acc, 8 * 4 + 8)
            rstd("mix", [(rs[:, 0:T], bank(6, T), D)], 1e-6)

            def pre_mix(o, frm, m):
                return ve.tensor_scalar(o, frm, v("g_pre_mix", m), None, ALU.mult)

            split_input(2, ((rs[:, 0:T], ALU.mult),), pre_mix, 3)
            ve.wait_ge(am_h, 1)
            lo3, hi3 = (t[:, :].rearrange("p (k t) -> p k t", k=KT)[:, :, 0:META] for t in (a_lo, a_hi))
            sub_hi(lo3, mt[:, :].rearrange("p (k t) -> p k t", k=KT), hi3).then_inc(am_l, 1)

            ahead = TAPS - 1 - META
            ve.wait_ge(ada_summed, 3 * DEPTH - 2)
            own.link(ve.memset(pad[:, 0:ahead], 0.0))

            def taps(j, lo, hi):
                for k in range(lo, hi):
                    w = v("w_dw", j * TAPS + k)
                    acc = mu[:, :] if k % 2 else conv_out[:, j * T:(j + 1) * T]
                    if k < 2:
                        o = ve.tensor_scalar(acc, pad[:, k:k + T], w, None, ALU.mult)
                    else:
                        o = ve.scalar_tensor_tensor(out=acc, in0=pad[:, k:k + T], scalar=w, in1=acc,
                                                    op0=ALU.mult, op1=ALU.add)
                    own.link(o, lag=1 if k < TAPS - 1 else 0)

            def pool_tile(j):
                ve.wait_ge(pl_in, j + 1)
                if j:
                    ve.wait_ge(pl_l, j)
                w = WINDOWS[j // 2]
                src, n, bufs = pool_z, 1, (pool_a, pool_b)
                while n < w:
                    to, first = bufs[0], 2 * n - 1
                    own.link(ve.tensor_tensor(to[:, first:TM], src[:, first:TM], src[:, first - n:TM - n], ALU.add))
                    src, n, bufs = to, 2 * n, bufs[::-1]
                ve.scalar_tensor_tensor(out=zs[:, :], in0=src[:, META:TM], scalar=1.0 / w, in1=pool_z[:, META:TM],
                                        op0=ALU.mult, op1=ALU.subtract).then_inc(pl_sum, 1)

            for j in range(CONV):
                g = B2_MIX + MIX * j
                if j:
                    ve.wait_ge(cv_done, j)
                after(g, g)
                ve.wait_ge(cv_tanh, j + 1)
                ve.scalar_tensor_tensor(out=pad[:, ahead:ahead + TM], in0=th[:, :], scalar=1.0, in1=bank(0, 0, TM),
                                        op0=ALU.add, op1=ALU.mult).then_inc(cv_in, 1)
                ve.wait_ge(cv_in, j + 1)
                after(g + 1, g + 1)
                taps(j, 0, 8)
                pool_tile(j)
                after(g + 2, g)
                taps(j, 8, 16)
                after(g + 3, g + 1)
                ve.wait_ge(pl_h, j + 1)
                s = slice(j * T, (j + 1) * T)
                sub_hi(y_lo[:, s], zs[:, :], y_hi[:, s]).then_inc(pl_l, 1)
                taps(j, 16, 24)
                if j < CONV - 1:
                    after(g + 4, g)
                taps(j, 24, TAPS)
                c = conv_out[:, j * T:(j + 1) * T]
                own.link(ve.tensor_tensor(c, c, mu[:, :], ALU.add))
                ve.tensor_scalar(c, c, 0.5, v("b_dw", j), ALU.mult, ALU.add).then_inc(cv_done, 1)
                if j == CONV - 1:
                    after(g + 4, g)
            for i, m in enumerate((0, 2, 4, 6, 1, 3, 5, 7)):
                ve.wait_ge(gp_h, i + 1)
                s = slice((CONV + m) * T, (CONV + m + 1) * T)
                ve.scalar_tensor_tensor(out=y_lo[:, s], in0=grp_ps(m), scalar=v("pool_scale", m),
                                        in1=y_hi[:, s].bitcast(F32), op0=ALU.mult, op1=ALU.subtract).then_inc(gp_l, 1)
            after(B2_GRP, B2_GRP)
            ve.wait_ge(cm_ps, 1)
            own.link(ve.tensor_scalar(mu[:, :], bank(6), 1.0 / (CONV * P), None, ALU.mult))
            for i in range(CONV // 2):
                s = tiles(conv_out[:, 2 * i * T:(2 * i + 2) * T], 2)
                ve.tensor_tensor(s, s, over_tokens(mu[:, :], 2), ALU.subtract).then_inc(cm_cent, 1)
                if i:
                    add_square(i - 1, rs[:, :], cm_sq, cm_sum)
            add_square(CONV // 2 - 1, rs[:, :], cm_sq, cm_sum)
            ve.wait_ge(cm_sum, CONV // 2)
            ve.tensor_tensor(zs[:, :], rs[:, 0:T], rs[:, T:2 * T], ALU.add).then_inc(cm_fold, 1)
            after(B2_GATE, B2_GATE)
            ve.wait_ge(cm_acc, 1)
            rstd("conv", [(rs[:, 0:T], bank(6, T), CONV * P)], 1e-5)
            for k in range(CONV):
                c = conv_out[:, k * T:(k + 1) * T]
                own.link(ve.tensor_tensor(c, c, rs[:, 0:T], ALU.mult))
                ve.tensor_scalar(c, c, v("conv_ln_g", k), v("conv_ln_b", k), ALU.mult, ALU.add).then_inc(cn_y, 1)
                ve.wait_ge(cn_tanh, k + 1)
                ve.scalar_tensor_tensor(out=zs[:, :], in0=th[:, 0:T], scalar=1.0, in1=c, op0=ALU.add,
                                        op1=ALU.mult).then_inc(cn_mul, 1)
                ve.wait_ge(cn_h, k + 1)
                s = slice(k * T, (k + 1) * T)
                ve.scalar_tensor_tensor(out=y_lo[:, s], in0=zs[:, :], scalar=0.5, in1=y_hi[:, s].bitcast(F32),
                                        op0=ALU.mult, op1=ALU.subtract).then_inc(cn_l, 1)
                if k == 0:
                    after(B2_GATE + 1, B2_GATE + 1)

            def gate_b(i):
                for b in range(2):
                    after(B2_GATE + 4 * i + b, B2_GATE + b)

            def branches(i, b):
                g, g0 = B2_GATE + 4 * i + 2 + b, B2_GATE + b
                w = wide[:, bass.ds((2 * i + b) * T, T)]
                gb = sc[:, (2 + b) * T:(3 + b) * T]
                ve.wait_ge(gt_tanh, KT + 2)
                ve.wait_ge(weights_used, g + 1)
                ve.scalar_tensor_tensor(out=w, in0=w, scalar=1.0, in1=bank((0, 2)[b]), op0=ALU.add, op1=ALU.mult)
                own.link(ve.scalar_tensor_tensor(out=gb, in0=sc[:, b * T:(b + 1) * T], scalar=1.0,
                                                 in1=bank((1, 5)[b]), op0=ALU.add, op1=ALU.mult))
                ve.tensor_tensor(w, w, gb, ALU.add).then_inc(gt_done, 1)
                after(g, g0)

            branches(0, 0)
            branches(0, 1)
            with own.loop(1, KT // 2 - 1, 2) as i:
                gate_b(i)
                branches(i, 0)
                branches(i, 1)
            last = KT // 2 - 1
            gate_b(last)
            for i in range(KT // 2):
                if i == 3:
                    branches(last, 0)
                if i == last:
                    branches(last, 1)
                ve.wait_ge(mm_h, i + 1)
                to, hi = (t[:, i * 2 * TM:(i + 1) * 2 * TM].rearrange("p (k t) -> p k t", k=2)[:, :, META:TM]
                          for t in (a_lo, a_hi))
                ve.scalar_tensor_tensor(out=to, in0=tiles(wide[:, i * 2 * T:(i + 1) * 2 * T], 2), scalar=0.5,
                                        in1=hi.bitcast(F32), op0=ALU.mult, op1=ALU.subtract).then_inc(mm_l, 1)

            def wo_tile(i, b, first):
                m = 2 * i + b
                ve.wait_ge(wo_sq, m + 1)
                s = sc[:, b * T:(b + 1) * T]
                if first and b == 0:
                    ve.tensor_copy(mu[:, :], s).then_inc(wo_acc, 1)
                else:
                    ve.wait_ge(wo_acc, m)
                    ve.tensor_tensor(mu[:, :], mu[:, :], s, ALU.add).then_inc(wo_acc, 1)
                after(m + B2_WO, B2_WO + b)

            for b in range(2):
                wo_tile(0, b, True)
            with ve.Fori(1, KT // 2) as i:
                for b in range(2):
                    wo_tile(i, b, False)
            ve.wait_ge(wo_stat, 1)
            ve.wait_ge(wo_out, KT)
            rstd("wo", [(rs[:, 0:T], bank(6), D)], 1e-6)

            def new_h(m, par):
                buf = sc[:, par * T:(par + 1) * T]
                xm = X[:, bass.ds(m * T, T)]
                own.link(ve.scalar_tensor_tensor(out=buf, in0=wide[:, bass.ds(m * T, T)],
                                                 scalar=v("g_post_mix", m), in1=rs[:, 0:T],
                                                 op0=ALU.mult, op1=ALU.mult))
                ve.tensor_tensor(xm, xm, buf, ALU.add).then_inc(h_new, 1)

            def rest_h(m, par, first):
                ve.wait_ge(h_hi, m + 1)
                ve.wait_ge(h_new, m + 1)
                ve.scalar_tensor_tensor(out=a_tile(a_lo, m), in0=X[:, bass.ds(m * T, T)], scalar=v("g_pre_mlp", m),
                                        in1=a_tile(a_hi, m).bitcast(F32), op0=ALU.mult, op1=ALU.subtract)\
                    .then_inc(h_lo, 1)
                ve.wait_ge(h_sq, m + 1)
                s = sc[:, (2 + par) * T:(3 + par) * T]
                if first:
                    ve.tensor_copy(mu[:, :], s).then_inc(h_acc, 1)
                else:
                    ve.wait_ge(h_acc, m)
                    ve.tensor_tensor(mu[:, :], mu[:, :], s, ALU.add).then_inc(h_acc, 1)

            new_h(0, 0)
            new_h(1, 1)
            rest_h(0, 0, True)
            with own.loop(1, KT // 2, 2) as i:
                for b in range(2):
                    new_h(2 * i + b, b)
                    rest_h(2 * i + b - 1, 1 - b, False)
            rest_h(KT - 1, 1, False)

            def up(f, i, b):
                m = 16 * f + 2 * i + b
                g = B2_FF + 32 * f + 2 * i + b
                r, s = sc[:, b * T:(b + 1) * T], sc[:, (2 + b) * T:(3 + b) * T]
                ve.wait_ge(f_relu, m + 1)
                ve.tensor_tensor(s, r, r, ALU.mult).then_inc(f_sq, 1)
                ve.wait_ge(f_sq, m + 1)
                ve.wait_ge(f_hi, m + 1)
                at = bass.ds((2 * i + b) * T, T)
                sub_hi(y_lo[:, at], s, y_hi[:, at]).then_inc(f_lo, 1)
                after(g, B2_FF + b)

            def down(f, i, b, last=False):
                m = 16 * f + 2 * i + b
                g = B2_FF + KT + 32 * f + 2 * i + b
                ve.wait_ge(weights_used, g + 1)
                o = wide[:, bass.ds((2 * i + b) * T, T)]
                if isinstance(f, int) and f == 0:
                    ve.tensor_copy(o, bank(2 + b)).then_inc(f_acc, 1)
                else:
                    ve.wait_ge(f_acc, m - 15)
                    ve.tensor_tensor(o, o, bank(2 + b), ALU.add).then_inc(f_acc, 1)
                if not last:
                    after(g, B2_FF + b)

            with ve.Fori(0, KT // 2) as i:
                for b in range(2):
                    up(0, i, b)
            ve.wait_ge(h_stat, 1)
            own.link(ve.tensor_scalar(rs[:, 0:T], bank(6, T), 1.0 / D, 1e-6, ALU.mult, ALU.add))
            own.link(ve.reciprocal(rs[:, 0:T], rs[:, 0:T]))
            with ve.Fori(0, KT // 2) as i:
                for b in range(2):
                    down(0, i, b)
            with ve.Fori(1, FF_BLOCKS - 1) as f:
                with ve.Fori(0, KT // 2) as i:
                    for b in range(2):
                        up(f, i, b)
                with ve.Fori(0, KT // 2) as i:
                    for b in range(2):
                        down(f, i, b)
            f = FF_BLOCKS - 1
            with ve.Fori(0, KT // 2) as i:
                for b in range(2):
                    up(f, i, b)
            with ve.Fori(0, KT // 2 - 1) as i:
                for b in range(2):
                    down(f, i, b)
            for b in range(2):
                down(f, KT // 2 - 1, b, True)
            ve.wait_ge(f_osum, KT // 2)
            own.link(ve.tensor_tensor(mu[:, :], rs[:, 0:T], rs[:, 0:T], ALU.mult))
            own.link(ve.scalar_tensor_tensor(out=rs[:, T:2 * T], in0=bank(6), scalar=1.0 / D, in1=mu[:, :],
                                             op0=ALU.mult, op1=ALU.mult))
            ve.tensor_scalar(rs[:, T:2 * T], rs[:, T:2 * T], 1e-6, None, ALU.add).then_inc(ln_var, 1)
            ve.wait_ge(ln_std, NORM["out"] + 1)
            own.link(ve.reciprocal(rs[:, T:2 * T], rs[:, T:2 * T]))
            own.link(ve.tensor_tensor(rs[:, 0:T], rs[:, 0:T], rs[:, T:2 * T], ALU.mult))
            ve.wait_ge(f_acc, 16 * FF_BLOCKS)
            for m in range(KT):
                s = slice(m * T, (m + 1) * T)
                t = sc[:, (m % 4) * T:(m % 4 + 1) * T]
                own.link(ve.scalar_tensor_tensor(out=t, in0=wide[:, s], scalar=v("g_post_mlp", m),
                                                 in1=rs[:, 0:T], op0=ALU.mult, op1=ALU.mult))
                ve.tensor_tensor(X[:, s], X[:, s], t, ALU.add).then_inc(y_out, 1)


def by_tile(w):
    k, n = w.shape
    return w.reshape(k // P, P, n // P, P).transpose(2, 1, 0, 3).reshape(n // P, P, k)


def padded(chunks):
    out = np.zeros((chunks.shape[0], P, CH), np.float32)
    out[:, :, :chunks.shape[2]] = chunks
    return out


def columns(a):
    return np.asarray(a).reshape(-1, P).T


def swap_halves(w):
    h = ROPE // 2
    return np.concatenate([w[..., h:], w[..., :h]], axis=-1)


def dft(n):
    k = np.outer(np.arange(n), np.arange(n)) % n
    return (np.cos(2 * np.pi * k / n) / np.sqrt(n)), (np.sin(2 * np.pi * k / n) / np.sqrt(n))


def weight_stream(i):
    parts = []
    cos_s, sin_s = dft(T)
    cos_c, sin_c = dft(P)
    seq = np.concatenate([t.reshape(2, P, T).transpose(1, 0, 2).reshape(P, 2 * T) for t in (cos_s, -sin_s)], axis=1)
    seq = seq.astype(np.float32)
    chan = np.concatenate([cos_c, sin_c], axis=1).astype(np.float32)
    for l in range(DEPTH):
        w = np.asarray(i["w_in"][l])
        u, z, cq, ckv, kr, za = np.split(w, np.cumsum([1024, 1024, 512, 256, ROPE]), axis=1)
        parts.append(by_tile(np.concatenate([cq, ckv, kr, swap_halves(kr)], axis=1)))
        parts.append(padded(seq[None]))
        fm = np.asarray(i["w_fmix"][l]).transpose(1, 0, 2).reshape(P, GROUPS * P)
        parts.append(padded(np.concatenate([fm, chan], axis=1)[None]))
        parts.append(np.stack([by_tile(u), by_tile(z)], axis=1).reshape(2 * GROUPS, P, CH))
        wq = np.asarray(i["w_q_b"][l]).reshape(QT, P, HEADS, P + ROPE)
        wkv = np.asarray(i["w_kv_b"][l]).reshape(CT, P, HEADS, 2, P)
        nope, rp = wq[..., :P], wq[..., P:]
        rp = np.concatenate([rp, swap_halves(rp)], axis=-1)
        head = np.concatenate([nope, rp, wkv[:, :, :, 0], wkv[:, :, :, 1]], axis=0)
        head = head.transpose(2, 1, 0, 3).reshape(HEADS, P, 12 * P)
        parts.append(np.stack([padded(head), by_tile(za)], axis=1).reshape(2 * HEADS, P, CH))
        parts.append(by_tile(np.asarray(i["w_out"][l])))
    w = by_tile(np.asarray(i["w_in_2"][0]))
    z, val, gat, ga, gb = np.split(w, np.cumsum([CONV, CONV, CONV, KT]), axis=0)
    mix = np.concatenate([np.stack([val, gat, z], axis=1), ga.reshape(CONV, 2, P, CH)], axis=1)
    parts.append(mix.reshape(MIX * CONV, P, CH))
    grp = np.asarray(i["w_pool_grp_2"][0]).reshape(4, 2, P, 2, P)
    parts.append(grp.transpose(2, 0, 3, 1, 4).reshape(1, P, CH))
    po, co = (np.asarray(i[n][0]).reshape(CONV, P, KT, P).transpose(2, 1, 0, 3).reshape(KT, P, HALF)
              for n in ("w_pool_out_2", "w_conv_out_2"))
    branch = np.concatenate([po, co], axis=2).reshape(KT // 2, 2, P, CH)
    parts.append(np.concatenate([gb.reshape(KT // 2, 2, P, CH), branch], axis=1).reshape(2 * KT, P, CH))
    parts.append(by_tile(np.asarray(i["w_o_2"][0])))
    up = by_tile(np.asarray(i["w_up_2"][0])).reshape(FF_BLOCKS, KT, P, CH)
    down = np.asarray(i["w_down_2"][0]).reshape(FF_BLOCKS, KT, P, KT, P).transpose(0, 3, 2, 1, 4)
    parts.append(np.concatenate([up, down.reshape(FF_BLOCKS, KT, P, CH)], axis=1).reshape(-1, P, CH))
    return np.concatenate(parts, axis=0)


def kernel(**i):
    import concourse.bacc as bacc
    from concourse.bass_utils import run_bass_kernel_spmd

    def f32(name):
        return np.asarray(i[name])

    stream = weight_stream(i)
    assert stream.shape == (CHUNKS, P, CH), stream.shape
    ada = f32("w_ada").reshape(DEPTH, KT, P, 3, D).transpose(0, 3, 1, 2, 4).reshape(ADA, P, D)[ADA0:]
    ada0 = f32("w_ada")[0].reshape(4, 4, P, 3, 4, 512)[:, :, :, :2].transpose(4, 3, 0, 2, 1, 5)
    ada0 = ada0.reshape(ADA0, P, CH)
    taps = f32("w_dw_2")[0].reshape(TAPS, CONV, P).transpose(1, 0, 2)
    named = {"c": f32("c"), "b_ada": f32("b_ada"), "q_norm": f32("q_norm"), "kv_norm": f32("kv_norm"),
             "ln_g": f32("ln_g"), "ln_b": f32("ln_b"), "g_pre_mix": f32("g_pre_mix_2"),
             "pool_scale": f32("pool_scale_2"), "w_dw": taps, "b_dw": f32("b_dw_2"),
             "conv_ln_g": f32("conv_ln_g_2"), "conv_ln_b": f32("conv_ln_b_2"),
             "g_post_mix": f32("g_post_mix_2"), "g_pre_mlp": f32("g_pre_mlp_2"), "g_post_mlp": f32("g_post_mlp_2")}
    vectors = np.concatenate([columns(named[n]) for n, _ in VECTORS], axis=1)
    p = np.arange(P)
    freq = np.float32(10000.0) ** (-np.arange(0, ROPE, 2, dtype=np.float32) / np.float32(ROPE))
    consts = np.concatenate([
        np.eye(P), (p[:, None] % ROPE == p[None] % ROPE), freq[p % (ROPE // 2)][:, None],
        np.where(p < ROPE, np.pi / 2, 0.0)[:, None],
        np.where((p >= ROPE) & (p < ROPE + ROPE // 2), -1.0, 1.0)[:, None]], axis=1).astype(np.float32)
    positions = np.ascontiguousarray(np.broadcast_to(np.asarray(i["positions"]).astype(np.int32), (P, T)))
    x = f32("x")[0].reshape(T, KT, P).transpose(2, 1, 0).reshape(P, KT * T)
    meta = f32("meta_2").reshape(META, KT, P).transpose(2, 1, 0).reshape(P, KT * META)
    arrays = {"stream": stream, "ada0": ada0, "ada": ada, "vectors": vectors, "consts": consts, "positions": positions,
              "x": x, "meta": meta}
    nc = bacc.Bacc("TRN2", target_bir_lowering=False, num_devices=1)
    aps = {}
    for name, a in arrays.items():
        arrays[name] = a = np.ascontiguousarray(a)
        aps[name] = nc.dram_tensor(f"in_{name}", a.shape, mybir.dt.from_np(a.dtype), kind="ExternalInput").ap()
    out = nc.dram_tensor("out", (P, KT * T), F32, kind="ExternalOutput").ap()
    build(nc, **aps, out=out)
    r = run_bass_kernel_spmd(nc, [{f"in_{n}": a for n, a in arrays.items()}], core_ids=[0])
    y = np.asarray(r.results[0]["out"])
    return y.reshape(P, KT, T).transpose(2, 1, 0).reshape(1, T, D)
```

```python
from contextlib import ExitStack, contextmanager

import numpy as np
import concourse.bass as bass
from concourse import mybir

F32 = mybir.dt.float32
F32R = mybir.dt.float32r
I32 = mybir.dt.int32
ALU = mybir.AluOpType
ACT = mybir.ActivationFunctionType
AX = mybir.AxisListType

P = 128
T = 256
META = 16
TM = T + META
D = 2048
KT = D // P
DEPTH = 2
HEADS = 8
GROUPS = 8
ROPE = 64
QT = 512 // P
CT = 256 // P
LAT = QT + CT + 1
CONV = 1024 // P
TAPS = 31
WINDOWS = (2, 4, 8, 16)
FF_BLOCKS = 8192 // D
ALPHA = (2 * DEPTH) ** 0.25
SM_SCALE = 1.0 / float(np.sqrt(192.0))

CH = 16 * P
HALF = CH // 2
RAW = 3

L_DFT = LAT
L_FMIX = LAT + 1
L_FOUR = LAT + 2
L_HEAD = L_FOUR + 2 * GROUPS
L_OUT = L_HEAD + 2 * HEADS
PER_LAYER = L_OUT + KT
B2_MIX = DEPTH * PER_LAYER
MIX = 5
B2_GRP = B2_MIX + MIX * CONV
B2_GATE = B2_GRP + 1
B2_WO = B2_GATE + 2 * KT
B2_FF = B2_WO + KT
CHUNKS = B2_FF + 2 * KT * FF_BLOCKS
ADA = 3 * DEPTH * KT
ADA0 = 2 * KT

VECTORS = (("c", KT), ("b_ada", 3 * DEPTH * KT), ("q_norm", DEPTH * QT), ("kv_norm", DEPTH * CT),
           ("ln_g", DEPTH * KT), ("ln_b", DEPTH * KT), ("g_pre_mix", KT), ("pool_scale", CONV),
           ("w_dw", TAPS * CONV), ("b_dw", CONV), ("conv_ln_g", CONV), ("conv_ln_b", CONV),
           ("g_post_mix", KT), ("g_pre_mlp", KT), ("g_post_mlp", KT))
COL = {}
NV = 0
for _name, _n in VECTORS:
    COL[_name] = NV
    NV += _n
NC_ = 2 * P + 3


FOLDED = 3


class Chain:

    def __init__(self, eng, sem):
        self.eng, self.sem, self.n, self.i, self.per = eng, sem, 0, None, 0

    def link(self, ins, lag=0):
        self.n += 1
        ins.then_inc(self.sem, 1)
        n = self.n - lag
        self.eng.wait_ge(self.sem, n if self.i is None else self.i * self.per + n)

    @contextmanager
    def loop(self, start, end, per):
        base = self.n
        with self.eng.Fori(start, end) as i:
            self.i, self.per, self.n = i, per, base - start * per
            yield i
            assert self.n == base - start * per + per, (self.n - base + start * per, per)
        self.i, self.n = None, base + per * (end - start)


def build(nc, stream, ada0, ada, vectors, consts, positions, x, meta, out):
    with ExitStack() as ctx:
        def sb(name, cols, dt=F32):
            return ctx.enter_context(nc.sbuf_tensor(name, [P, cols], dt))

        def sem(name):
            return ctx.enter_context(nc.semaphore(name))

        raw = sb("raw", RAW * CH)
        w_hi = sb("w_hi", 2 * CH, F32R)
        w_lo = sb("w_lo", 2 * CH, F32R)
        area = sb("area", 3 * CH)
        X = sb("X", KT * T)
        a_hi = sb("a_hi", KT * TM, F32R)
        a_lo = sb("a_lo", KT * TM, F32R)
        y_hi = sb("y_hi", KT * T, F32R)
        y_lo = sb("y_lo", KT * T, F32R)
        lat_hi = sb("lat_hi", (QT + CT) * T, F32R)
        lat_lo = sb("lat_lo", (QT + CT) * T, F32R)
        st = sb("st", 14 * T, F32R)
        kr_hi = sb("kr_hi", T, F32R)
        kr_lo = sb("kr_lo", T, F32R)
        rope = sb("rope", T)
        sc = sb("sc", 4 * T)
        rs = sb("rs", 2 * T)
        mu = sb("mu", T)
        zs = sb("zs", T)
        th = sb("th", TM)
        vec = sb("vec", NV)
        con = sb("con", NC_)
        mod = sb("mod", ADA)
        ones = sb("ones", P)
        csil = sb("csil", 2 * KT)
        row = sb("row", 512)
        mt = sb("mt", KT * META)
        stat = sb("stat", 8)
        pos = th[:, 0:T].bitcast(I32)

        ps = ctx.enter_context(nc.psum_tensor("ps", [P, 8 * 512], F32))

        def bank(b, a=0, n=T):
            return ps[:, b * 512 + a:b * 512 + a + n]

        def two_tiles(t, i):
            return t[:, i * 2 * TM:(i + 1) * 2 * TM].rearrange("p (k t) -> p k t", k=2)[:, :, META:TM]

        def cn_buf(k):
            return (sc[:, 2 * T:3 * T], sc[:, 3 * T:4 * T], zs[:, :], th[:, 0:T])[k % 4]

        def ada0_slot(s):
            return raw[:, 2 * CH:3 * CH] if s == 3 else area[:, s * CH:(s + 1) * CH]

        def lat_ps(m):
            return bank(4 + m % 3, m // 3 * T)

        def grp_ps(m):
            return bank((0, 1, 5, 7)[m // 2], (m % 2) * T)

        def v(name, i, n=1):
            return vec[:, bass.ds(COL[name] + i, n)]

        ident, pairs = con[:, 0:P], con[:, P:2 * P]
        ada_ring = area[:, 0:2 * CH]
        ada_acc = area[:, 2 * CH:3 * CH]
        dft_hi, dft_lo = st[:, 0:4 * T], st[:, 4 * T:8 * T]
        u_hi, u_lo = st[:, 8 * T:9 * T], st[:, 9 * T:10 * T]
        t_hi, t_lo = st[:, 10 * T:12 * T], st[:, 12 * T:14 * T]
        qn_hi, qn_lo, qr_hi, qr_lo = (st[:, i * T:(i + 1) * T] for i in range(4))
        kn_hi, kn_lo, vv_hi, vv_lo = (st[:, i * T:(i + 1) * T] for i in range(4, 8))
        pt_hi, pt_lo = st[:, 8 * T:10 * T], st[:, 10 * T:12 * T]
        cw_hi, cw_lo = y_hi[:, 8 * T:16 * T], y_lo[:, 8 * T:16 * T]
        wide = area[:, 0:KT * T]
        conv_out = area[:, KT * T:(KT + CONV) * T]
        pad = rs[:, 0:TAPS - 1 - META + TM]
        pool_z, pool_a, pool_b = (sc[:, at:at + TM] for at in (0, TM, 2 * TM))

        def a_tile(t, k, lo=META, n=T):
            return t[:, bass.ds(k * TM + lo, n)]

        landed = [sem("landed0"), sem("landed1")]
        hi_ready, lo_ready = sem("hi_ready"), sem("lo_ready")
        weights_used = sem("weights_used")
        ada0_landed = [sem(f"ada0_landed{i}") for i in range(4)]
        ada0_fold = sem("ada0_fold")
        ada0_used = sem("ada0_used")
        row_in = sem("row_in")
        col_ps, col_in = sem("col_ps"), sem("col_in")
        ada_landed = [sem("ada_landed0"), sem("ada_landed1")]
        ada_step = sem("ada_step")
        ada_clear = sem("ada_clear")
        ada_summed = sem("ada_summed")
        mod_ready = sem("mod_ready")
        vec_in = sem("vec_in")
        x_in = sem("x_in")
        small = sem("small")
        ones_set, c_tanh, c_ready = sem("ones_set"), sem("c_tanh"), sem("c_ready")
        rope_arg, rope_sin = sem("rope_arg"), sem("rope_sin")
        dve = sem("dve")
        ln_mean = sem("ln_mean")
        ln_cent, ln_sq, ln_acc = sem("ln_cent"), sem("ln_sq"), sem("ln_acc")
        ln_var, ln_std = sem("ln_var"), sem("ln_std")
        ln_y, ln_hi, ln_lo = sem("ln_y"), sem("ln_hi"), sem("ln_lo")
        x_sum, x_fold = sem("x_sum"), sem("x_fold")
        x_stat = sem("x_stat")
        r_acc = sem("r_acc")
        in_norm, mix_norm = sem("in_norm"), sem("mix_norm")
        mix_hi = sem("mix_hi")
        ln_app, x_new, x_sq = sem("ln_app"), sem("x_new"), sem("x_sq")
        lat_sq, lat_acc, lat_stat = sem("lat_sq"), sem("lat_acc"), sem("lat_stat")
        lat_y, lat_h, lat_l = sem("lat_y"), sem("lat_h"), sem("lat_l")
        cw_h, cw_l = sem("cw_h"), sem("cw_l")
        kr_rot, kr_sum, kr_h, kr_l = sem("kr_rot"), sem("kr_sum"), sem("kr_h"), sem("kr_l")
        u_h, u_l = sem("u_h"), sem("u_l")
        t_ps, t_h, t_l, yf_ps = sem("t_ps"), sem("t_h"), sem("t_l"), sem("yf_ps")
        z_tanh, z_ready = sem("z_tanh"), sem("z_ready")
        y_mul, y_h, y_l = sem("y_mul"), sem("y_h"), sem("y_l")
        q_h, q_l, qr_rot = sem("q_h"), sem("q_l"), sem("qr_rot")
        v_h, v_l = sem("v_h"), sem("v_l")
        s_ps, s_max, s_exp, p_ready = sem("s_ps"), sem("s_max"), sem("s_exp"), sem("p_ready")
        s_sum = sem("s_sum")
        pt_ps, pt_h, pt_l, o_ps = sem("pt_ps"), sem("pt_h"), sem("pt_l"), sem("o_ps")
        g_tmp, g_mul = sem("g_tmp"), sem("g_mul")
        m_sq, m_acc = sem("m_sq"), sem("m_acc")
        am_y, am_h, am_l = sem("am_y"), sem("am_h"), sem("am_l")
        cv_tanh, cv_in, cv_done = sem("cv_tanh"), sem("cv_in"), sem("cv_done")
        pl_in, pl_sum, pl_h, pl_l = sem("pl_in"), sem("pl_sum"), sem("pl_h"), sem("pl_l")
        gp_h, gp_l = sem("gp_h"), sem("gp_l")
        cm_sum = sem("cm_sum")
        cm_fold = sem("cm_fold")
        cm_ps, cm_cent, cm_sq, cm_acc = sem("cm_ps"), sem("cm_cent"), sem("cm_sq"), sem("cm_acc")
        cn_y, cn_tanh, cn_mul, cn_h, cn_l = (sem(n) for n in ("cn_y", "cn_tanh", "cn_mul", "cn_h", "cn_l"))
        gt_tanh, gt_done = sem("gt_tanh"), sem("gt_done")
        mm_h, mm_l = sem("mm_h"), sem("mm_l")
        wo_out, wo_sq, wo_acc, wo_stat = sem("wo_out"), sem("wo_sq"), sem("wo_acc"), sem("wo_stat")
        h_new, h_hi, h_sq, h_lo, h_acc, h_stat = (sem(n) for n in ("h_new", "h_hi", "h_sq", "h_lo", "h_acc", "h_stat"))
        f_relu, f_sq, f_hi, f_lo, f_acc = (sem(n) for n in ("f_relu", "f_sq", "f_hi", "f_lo", "f_acc"))
        f_osq, f_osum = sem("f_osq"), sem("f_osum")
        y_out, stored = sem("y_out"), sem("stored")

        SMALL = 3 * 16
        NORM = {n: i for i, n in enumerate(("pre0", "meta", "lat0", "post0", "pre1", "lat1", "post1",
                                            "mix", "conv", "wo", "out"))}
        block = ctx.enter_context(nc.Block())

        @block.sync
        def _(sp):
            sp.dma_start(vec[:, :], vectors).then_inc(vec_in, 16)
            for s in range(4):
                sp.dma_start(ada0_slot(s), ada0[s]).then_inc(ada0_landed[s], 16)
            sp.dma_start(X[:, :], x).then_inc(x_in, 16)
            sp.dma_start(con[:, :], consts).then_inc(small, 16)
            sp.dma_start(pos, positions).then_inc(small, 16)
            sp.dma_start(mt[:, :], meta).then_inc(small, 16)

            def load(g, par, waits):
                if waits:
                    split_before = sp.snap(sp.to_reg(2 * g - 2 * RAW + 2))
                    landed_before = sp.snap(sp.to_reg(8 * (g - par)))
                    sp.wait_ge(lo_ready, split_before)
                    sp.wait_ge(landed[par], landed_before)
                sp.dma_start(raw[:, bass.ds((g % RAW) * CH, CH)],
                             stream[bass.ds(g, 1)].rearrange("a p n -> (a p) n")).then_inc(landed[par], 16)

            load(0, 0, False)
            load(1, 1, False)
            with sp.Fori(1, ADA0 // 4) as i:
                for s in range(4):
                    sp.wait_ge(ada0_used, 4 * i + s - 3)
                    sp.dma_start(ada0_slot(s), ada0[bass.ds(4 * i + s, 1)].rearrange("a p n -> (a p) n"))\
                        .then_inc(ada0_landed[s], 16)
            sp.wait_ge(landed[0], 16)
            sp.wait_ge(ada0_used, ADA0)
            load(2, 0, False)
            sp.wait_ge(landed[1], 16)
            sp.wait_ge(lo_ready, 2)
            load(3, 1, False)
            with sp.Fori(2, CHUNKS // 2) as i:
                for par in range(2):
                    load(2 * i + par, par, True)
            sp.wait_ge(lo_ready, 2 * (CHUNKS - RAW))
            sp.wait_ge(landed[0], 8 * (CHUNKS - 1))
            load(CHUNKS - 1, 0, False)
            for q in range(4):
                sp.wait_ge(y_out, 4 * q + 4)
                sp.dma_start(out[:, q * 4 * T:(q + 1) * 4 * T],
                             X[:, q * 4 * T:(q + 1) * 4 * T]).then_inc(stored, 16)
            sp.wait_ge(stored, 4 * 16)

        @block.gpsimd
        def _(pool):
            pool.wait_ge(ada0_used, ADA0)
            for a in range(2):
                pool.dma_start(ada_ring[:, a * CH:(a + 1) * CH], ada[a]).then_inc(ada_landed[a], 16)
            with pool.Fori(1, (ADA - ADA0) // 2) as i:
                for par in range(2):
                    pool.wait_ge(ada_step, 2 * i + par - 1)
                    pool.dma_start(ada_ring[:, par * CH:(par + 1) * CH],
                                   ada[bass.ds(2 * i + par, 1)].rearrange("a p n -> (a p) n"))\
                        .then_inc(ada_landed[par], 16)

        @block.tensor
        def _(pe):
            def mm3(o, w, a, first, last):
                pe.matmul(o, w[1], a[0], start=first, stop=False)
                pe.matmul(o, w[0], a[1], start=False, stop=False)
                return pe.matmul(o, w[0], a[0], start=False, stop=last)

            def wb(par, k, n=P):
                at = par * CH + k * P
                return w_hi[:, at:at + n], w_lo[:, at:at + n]

            def a_ops(k):
                return a_tile(a_hi, k), a_tile(a_lo, k)

            def am_ops(k):
                return a_tile(a_hi, k, 0, TM), a_tile(a_lo, k, 0, TM)

            def y_ops(k):
                return y_hi[:, k * T:(k + 1) * T], y_lo[:, k * T:(k + 1) * T]

            def half(g, h):
                pe.wait_ge(lo_ready, 2 * g + h + 1)

            def blocks(par, o, ops, ks, first, last, w0=0):
                for k in ks:
                    r = mm3(o, wb(par, w0 + k), ops(k), first and k == ks[0], last and k == ks[-1])
                return r

            def chunk(g, par, o, ops):
                half(g, 0)
                blocks(par, o, ops, range(8), True, False)
                half(g, 1)
                blocks(par, o, ops, range(8, 16), False, True).then_inc(weights_used, 1)

            def first_chunk(g, o, ops, n):
                for k in range(KT):
                    if k % 8 == 0:
                        half(g, k // 8)
                    if k % 2 == 0:
                        pe.wait_ge(ln_lo, 8 * n + k // 2 + 1)
                    r = mm3(o, wb(g % 2, k), ops(k), k == 0, k == KT - 1)
                r.then_inc(weights_used, 1)

            def ada_sum(r):
                pe.wait_ge(ada_step, KT * (r - 1))
                if r > 2:
                    pe.wait_ge(mod_ready, r - 2)
                for m in range(KT):
                    o = pe.matmul(bank(7, m, 1), ada_acc[:, m * P:(m + 1) * P], ones[:, 0:1],
                                  start=True, stop=True)
                o.then_inc(ada_summed, 1)


            def squares(n):
                for i in range(KT // 2):
                    pe.wait_ge(ln_sq, 8 * n + i + 1)
                    for j in range(2):
                        at = (i % 2) * 2 * T + j * T
                        o = pe.matmul(bank(6, T), ones[:, :], sc[:, at:at + T],
                                      start=i + j == 0, stop=i == KT // 2 - 1 and j == 1)
                    o.then_inc(ln_acc, 1)

            def ada_row(r):
                if r >= 2:
                    pe.wait_ge(row_in, r - 1)
                for s in range(4):
                    pe.wait_ge(ada0_landed[s], 16 * r + 16)
                    w = ada0_slot(s)
                    folded = s % 2 if r >= FOLDED else 0
                    if folded:
                        pe.wait_ge(ada0_fold, 2 * (r - FOLDED) + s // 2 + 1)
                    for k in range(folded, 4):
                        c = KT + 4 * s + k
                        o = pe.matmul(ps[0:1, (1 + r % 2) * 512:(2 + r % 2) * 512],
                                      ones[:, 0:1] if k == folded == 1 else csil[:, c:c + 1],
                                      w[:, k * 512:(k + 1) * 512], start=s + k == 0, stop=s + k == 6)
                    o.then_inc(ada0_used, 1)

            def turn_row(r):
                pe.wait_ge(row_in, r + 1)
                if r >= 4:
                    pe.wait_ge(col_in, r // 2 - 1)
                for t in range(4):
                    o = pe.matmul(bank((3, 7)[r // 2 % 2], 4 * (r % 2) + t, 1), row[0:1, t * P:(t + 1) * P],
                                  ones[0:1, 0:1], start=True, stop=True)
                o.then_inc(col_ps, 1)

            pe.wait_ge(ones_set, 1)
            pe.wait_ge(c_ready, 1)
            for r in range(ADA0 // 4):
                ada_row(r)
                if r:
                    turn_row(r - 1)
                if r == 0:
                    pe.wait_ge(x_sum, 1)
                    pe.matmul(bank(6), ones[:, :], mu[:, :], start=True, stop=True).then_inc(ln_mean, 1)
                if r == 1:
                    pe.wait_ge(x_fold, 1)
                    pe.matmul(bank(6, T), ones[:, :], sc[:, 0:T], start=True, stop=True).then_inc(x_stat, 1)
                    pe.wait_ge(m_sq, 1)
                    pe.matmul(bank(5, 0, META), ones[:, :], zs[:, 0:META], start=True, stop=True)\
                        .then_inc(m_acc, 1)
            turn_row(ADA0 // 4 - 1)

            for l in range(DEPTH):
                G = l * PER_LAYER
                pe.wait_ge(ln_var, NORM["meta"] + 1)
                for m in range(LAT - 1):
                    if m >= 3:
                        pe.wait_ge(lat_sq, 6 * l + m - 2)
                    if m:
                        chunk(G + m, (G + m) % 2, lat_ps(m), a_ops)
                    else:
                        first_chunk(G, lat_ps(0), a_ops, l)
                if l:
                    pe.wait_ge(mod_ready, 3)
                chunk(G + LAT - 1, (G + LAT - 1) % 2, bank(7), a_ops)
                pe.wait_ge(lat_acc, 6 * (l + 1))
                pe.matmul(bank(3, 0, 2 * T), ones[:, :], sc[:, 0:2 * T], start=True, stop=True)\
                    .then_inc(lat_stat, 1)
                pe.wait_ge(lo_ready, 2 * (G + L_DFT) + 2)
                pe.wait_ge(weights_used, G + L_DFT)
                pe.nop().then_inc(weights_used, 1)
                g = G + L_FMIX
                half(g, 0)
                half(g, 1)
                pe.wait_ge(kr_rot, l + 1)
                for j, b in enumerate((0, 1, 2, 7)):
                    o = mm3(bank(b, 0, 512), wb(g % 2, 8 + j // 2), wb(g % 2, 4 * (j % 2), 512), True, True)
                o.then_inc(weights_used, 1)
                def seq_dft(q, first):
                    pe.wait_ge(t_l, 8 * l + q + 1)
                    if first:
                        pe.wait_ge(cw_l, 4 * l + 3)
                    else:
                        pe.wait_ge(y_mul, 16 * l + q)
                    for j in range(4):
                        tile_, trig = j // 2, j % 2
                        at, rhs = tile_ * T + trig * P, (2 * trig + tile_) * T
                        o = mm3(bank(2), (t_hi[:, at:at + P], t_lo[:, at:at + P]),
                                (dft_hi[:, rhs:rhs + T], dft_lo[:, rhs:rhs + T]), j == 0, j == 3)
                    o.then_inc(yf_ps, 1)

                def group(q, first, second=False):
                    g = G + L_FOUR + 2 * q
                    g0 = G + L_FOUR
                    if first:
                        pe.wait_ge(cw_l, 4 * l + 1)
                    chunk(g, g0 % 2, bank(0), a_ops)
                    if first:
                        pe.wait_ge(cw_l, 4 * l + 2)
                    else:
                        seq_dft(q - 1, second)
                        pe.wait_ge(z_ready, 16 * l + q)
                    chunk(g + 1, (g0 + 1) % 2, bank(1), a_ops)
                    pe.wait_ge(u_l, 8 * l + q + 1)
                    if first:
                        pe.wait_ge(cw_l, 4 * (l + 1))
                        pe.wait_ge(ln_var, NORM[f"lat{l}"] + 1)
                    for j in range(2):
                        o = mm3(bank(3, j * T), (u_hi[:, j * P:(j + 1) * P], u_lo[:, j * P:(j + 1) * P]),
                                (cw_hi[:, bass.ds(q * T, T)], cw_lo[:, bass.ds(q * T, T)]), True, True)
                    o.then_inc(t_ps, 1)

                group(0, True)
                group(1, False, True)
                with pe.Fori(2, GROUPS // 2 + 1) as q:
                    group(q, False)
                ada_sum(2 if l == 0 else 5)
                with pe.Fori(GROUPS // 2 + 1, GROUPS) as q:
                    group(q, False)
                pe.wait_ge(lat_l, 6 * (l + 1))
                pe.matmul(bank(4), pairs, sc[:, 3 * T:4 * T], start=True, stop=True).then_inc(kr_sum, 1)

                def project(h, first):
                    g = G + L_HEAD + 2 * h
                    par = (G + L_HEAD) % 2
                    half(g, 0)
                    if first:
                        pe.wait_ge(lat_l, 6 * (l + 1))
                        pe.wait_ge(z_ready, 16 * l + GROUPS)

                    def lat(k):
                        return lat_hi[:, k * T:(k + 1) * T], lat_lo[:, k * T:(k + 1) * T]
                    blocks(par, bank(0), lat, range(QT), True, True)
                    blocks(par, bank(0, T), lat, range(QT), True, True, QT)
                    half(g, 1)
                    if not first:
                        pe.wait_ge(v_l, 8 * l + h)
                    for k in range(CT):
                        mm3(bank(1), wb(par, 8 + k), lat(QT + k), k == 0, k == CT - 1)
                    for tt in range(2):
                        for k in range(CT):
                            o = mm3(bank(1, T + tt * P, P),
                                    tuple(t[:, tt * P:(tt + 1) * P] for t in lat(QT + k)),
                                    wb(par, 10 + k), k == 0, k == CT - 1)
                    o.then_inc(weights_used, 1)

                def turn(h):
                    pe.wait_ge(p_ready, 2 * (8 * l + h) + 2)
                    for qt in range(2):
                        for kt in range(2):
                            o = pe.transpose(bank(3, kt * T + qt * P, P),
                                             sc[:, qt * T + kt * P:qt * T + kt * P + P], ident)
                    o.then_inc(pt_ps, 1)

                def attend(h, first=False):
                    pe.wait_ge(pt_l, 8 * l + h + 1)
                    pe.wait_ge(v_l, 8 * l + h + 1)
                    if not first:
                        pe.wait_ge(y_mul, 16 * l + GROUPS + h)
                    for k in range(2):
                        o = mm3(bank(4), (vv_hi[:, k * P:(k + 1) * P], vv_lo[:, k * P:(k + 1) * P]),
                                (pt_hi[:, k * T:(k + 1) * T], pt_lo[:, k * T:(k + 1) * T]), k == 0, k == 1)
                    o.then_inc(o_ps, 1)

                def head(h, first, second=False):
                    g = G + L_HEAD + 2 * h
                    par = (G + L_HEAD + 1) % 2
                    project(h, first)
                    if first:
                        seq_dft(GROUPS - 1, False)
                    half(g + 1, 0)
                    if first:
                        pe.wait_ge(y_mul, 16 * l + GROUPS)
                    else:
                        pe.wait_ge(z_ready, 16 * l + GROUPS + h)
                    blocks(par, bank(2), a_ops, range(8), True, False)
                    if not first:
                        turn(h - 1)
                    half(g + 1, 1)
                    blocks(par, bank(2), a_ops, range(8, 16), False, True).then_inc(weights_used, 1)
                    pe.wait_ge(q_l, 3 * (8 * l + h) + 3)
                    if first:
                        pe.wait_ge(kr_l, l + 1)
                    for qt in range(2):
                        s = slice(qt * P, (qt + 1) * P)
                        mm3(bank(5, qt * T), (qn_hi[:, s], qn_lo[:, s]), (kn_hi, kn_lo), True, False)
                        o = mm3(bank(5, qt * T), (qr_hi[:, s], qr_lo[:, s]), (kr_hi[:, :], kr_lo[:, :]),
                                False, True)
                    o.then_inc(s_ps, 1)
                    if not first:
                        attend(h - 1, second)

                head(0, True)
                head(1, False, True)
                with pe.Fori(2, HEADS - 1) as h:
                    head(h, False)
                if l == 0:
                    ada_sum(3)
                head(HEADS - 1, False)

                g = G + L_OUT
                half(g, 0)
                blocks(g % 2, bank(0), y_ops, range(8), True, False)
                half(g, 1)
                pe.wait_ge(y_l, 16 * l + 15)
                blocks(g % 2, bank(0), y_ops, range(8, 12), False, False)
                turn(HEADS - 1)
                blocks(g % 2, bank(0), y_ops, range(12, 15), False, False)
                attend(HEADS - 1)
                half(g + 1, 0)
                blocks((g + 1) % 2, bank(1), y_ops, range(8), True, False)
                pe.wait_ge(y_l, 16 * (l + 1))
                blocks(g % 2, bank(0), y_ops, range(15, 16), False, True).then_inc(weights_used, 1)
                half(g + 1, 1)
                blocks((g + 1) % 2, bank(1), y_ops, range(8, 16), False, True).then_inc(weights_used, 1)
                with pe.Fori(1, KT // 2) as i:
                    for b in range(2):
                        pe.wait_ge(g_tmp, 16 * l + 2 * i + b - 1)
                        chunk(g + 2 * i + b, (g + b) % 2, bank(b), y_ops)
                pe.wait_ge(r_acc, l + 1)
                pe.matmul(bank(6), ones[:, :], mu[:, :], start=True, stop=True).then_inc(ln_mean, 1)
                squares(2 * l + 1)
                if l == 0:
                    ada_sum(4)
                    for k in range(KT):
                        pe.wait_ge(x_new, k + 1)
                        o = pe.matmul(bank(6), ones[:, :], X[:, k * T:(k + 1) * T], start=k == 0, stop=k == KT - 1)
                    o.then_inc(ln_mean, 1)
                    squares(2)

            for k in range(KT):
                pe.wait_ge(x_sq, k // 2 + 1)
                o = pe.matmul(bank(6, T), ones[:, :], wide[:, k * T:(k + 1) * T], start=k == 0, stop=k == KT - 1)
            o.then_inc(x_stat, 1)

            def mix_tile(j, par, first):
                g = B2_MIX + MIX * j
                p0 = B2_MIX + par
                if first and par == 0:
                    pe.wait_ge(am_l, 1)
                    first_chunk(g, bank(0, 0, TM), am_ops, 2)
                else:
                    pe.wait_ge(cv_in, j)
                    chunk(g, p0 % 2, bank(0, 0, TM), am_ops)
                chunk(g + 1, (p0 + 1) % 2, bank(1, 0, TM), am_ops)
                if not (first and par == 0):
                    pe.wait_ge(pl_in, j)
                chunk(g + 2, p0 % 2, bank(2, 0, TM), am_ops)
                for b in range(2):
                    if not (first and par == 0):
                        pe.wait_ge(gt_tanh, 2 * j + b - 1)
                    chunk(g + 3 + b, (p0 + 1 + b) % 2, bank(3 + b), a_ops)

            for par in range(2):
                mix_tile(par, par, True)
            with pe.Fori(1, CONV // 2) as i:
                for par in range(2):
                    mix_tile(2 * i + par, par, False)
            half(B2_GRP, 0)
            half(B2_GRP, 1)
            pe.wait_ge(cv_in, CONV)
            pe.wait_ge(pl_l, CONV)
            for m in range(CONV):
                for k in range(2):
                    o = mm3(grp_ps(m), wb(B2_GRP % 2, 2 * m + k), y_ops(2 * (m // 2) + k), k == 0, k == 1)
            o.then_inc(weights_used, 1)
            for k in range(CONV):
                pe.wait_ge(cv_done, k + 1)
                o = pe.matmul(bank(6), ones[:, :], conv_out[:, k * T:(k + 1) * T], start=k == 0, stop=k == CONV - 1)
            o.then_inc(cm_ps, 1)

            def gate_b(i, b):
                g, g0 = B2_GATE + 4 * i + b, B2_GATE + b
                pe.wait_ge(gt_tanh, KT + 2 * i + b - 1)
                chunk(g, g0 % 2, bank(3 + b), a_ops)

            def pool_part(i, b, first):
                half(B2_GATE + 4 * i + 2 + b, 0)
                if first:
                    pe.wait_ge(gp_l, CONV)
                else:
                    pe.wait_ge(gt_done, 2 * i + b - 1)
                for k in range(CONV):
                    mm3(bank((0, 2)[b]), wb((B2_GATE + b) % 2, k), y_ops(CONV + k), k == 0, k == CONV - 1)

            def conv_part(i, b, first):
                half(B2_GATE + 4 * i + 2 + b, 1)
                if first:
                    pe.wait_ge(cn_l, CONV)
                for k in range(CONV):
                    o = mm3(bank((1, 5)[b]), wb((B2_GATE + b) % 2, CONV + k), y_ops(k), k == 0, k == CONV - 1)
                o.then_inc(weights_used, 1)

            gate_b(0, 0)
            pe.wait_ge(cm_fold, 1)
            pe.matmul(bank(6, T), ones[:, :], zs[:, :], start=True, stop=True).then_inc(cm_acc, 1)
            gate_b(0, 1)
            pool_part(0, 0, True)
            pool_part(0, 1, True)
            conv_part(0, 0, True)
            conv_part(0, 1, True)
            with pe.Fori(1, KT // 2) as i:
                for b in range(2):
                    gate_b(i, b)
                for b in range(2):
                    pool_part(i, b, False)
                    conv_part(i, b, False)
            pe.wait_ge(gt_done, KT)
            for k in range(KT):
                if k % 8 == 0:
                    half(B2_WO, k // 8)
                if k % 2 == 0:
                    pe.wait_ge(mm_l, k // 2 + 1)
                o = mm3(bank(0), wb(B2_WO % 2, k), a_ops(k), k == 0, k == KT - 1)
            o.then_inc(weights_used, 1)
            chunk(B2_WO + 1, (B2_WO + 1) % 2, bank(1), a_ops)
            with pe.Fori(1, KT // 2) as i:
                for b in range(2):
                    pe.wait_ge(wo_sq, 2 * i + b - 1)
                    chunk(B2_WO + 2 * i + b, (B2_WO + b) % 2, bank(b), a_ops)
            pe.wait_ge(wo_acc, KT)
            pe.matmul(bank(6), ones[:, :], mu[:, :], start=True, stop=True).then_inc(wo_stat, 1)

            def up(f, i, b, first):
                if not first:
                    pe.wait_ge(f_relu, 16 * f + 2 * i + b - 1)
                chunk(B2_FF + 32 * f + 2 * i + b, (B2_FF + b) % 2, bank(b), a_ops)

            def down(f, i, b, first):
                if not first:
                    pe.wait_ge(f_acc, 16 * f + 2 * i + b - 1)
                chunk(B2_FF + 32 * f + KT + 2 * i + b, (B2_FF + b) % 2, bank(2 + b), y_ops)

            for k in range(KT):
                if k % 8 == 0:
                    half(B2_FF, k // 8)
                pe.wait_ge(h_lo, k + 1)
                o = mm3(bank(0), wb(B2_FF % 2, k), a_ops(k), k == 0, k == KT - 1)
            o.then_inc(weights_used, 1)
            up(0, 0, 1, True)
            with pe.Fori(1, KT // 2) as i:
                for b in range(2):
                    up(0, i, b, False)
            pe.wait_ge(h_acc, KT)
            pe.matmul(bank(6, T), ones[:, :], mu[:, :], start=True, stop=True).then_inc(h_stat, 1)
            pe.wait_ge(f_lo, 16)
            for b in range(2):
                down(0, 0, b, True)
            with pe.Fori(1, KT // 2) as i:
                for b in range(2):
                    down(0, i, b, False)
            with pe.Fori(1, FF_BLOCKS) as f:
                with pe.Fori(0, KT // 2) as i:
                    for b in range(2):
                        up(f, i, b, False)
                with pe.Fori(0, KT // 2) as i:
                    pe.wait_ge(f_lo, 16 * f + 16)
                    for b in range(2):
                        down(f, i, b, False)
            for i in range(KT // 2):
                pe.wait_ge(f_osq, i + 1)
                for j in range(2):
                    at = (i % 2) * 2 * T + j * T
                    o = pe.matmul(bank(6), ones[:, :], sc[:, at:at + T],
                                  start=i + j == 0, stop=i == KT // 2 - 1 and j == 1)
                o.then_inc(f_osum, 1)

        @block.scalar
        def _(ac):
            def split(g, par, dft=False):
                ac.wait_ge(landed[par], 8 * (g - par) + 16)
                if not (isinstance(g, int) and g < 2):
                    ac.wait_ge(weights_used, g - 1)
                n = HALF // 2 if dft else HALF
                for h in range(2):
                    to = dft_hi[:, h * n:(h + 1) * n] if dft else w_hi[:, par * CH + h * n:par * CH + (h + 1) * n]
                    ac.copy(to, raw[:, bass.ds((g % RAW) * CH + h * n, n)]).then_inc(hi_ready, 1)

            def after(g, base):
                split(g + 2, base % 2)

            def rstd(name, n=T, at=0):
                ac.wait_ge(ln_var, NORM[name] + 1)
                ac.activation(rs[:, at:at + n], rs[:, at:at + n], ACT.Sqrt).then_inc(ln_std, 1)

            def square_x(n):
                for i in range(KT // 2):
                    ac.wait_ge(ln_cent, 8 * n + i + 1)
                    if i >= 2:
                        ac.wait_ge(ln_acc, 8 * n + i - 1)
                    ac.activation(sc[:, (i % 2) * 2 * T:(i % 2 + 1) * 2 * T], X[:, 2 * i * T:(2 * i + 2) * T],
                                  ACT.Square).then_inc(ln_sq, 1)

            def modulated(l, i):
                ac.wait_ge(in_norm, i + 1)
                for j in range(2):
                    m = 2 * i + j
                    s = sc[:, (m % 4) * T:(m % 4 + 1) * T]
                    ac.activation(s, s, ACT.Identity, scale=mod[:, (3 * l + 1) * KT + m:(3 * l + 1) * KT + m + 1],
                                  bias=mod[:, 3 * l * KT + m:3 * l * KT + m + 1]).then_inc(ln_y, 1)
                input_hi(l, i)

            def input_hi(n, i):
                ac.wait_ge(ln_y, KT * n + 2 * i + 2)
                ac.copy(two_tiles(a_hi, i), sc[:, (i % 2) * 2 * T:(i % 2 + 1) * 2 * T]
                        .rearrange("p (k t) -> p k t", k=2)).then_inc(ln_hi, 1)

            ac.wait_ge(vec_in, 16)
            ac.activation(csil[:, 0:KT], v("c", 0, KT), ACT.Tanh, scale=0.5).then_inc(c_tanh, 1)

            def take_row(r):
                ac.wait_ge(ada0_used, 4 * r + 4)
                if r:
                    ac.wait_ge(col_ps, r)
                ac.copy(row[0:1, :], ps[0:1, (1 + r % 2) * 512:(2 + r % 2) * 512]).then_inc(row_in, 1)

            take_row(0)
            square_x(0)
            take_row(1)
            rstd("pre0")
            rstd("meta", META, T)
            ac.wait_ge(am_y, 1)
            ac.copy(a_hi[:, :].rearrange("p (k t) -> p k t", k=KT)[:, :, 0:META],
                    mt[:, :].rearrange("p (k t) -> p k t", k=KT)).then_inc(am_h, 1)
            ac.wait_ge(rope_arg, 1)
            ac.activation(rope[:, :], zs[:, :], ACT.Sin).then_inc(rope_sin, 1)
            split(0, 0)
            split(1, 1)
            for r in range(2, ADA0 // 4 + 2, 2):
                for q in (r, r + 1):
                    if q == r + 1:
                        for i in (r - 2, r - 1):
                            input_hi(0, i)
                    if q < ADA0 // 4:
                        take_row(q)

            for l in range(DEPTH):
                G = l * PER_LAYER
                for m in range(LAT):
                    ac.wait_ge(weights_used, G + m + 1)
                    if m < QT + CT:
                        if m:
                            ac.wait_ge(lat_acc, 6 * l + m)
                        ac.activation(sc[:, 2 * T:3 * T], lat_ps(m),
                                      ACT.Square).then_inc(lat_sq, 1)
                    split(G + m + 2, (G + m) % 2, dft=m + 2 == L_DFT)
                ac.wait_ge(weights_used, G + L_DFT + 1)
                after(G + L_DFT, G + L_DFT)
                ac.wait_ge(weights_used, G + L_FMIX + 1)

                def cw(j):
                    b, trig, g4 = (0, 1, 2, 7)[j], j // 2, j % 2
                    to = cw_hi[:, g4 * 4 * T:(g4 + 1) * 4 * T].rearrange("p (g c) -> p g c", g=4)
                    ac.copy(to[:, :, trig * P:(trig + 1) * P],
                            bank(b, 0, 512).rearrange("p (g c) -> p g c", g=4)).then_inc(cw_h, 1)

                cw(0)
                cw(1)
                after(G + L_FMIX, G + L_FMIX)
                cw(2)
                cw(3)
                rstd(f"lat{l}", 2 * T)
                def y_part(t):
                    ac.wait_ge(y_mul, 16 * l + t + 1)
                    ac.copy(y_hi[:, bass.ds(t * T, T)], sc[:, 2 * T:3 * T]).then_inc(y_h, 1)

                def group(q, first):
                    g, g0 = G + L_FOUR + 2 * q, G + L_FOUR
                    ac.wait_ge(weights_used, g + 1)
                    ac.copy(u_hi, bank(0)).then_inc(u_h, 1)
                    after(g, g0)
                    if not first:
                        y_part(q - 1)
                    ac.wait_ge(weights_used, g + 2)
                    ac.activation(th[:, 0:T], bank(1), ACT.Tanh, scale=0.5).then_inc(z_tanh, 1)
                    after(g + 1, g0 + 1)
                    ac.wait_ge(t_ps, 8 * l + q + 1)
                    ac.copy(t_hi, bank(3, 0, 2 * T)).then_inc(t_h, 1)

                group(0, True)
                with ac.Fori(1, GROUPS // 2 + 1) as q:
                    group(q, False)

                def latents(tiles_):
                    for m in tiles_:
                        ac.wait_ge(lat_y, 6 * l + m + 1)
                        ac.copy(lat_hi[:, m * T:(m + 1) * T], sc[:, (m % 2) * T:(m % 2 + 1) * T]).then_inc(lat_h, 1)

                latents(range(3))
                group(GROUPS // 2 + 1, False)
                latents(range(3, QT + CT))
                with ac.Fori(GROUPS // 2 + 2, GROUPS) as q:
                    group(q, False)
                ac.wait_ge(kr_sum, l + 1)
                ac.copy(kr_hi[:, :], bank(4)).then_inc(kr_h, 1)
                y_part(GROUPS - 1)

                def turned(h):
                    ac.wait_ge(pt_ps, 8 * l + h + 1)
                    ac.copy(pt_hi, bank(3, 0, 2 * T)).then_inc(pt_h, 1)

                def head(h, first):
                    g, g0 = G + L_HEAD + 2 * h, G + L_HEAD
                    ac.wait_ge(weights_used, g + 1)
                    ac.copy(qn_hi, bank(0)).then_inc(q_h, 1)
                    ac.copy(kn_hi, bank(1)).then_inc(q_h, 1)
                    ac.wait_ge(qr_rot, 8 * l + h + 1)
                    ac.copy(qr_hi, sc[:, 3 * T:4 * T]).then_inc(q_h, 1)
                    after(g, g0)
                    if not first:
                        turned(h - 1)
                    ac.wait_ge(weights_used, g + 2)
                    if not first:
                        ac.wait_ge(z_ready, 16 * l + GROUPS + h)
                    ac.activation(th[:, 0:T], bank(2), ACT.Tanh, scale=0.5).then_inc(z_tanh, 1)
                    if not first:
                        ac.wait_ge(o_ps, 8 * l + h)
                    ac.wait_ge(q_l, 3 * (8 * l + h) + 2)
                    ac.copy(vv_hi, bank(1, T)).then_inc(v_h, 1)
                    after(g + 1, g0 + 1)
                    if not first:
                        y_part(GROUPS + h - 1)
                    ac.wait_ge(s_max, 8 * l + h + 1)
                    for qt in range(2):
                        ac.activation(sc[:, qt * T:(qt + 1) * T], bank(5, qt * T), ACT.Exp,
                                      bias=stat[:, 2 + qt:3 + qt], scale=SM_SCALE,
                                      accum_out=stat[:, 4 + qt:5 + qt]).then_inc(s_exp, 1)
                    ac.wait_ge(s_sum, 8 * l + h + 1)
                    for qt in range(2):
                        s = sc[:, qt * T:(qt + 1) * T]
                        ac.mul(s, s, stat[:, 6 + qt:7 + qt]).then_inc(p_ready, 1)

                head(0, True)
                with ac.Fori(1, HEADS) as h:
                    head(h, False)

                def out_tile(i, b, first):
                    g = G + L_OUT
                    m = 2 * i + b
                    ac.wait_ge(weights_used, m + (g + 1))
                    if not first:
                        ac.wait_ge(g_mul, m + (16 * l - 1))
                    ac.activation(sc[:, b * T:(b + 1) * T], bank(b), ACT.Copy,
                                  scale=mod[:, bass.ds(m + (3 * l + 2) * KT, 1)]).then_inc(g_tmp, 1)
                    after(m + g, g + b)

                turned(HEADS - 1)
                y_part(2 * HEADS - 1)
                ac.wait_ge(mod_ready, 3 * l + 1)
                for b in range(2):
                    out_tile(0, b, True)
                with ac.Fori(1, KT // 2) as i:
                    for b in range(2):
                        out_tile(i, b, False)
                square_x(2 * l + 1)
                rstd(f"post{l}")
                for m in range(KT):
                    ac.wait_ge(ln_app, 8 * l + m // 2 + 1)
                    ac.activation(X[:, m * T:(m + 1) * T], sc[:, (m % 4) * T:(m % 4 + 1) * T], ACT.Identity,
                                  scale=v("ln_g", l * KT + m), bias=v("ln_b", l * KT + m)).then_inc(x_new, 1)
                if l == 0:
                    square_x(2)
                    rstd("pre1")
                    ac.wait_ge(mod_ready, 3)
                    for i in range(KT // 2):
                        modulated(1, i)

            rstd("mix")
            for m in range(KT):
                ac.wait_ge(mix_norm, m // 2 + 1)
                ac.activation(a_tile(a_hi, m), sc[:, (m % 4) * T:(m % 4 + 1) * T], ACT.Copy,
                              scale=v("g_pre_mix", m)).then_inc(mix_hi, 1)
            def mix_tile(j, par, first):
                g, p0 = B2_MIX + MIX * j, B2_MIX + par
                ac.wait_ge(weights_used, g + 1)
                after(g, p0)
                ac.wait_ge(weights_used, g + 2)
                ac.activation(th[:, :], bank(1, 0, TM), ACT.Tanh, scale=0.5).then_inc(cv_tanh, 1)
                after(g + 1, p0 + 1)
                ac.wait_ge(weights_used, g + 3)
                if not first:
                    ac.wait_ge(pl_sum, j)
                ac.copy(pool_z, bank(2, 0, TM)).then_inc(pl_in, 1)
                after(g + 2, p0)
                for b in range(2):
                    ac.wait_ge(weights_used, g + 4 + b)
                    ac.activation(wide[:, bass.ds((2 * j + b) * T, T)], bank(3 + b), ACT.Tanh, scale=0.5)\
                        .then_inc(gt_tanh, 1)
                    if b == 0:
                        after(g + 3, p0 + 1)
                        ac.wait_ge(pl_sum, j + 1)
                        ac.copy(y_hi[:, bass.ds(j * T, T)], zs[:, :]).then_inc(pl_h, 1)
                    else:
                        after(g + 4, p0)

            mix_tile(0, 0, True)
            mix_tile(1, 1, False)
            with ac.Fori(1, CONV // 2) as i:
                for par in range(2):
                    mix_tile(2 * i + par, par, False)
            ac.wait_ge(weights_used, B2_GRP + 1)
            for i, m in enumerate((0, 2, 4, 6, 1, 3, 5, 7)):
                if m % 2:
                    ac.wait_ge(gp_l, i - 3)
                ac.activation(y_hi[:, (CONV + m) * T:(CONV + m + 1) * T], grp_ps(m), ACT.Copy,
                              scale=v("pool_scale", m)).then_inc(gp_h, 1)
            after(B2_GRP, B2_GRP)
            for i in range(CONV // 2):
                ac.wait_ge(cm_cent, i + 1)
                if i >= 2:
                    ac.wait_ge(cm_sum, i - 1)
                ac.activation(sc[:, (i % 2) * 2 * T:(i % 2 + 1) * 2 * T], conv_out[:, 2 * i * T:(2 * i + 2) * T],
                              ACT.Square).then_inc(cm_sq, 1)

            def gate_b(i, b, first=False):
                g, g0 = B2_GATE + 4 * i + b, B2_GATE + b
                ac.wait_ge(weights_used, g + 1)
                if not first:
                    ac.wait_ge(gt_done, 2 * i)
                ac.activation(sc[:, b * T:(b + 1) * T], bank(3 + b), ACT.Tanh, scale=0.5).then_inc(gt_tanh, 1)
                after(g, g0)

            def branches(i, b):
                g, g0 = B2_GATE + 4 * i + 2 + b, B2_GATE + b
                ac.wait_ge(weights_used, g + 1)
                after(g, g0)

            ac.wait_ge(cm_fold, 1)
            gate_b(0, 0, True)
            rstd("conv")
            for k in range(CONV + 2):
                if k < CONV:
                    ac.wait_ge(cn_y, k + 1)
                    ac.activation(cn_buf(k), conv_out[:, k * T:(k + 1) * T], ACT.Tanh, scale=0.5).then_inc(cn_tanh, 1)
                if k >= 2:
                    ac.wait_ge(cn_mul, k - 1)
                    ac.activation(y_hi[:, (k - 2) * T:(k - 1) * T], conv_out[:, (k - 2) * T:(k - 1) * T],
                                  ACT.Copy, scale=0.5).then_inc(cn_h, 1)
                if k == 3:
                    gate_b(0, 1, True)
            branches(0, 0)
            branches(0, 1)
            with ac.Fori(1, KT // 2 - 1) as i:
                for b in range(2):
                    gate_b(i, b)
                for b in range(2):
                    branches(i, b)
            last = KT // 2 - 1
            for b in range(2):
                gate_b(last, b)
            for i in range(KT // 2):
                if i == 3:
                    branches(last, 0)
                if i == last:
                    branches(last, 1)
                ac.wait_ge(gt_done, 2 * i + 2)
                to = a_hi[:, i * 2 * TM:(i + 1) * 2 * TM].rearrange("p (k t) -> p k t", k=2)[:, :, META:TM]
                ac.activation(to, wide[:, i * 2 * T:(i + 1) * 2 * T].rearrange("p (k t) -> p k t", k=2),
                              ACT.Copy, scale=0.5).then_inc(mm_h, 1)

            def wo_tile(i, b, first):
                m = 2 * i + b
                ac.wait_ge(weights_used, m + (B2_WO + 1))
                ac.activation(wide[:, bass.ds(m * T, T)], bank(b), ACT.Copy, scale=v("g_post_mix", m))\
                    .then_inc(wo_out, 1)
                if not first:
                    ac.wait_ge(wo_acc, m - 1)
                ac.activation(sc[:, b * T:(b + 1) * T], bank(b), ACT.Square).then_inc(wo_sq, 1)
                after(m + B2_WO, B2_WO + b)

            for b in range(2):
                wo_tile(0, b, True)
            with ac.Fori(1, KT // 2) as i:
                for b in range(2):
                    wo_tile(i, b, False)
            rstd("wo")
            for m in range(KT):
                ac.wait_ge(h_new, m // 2 + 1)
                ac.activation(a_tile(a_hi, m), X[:, m * T:(m + 1) * T], ACT.Copy,
                              scale=v("g_pre_mlp", m)).then_inc(h_hi, 1)

            def up(f, i, b, first):
                m = 16 * f + 2 * i + b
                g = B2_FF + 32 * f + 2 * i + b
                ac.wait_ge(weights_used, g + 1)
                if not first:
                    ac.wait_ge(f_lo, m - 1)
                ac.activation(sc[:, b * T:(b + 1) * T], bank(b), ACT.Relu).then_inc(f_relu, 1)
                ac.wait_ge(f_relu, m + 1)
                ac.activation(y_hi[:, bass.ds((2 * i + b) * T, T)], sc[:, b * T:(b + 1) * T], ACT.Square)\
                    .then_inc(f_hi, 1)
                after(g, B2_FF + b)

            def square_h(m, b, first):
                if not first:
                    ac.wait_ge(h_acc, m - 1)
                ac.activation((zs[:, :], th[:, 0:T])[b], X[:, bass.ds(m * T, T)], ACT.Square).then_inc(h_sq, 1)

            for b in range(2):
                up(0, 0, b, True)
                square_h(b, b, True)
            with ac.Fori(1, KT // 2) as i:
                for b in range(2):
                    up(0, i, b, False)
                    square_h(2 * i + b, b, False)
            with ac.Fori(0, KT // 2) as i:
                for b in range(2):
                    g = B2_FF + KT + 2 * i + b
                    ac.wait_ge(weights_used, g + 1)
                    after(g, B2_FF + b)
            with ac.Fori(1, FF_BLOCKS - 1) as f:
                with ac.Fori(0, KT // 2) as i:
                    for b in range(2):
                        up(f, i, b, False)
                with ac.Fori(0, KT // 2) as i:
                    for b in range(2):
                        g = B2_FF + KT + 32 * f + 2 * i + b
                        ac.wait_ge(weights_used, g + 1)
                        after(g, B2_FF + b)
            f = FF_BLOCKS - 1
            with ac.Fori(0, KT // 2) as i:
                for b in range(2):
                    up(f, i, b, False)
            with ac.Fori(0, KT // 2 - 1) as i:
                for b in range(2):
                    g = B2_FF + KT + 32 * f + 2 * i + b
                    ac.wait_ge(weights_used, g + 1)
                    after(g, B2_FF + b)
            for i in range(KT // 2):
                ac.wait_ge(f_acc, 16 * (FF_BLOCKS - 1) + 2 * i + 2)
                if i >= 2:
                    ac.wait_ge(f_osum, i - 1)
                ac.activation(sc[:, (i % 2) * 2 * T:(i % 2 + 1) * 2 * T], wide[:, 2 * i * T:(2 * i + 2) * T],
                              ACT.Square).then_inc(f_osq, 1)
            ac.wait_ge(ln_var, NORM["out"] + 1)
            ac.activation(rs[:, T:2 * T], rs[:, T:2 * T], ACT.Sqrt).then_inc(ln_std, 1)

        @block.vector
        def _(ve):
            own = Chain(ve, dve)

            def split(g, par, dft=False, halves=range(2)):
                n = HALF // 2 if dft else HALF
                for h in halves:
                    ve.wait_ge(hi_ready, 2 * g + h + 1)
                    if dft:
                        to, hi = dft_lo[:, h * n:(h + 1) * n], dft_hi[:, h * n:(h + 1) * n]
                    else:
                        s = slice(par * CH + h * n, par * CH + (h + 1) * n)
                        to, hi = w_lo[:, s], w_hi[:, s]
                    ve.tensor_tensor(to, raw[:, bass.ds((g % RAW) * CH + h * n, n)], hi.bitcast(F32),
                                     ALU.subtract).then_inc(lo_ready, 1)

            def after(g, base):
                split(g + 2, base % 2)

            def sub_hi(out_, exact, hi):
                return ve.tensor_tensor(out_, exact, hi.bitcast(F32), ALU.subtract)

            def over_tokens(t, k):
                return t.unsqueeze(1).to_broadcast([P, k, T])

            def tiles(t, k):
                return t.rearrange("p (k t) -> p k t", k=k)

            def add_ada(a, par):
                ve.wait_ge(ada_landed[par], 8 * (a - par) + (16 - 8 * ADA0))
                if not (isinstance(a, int) and a == ADA0):
                    ve.wait_ge(ada_step, a - ADA0)
                ve.scalar_tensor_tensor(out=ada_acc, in0=ada_ring[:, par * CH:(par + 1) * CH],
                                        scalar=csil[:, bass.ds(KT + a % KT, 1)], in1=ada_acc,
                                        op0=ALU.mult, op1=ALU.add).then_inc(ada_step, 1)

            def clear_ada(r):
                if r > 2:
                    ve.wait_ge(ada_summed, r - 2)
                ve.memset(ada_acc, 0.0).then_inc(ada_clear, 1)
                ve.wait_ge(ada_clear, r - 1)

            def read_mod(r):
                ve.wait_ge(ada_summed, r - 1)
                ve.scalar_tensor_tensor(out=mod[:, r * KT:(r + 1) * KT], in0=bank(7, 0, KT),
                                        scalar=1.0 if r % 3 == 1 else 0.0, in1=v("b_ada", r * KT, KT),
                                        op0=ALU.add, op1=ALU.add).then_inc(mod_ready, 1)
                if r + 1 < 3 * DEPTH:
                    clear_ada(r + 1)

            def rstd(name, parts, eps):
                for part, total, count in parts:
                    o = ve.tensor_scalar(part, total, 1.0 / count, eps, ALU.mult, ALU.add)
                    if part is not parts[-1][0]:
                        own.link(o)
                o.then_inc(ln_var, 1)
                ve.wait_ge(ln_std, NORM[name] + 1)
                whole = rs[:, 0:T * len(parts)] if name != "meta" else parts[0][0]
                own.link(ve.reciprocal(whole, whole))

            def centre(n):
                ve.wait_ge(ln_mean, n + 1)
                own.link(ve.tensor_scalar(mu[:, :], bank(6), 1.0 / D, None, ALU.mult))
                for i in range(KT // 2):
                    s = X[:, 2 * i * T:(2 * i + 2) * T]
                    ve.tensor_tensor(tiles(s, 2), tiles(s, 2), over_tokens(mu[:, :], 2), ALU.subtract)\
                        .then_inc(ln_cent, 1)
                ve.wait_ge(ln_acc, 8 * (n + 1))

            def normed(i):
                return ve.tensor_tensor(tiles(sc[:, (i % 2) * 2 * T:(i % 2 + 1) * 2 * T], 2),
                                        tiles(X[:, i * 2 * T:(i + 1) * 2 * T], 2), over_tokens(rs[:, 0:T], 2),
                                        ALU.mult)

            def split_input(l, make):
                def finish(i):
                    ve.wait_ge(ln_hi, 8 * l + i + 1)
                    ve.wait_ge(ln_y, KT * l + 2 * i + 2)
                    sub_hi(two_tiles(a_lo, i), tiles(sc[:, (i % 2) * 2 * T:(i % 2 + 1) * 2 * T], 2),
                           two_tiles(a_hi, i)).then_inc(ln_lo, 1)

                for i in range(KT // 2):
                    if i >= 2:
                        ve.wait_ge(ln_lo, 8 * l + i - 1)
                    make(i)
                    if i:
                        finish(i - 1)
                finish(KT // 2 - 1)

            ve.memset(ones[:, :], 1.0).then_inc(ones_set, 1)
            ve.wait_ge(c_tanh, 1)
            own.link(ve.scalar_tensor_tensor(out=csil[:, KT:2 * KT], in0=csil[:, 0:KT], scalar=1.0,
                                             in1=v("c", 0, KT), op0=ALU.add, op1=ALU.mult))
            ve.tensor_scalar(csil[:, KT:2 * KT], csil[:, KT:2 * KT], 0.5, None, ALU.mult).then_inc(c_ready, 1)
            ve.wait_ge(c_ready, 1)

            def fold_row(r):
                for s in (1, 3):
                    ve.wait_ge(ada0_landed[s], 16 * r + 16)
                    w, c = ada0_slot(s), KT + 4 * s
                    own.link(ve.tensor_scalar(w[:, 0:512], w[:, 0:512], csil[:, c:c + 1], None, ALU.mult))
                    ve.scalar_tensor_tensor(out=w[:, 512:1024], in0=w[:, 512:1024], scalar=csil[:, c + 1:c + 2],
                                            in1=w[:, 0:512], op0=ALU.mult, op1=ALU.add).then_inc(ada0_fold, 1)

            ve.wait_ge(x_in, 16)
            for i in range(1, KT // 2):
                own.link(ve.tensor_tensor(sc[:, 0:2 * T], X[:, 0:2 * T] if i == 1 else sc[:, 0:2 * T],
                                          X[:, 2 * i * T:(2 * i + 2) * T], ALU.add))
            ve.tensor_tensor(mu[:, :], sc[:, 0:T], sc[:, T:2 * T], ALU.add).then_inc(x_sum, 1)
            ve.wait_ge(ln_mean, 1)
            own.link(ve.tensor_scalar(mu[:, :], bank(6), 1.0 / D, None, ALU.mult))

            def add_square(i, acc, squares_sem, acc_sem):
                ve.wait_ge(squares_sem, i + 1)
                sq = sc[:, (i % 2) * 2 * T:(i % 2 + 1) * 2 * T]
                if i:
                    ve.wait_ge(acc_sem, i)
                    ve.tensor_tensor(acc, acc, sq, ALU.add).then_inc(acc_sem, 1)
                else:
                    ve.tensor_copy(acc, sq).then_inc(acc_sem, 1)

            for i in range(KT // 2):
                s = X[:, 2 * i * T:(2 * i + 2) * T]
                ve.tensor_tensor(tiles(s, 2), tiles(s, 2), over_tokens(mu[:, :], 2), ALU.subtract)\
                    .then_inc(ln_cent, 1)
                if i:
                    add_square(i - 1, rs[:, :], ln_sq, ln_acc)
            add_square(KT // 2 - 1, rs[:, :], ln_sq, ln_acc)
            ve.wait_ge(ln_acc, 8)
            ve.tensor_tensor(sc[:, 0:T], rs[:, 0:T], rs[:, T:2 * T], ALU.add).then_inc(x_fold, 1)
            ve.wait_ge(small, SMALL)
            ve.wait_ge(x_fold, 1)
            own.link(ve.tensor_tensor(sc[:, 2 * T:2 * T + KT * META], mt[:, :], mt[:, :], ALU.mult))
            ve.tensor_reduce(zs[:, 0:META], sc[:, 2 * T:2 * T + KT * META].rearrange("p (k t) -> p t k", k=KT),
                             AX.X, ALU.add).then_inc(m_sq, 1)
            ve.wait_ge(x_stat, 1)
            rstd("pre0", [(rs[:, 0:T], bank(6, T), D)], 1e-6)
            ve.wait_ge(m_acc, 1)
            rstd("meta", [(rs[:, T:T + META], bank(5, 0, META), D)], 1e-6)
            own.link(ve.tensor_tensor(mt[:, :].rearrange("p (k t) -> p k t", k=KT),
                                      mt[:, :].rearrange("p (k t) -> p k t", k=KT),
                                      rs[:, T:T + META].unsqueeze(1).to_broadcast([P, KT, META]), ALU.mult))
            ve.tensor_tensor(mt[:, :].rearrange("p (k t) -> p k t", k=KT),
                             mt[:, :].rearrange("p (k t) -> p k t", k=KT),
                             v("g_pre_mix", 0, KT).unsqueeze(2).to_broadcast([P, KT, META]), ALU.mult)\
                .then_inc(am_y, 1)
            two_pi = 2.0 * np.pi
            c1 = float(np.float32(6.28125))
            c2 = float(np.round((two_pi - c1) * 2.0 ** 17) / 2.0 ** 17)
            c3 = float(np.float32(two_pi - c1 - c2))
            freq, phase, sign = (con[:, 2 * P + i:2 * P + i + 1] for i in range(3))
            magic = 1.5 * 2.0 ** 23
            ang, turns_ = zs, mu
            own.link(ve.tensor_copy(ang[:, :], pos))
            own.link(ve.tensor_scalar(ang[:, :], ang[:, :], freq, None, ALU.mult))
            own.link(ve.tensor_scalar(sc[:, T:2 * T], ang[:, :], phase, 1.0 / two_pi, ALU.add, ALU.mult))
            own.link(ve.tensor_scalar(turns_[:, :], sc[:, T:2 * T], magic, None, ALU.add))
            own.link(ve.tensor_scalar(turns_[:, :], turns_[:, :], magic, None, ALU.subtract))
            for c in (c1, c2, c3):
                own.link(ve.scalar_tensor_tensor(out=ang[:, :], in0=turns_[:, :], scalar=-c, in1=ang[:, :],
                                                 op0=ALU.mult, op1=ALU.add))
            own.link(ve.tensor_scalar(ang[:, :], ang[:, :], phase, None, ALU.add))
            ve.tensor_scalar(ang[:, :], ang[:, :], float(np.float32(3.1415925)), float(np.float32(-3.1415925)),
                             ALU.min, ALU.max).then_inc(rope_arg, 1)
            ve.wait_ge(rope_sin, 1)
            own.link(ve.tensor_scalar(rope[:, :], rope[:, :], sign, None, ALU.mult))
            ve.wait_ge(am_h, 1)
            lo3, hi3 = (t[:, :].rearrange("p (k t) -> p k t", k=KT)[:, :, 0:META] for t in (a_lo, a_hi))
            sub_hi(lo3, mt[:, :].rearrange("p (k t) -> p k t", k=KT), hi3).then_inc(am_l, 1)
            split(0, 0)
            split(1, 1)

            def read_mod0(i):
                if FOLDED <= i + 2 < ADA0 // 4:
                    fold_row(i + 2)
                if i % 2:
                    return
                ve.wait_ge(col_ps, i + 2)
                for third in range(2):
                    ve_mod = mod[:, KT * third + 2 * i:KT * third + 2 * i + 4]
                    o = ve.scalar_tensor_tensor(out=ve_mod, in0=bank((3, 7)[i // 2 % 2], 4 * third, 4),
                                                scalar=float(third), in1=v("b_ada", KT * third + 2 * i, 4),
                                                op0=ALU.add, op1=ALU.add)
                o.then_inc(col_in, 1)
                ve.wait_ge(col_in, i // 2 + 1)

            def modulate(i):
                read_mod0(i)
                own.link(normed(i))
                for m in (2 * i, 2 * i + 1):
                    b = sc[:, (m % 4) * T:(m % 4 + 1) * T]
                    ve.tensor_scalar(b, b, mod[:, KT + m:KT + m + 1], mod[:, m:m + 1], ALU.mult, ALU.add)\
                        .then_inc(ln_y, 1)

            split_input(0, modulate)
            ve.wait_ge(ada0_used, ADA0)
            clear_ada(2)

            for l in range(DEPTH):
                G = l * PER_LAYER
                A = (2 + 3 * l) * KT
                for m in range(LAT):
                    if m < QT + CT:
                        ve.wait_ge(lat_sq, 6 * l + m + 1)
                        acc = sc[:, 0:T] if m < QT else sc[:, T:2 * T]
                        if m:
                            ve.wait_ge(lat_acc, 6 * l + m)
                        if m in (0, QT):
                            ve.tensor_copy(acc, sc[:, 2 * T:3 * T]).then_inc(lat_acc, 1)
                        else:
                            ve.tensor_tensor(acc, acc, sc[:, 2 * T:3 * T], ALU.add).then_inc(lat_acc, 1)
                    else:
                        ve.wait_ge(weights_used, G + m + 1)
                        ve.tensor_tensor(sc[:, 3 * T:4 * T], bank(7), rope[:, :], ALU.mult).then_inc(kr_rot, 1)
                    split(G + m + 2, (G + m) % 2, dft=m + 2 == L_DFT)
                    add_ada(A + m, (A + m) % 2)
                after(G + L_DFT, G + L_DFT)
                ve.wait_ge(lat_stat, l + 1)
                rs_parts = [(rs[:, 0:T], bank(3), QT * P), (rs[:, T:2 * T], bank(3, T), CT * P)]

                def cw(j):
                    b, trig, g4 = (0, 1, 2, 7)[j], j // 2, j % 2
                    to, hi = (t[:, g4 * 4 * T:(g4 + 1) * 4 * T].rearrange("p (g c) -> p g c", g=4)
                              [:, :, trig * P:(trig + 1) * P] for t in (cw_lo, cw_hi))
                    ve.wait_ge(cw_h, 4 * l + j + 1)
                    sub_hi(to, bank(b, 0, 512).rearrange("p (g c) -> p g c", g=4), hi).then_inc(cw_l, 1)

                cw(0)
                cw(1)
                after(G + L_FMIX, G + L_FMIX)
                cw(2)
                cw(3)
                for (part, total, count), o in zip(rs_parts, (own.link, lambda ins: ins.then_inc(ln_var, 1))):
                    o(ve.tensor_scalar(part, total, 1.0 / count, 1e-6, ALU.mult, ALU.add))

                def latents(tiles_):
                    if tiles_[0] == 0:
                        ve.wait_ge(ln_std, NORM[f"lat{l}"] + 1)
                        own.link(ve.reciprocal(rs[:, :], rs[:, :]))
                    for m in (*tiles_, None):
                        if m is not None:
                            gain = v("q_norm", l * QT + m) if m < QT else v("kv_norm", l * CT + m - QT)
                            row_ = rs[:, 0:T] if m < QT else rs[:, T:2 * T]
                            if m >= 2:
                                ve.wait_ge(lat_l, 6 * l + m - 1)
                            ve.scalar_tensor_tensor(out=sc[:, (m % 2) * T:(m % 2 + 1) * T], in0=lat_ps(m),
                                                    scalar=gain, in1=row_, op0=ALU.mult, op1=ALU.mult)\
                                .then_inc(lat_y, 1)
                        if m != tiles_[0]:
                            n = tiles_[-1] if m is None else m - 1
                            ve.wait_ge(lat_h, 6 * l + n + 1)
                            s = slice(n * T, (n + 1) * T)
                            sub_hi(lat_lo[:, s], sc[:, (n % 2) * T:(n % 2 + 1) * T], lat_hi[:, s])\
                                .then_inc(lat_l, 1)

                def y_tile(t, o):
                    ve.scalar_tensor_tensor(out=sc[:, 2 * T:3 * T], in0=o, scalar=0.5, in1=zs[:, :],
                                            op0=ALU.mult, op1=ALU.mult).then_inc(y_mul, 1)

                def y_rest(t):
                    ve.wait_ge(y_h, 16 * l + t + 1)
                    sub_hi(y_lo[:, bass.ds(t * T, T)], sc[:, 2 * T:3 * T], y_hi[:, bass.ds(t * T, T)])\
                        .then_inc(y_l, 1)

                def gate(t, b):
                    ve.wait_ge(z_tanh, 16 * l + t + 1)
                    ve.scalar_tensor_tensor(out=zs[:, :], in0=th[:, 0:T], scalar=1.0, in1=bank(b),
                                            op0=ALU.add, op1=ALU.mult).then_inc(z_ready, 1)

                def after_ada(g, base, a, par, with_ada):
                    if with_ada:
                        add_ada(a, par)
                    after(g, base)

                def group(q, first, adds=2, late=False):
                    a0 = A + (GROUPS - 4 if late else LAT)
                    a = 2 * q + a0
                    g, g0 = G + L_FOUR + 2 * q, G + L_FOUR
                    ve.wait_ge(u_h, 8 * l + q + 1)
                    sub_hi(u_lo, bank(0), u_hi).then_inc(u_l, 1)
                    after_ada(g, g0, a, a0 % 2, adds > 0)
                    if not first:
                        ve.wait_ge(yf_ps, 8 * l + q)
                        ve.wait_ge(z_ready, 16 * l + q)
                        y_tile(q - 1, bank(2))
                        y_rest(q - 1)
                    gate(q, 1)
                    after_ada(g + 1, g0 + 1, a + 1, (a0 + 1) % 2, adds > 1)
                    ve.wait_ge(t_h, 8 * l + q + 1)
                    sub_hi(t_lo, bank(3, 0, 2 * T), t_hi).then_inc(t_l, 1)

                group(0, True)
                with ve.Fori(1, GROUPS // 2) as q:
                    group(q, False)
                group(GROUPS // 2, False, 1)
                latents(range(3))
                read_mod(3 * l + 2)
                group(GROUPS // 2 + 1, False, 0)
                latents(range(3, QT + CT))
                with ve.Fori(GROUPS // 2 + 2, GROUPS) as q:
                    group(q, False, 2 if l == 0 else 0, late=True)
                ve.wait_ge(kr_h, l + 1)
                sub_hi(kr_lo[:, :], bank(4), kr_hi[:, :]).then_inc(kr_l, 1)
                ve.wait_ge(yf_ps, 8 * (l + 1))
                ve.wait_ge(z_ready, 16 * l + GROUPS)
                y_tile(GROUPS - 1, bank(2))
                y_rest(GROUPS - 1)

                def turned(h):
                    ve.wait_ge(pt_h, 8 * l + h + 1)
                    sub_hi(pt_lo, bank(3, 0, 2 * T), pt_hi).then_inc(pt_l, 1)

                def head(h, first, with_ada, late=False):
                    a = 2 * h + (A + 3 * GROUPS - (6 if late else 4))
                    g, g0 = G + L_HEAD + 2 * h, G + L_HEAD
                    ve.wait_ge(q_h, 3 * (8 * l + h) + 1)
                    ve.tensor_tensor(sc[:, 3 * T:4 * T], bank(0, T), rope[:, :], ALU.mult).then_inc(qr_rot, 1)
                    sub_hi(qn_lo, bank(0), qn_hi).then_inc(q_l, 1)
                    ve.wait_ge(q_h, 3 * (8 * l + h) + 2)
                    sub_hi(kn_lo, bank(1), kn_hi).then_inc(q_l, 1)
                    ve.wait_ge(q_h, 3 * (8 * l + h) + 3)
                    sub_hi(qr_lo, sc[:, 3 * T:4 * T], qr_hi).then_inc(q_l, 1)
                    if with_ada:
                        add_ada(a, 0)
                    split(g + 2, g0 % 2, halves=(0,))
                    if not first:
                        turned(h - 1)
                    split(g + 2, g0 % 2, halves=(1,))
                    if not first:
                        ve.wait_ge(o_ps, 8 * l + h)
                        ve.wait_ge(z_ready, 16 * l + GROUPS + h)
                        y_tile(GROUPS + h - 1, bank(4))
                        ve.wait_ge(y_mul, 16 * l + GROUPS + h)
                    gate(GROUPS + h, 2)
                    ve.wait_ge(v_h, 8 * l + h + 1)
                    sub_hi(vv_lo, bank(1, T), vv_hi).then_inc(v_l, 1)
                    after(g + 1, g0 + 1)
                    if not first:
                        y_rest(GROUPS + h - 1)
                    ve.wait_ge(s_ps, 8 * l + h + 1)
                    own.link(ve.tensor_reduce(stat[:, 0:2], bank(5, 0, 2 * T).rearrange("p (q k) -> p q k", q=2),
                                              AX.X, ALU.max))
                    ve.tensor_scalar(stat[:, 2:4], stat[:, 0:2], -SM_SCALE, None, ALU.mult).then_inc(s_max, 1)
                    ve.wait_ge(s_exp, 2 * (8 * l + h) + 2)
                    ve.reciprocal(stat[:, 6:8], stat[:, 4:6]).then_inc(s_sum, 1)
                    if with_ada:
                        add_ada(a + 1, 1)

                head(0, True, l == 0)
                with own.loop(1, HEADS - 2, 1) as h:
                    head(h, False, l == 0)
                head(HEADS - 2, False, False)
                if l == 0:
                    read_mod(3)
                head(HEADS - 1, False, l == 0, late=True)

                def out_tile(i, b, with_ada, with_sum=False):
                    g = G + L_OUT
                    m = 2 * i + b
                    ve.wait_ge(g_tmp, m + (16 * l + 1))
                    xm = X[:, bass.ds(m * T, T)]
                    ve.scalar_tensor_tensor(out=xm, in0=xm, scalar=ALPHA, in1=sc[:, b * T:(b + 1) * T],
                                            op0=ALU.mult, op1=ALU.add).then_inc(g_mul, 1)
                    ve.wait_ge(g_mul, m + (16 * l + 1))
                    own.link(ve.tensor_tensor(mu[:, :], mu[:, :], xm, ALU.add))
                    if with_sum:
                        ve.sem_inc(r_acc, 1)
                    after_ada(m + g, g + b, m + (A + 2 * KT + 2), b, with_ada)

                turned(HEADS - 1)
                ve.wait_ge(o_ps, 8 * (l + 1))
                ve.wait_ge(z_ready, 16 * (l + 1))
                y_tile(2 * HEADS - 1, bank(4))
                y_rest(2 * HEADS - 1)
                own.link(ve.memset(mu[:, :], 0.0))
                with own.loop(0, KT // 2 - 1, 2) as i:
                    for b in range(2):
                        out_tile(i, b, l == 0)
                for b in range(2):
                    out_tile(KT // 2 - 1, b, False, b == 1)
                centre(2 * l + 1)
                rstd(f"post{l}", [(rs[:, 0:T], bank(6, T), D)], 1e-6)
                if l == 0:
                    read_mod(4)

                def square_x(i):
                    ve.wait_ge(x_new, KT * l + 2 * i + 2)
                    s = slice(2 * i * T, (2 * i + 2) * T)
                    ve.tensor_tensor(wide[:, s], X[:, s], X[:, s], ALU.mult).then_inc(x_sq, 1)

                for i in range(KT // 2):
                    if i >= 2:
                        ve.wait_ge(x_new, KT * l + 2 * i - 2)
                    normed(i).then_inc(ln_app, 1)
                    if l and i:
                        square_x(i - 1)
                if l == 0:
                    centre(2)
                    rstd("pre1", [(rs[:, 0:T], bank(6, T), D)], 1e-6)
                    split_input(1, lambda i: normed(i).then_inc(in_norm, 1))
                else:
                    square_x(KT // 2 - 1)

            ve.wait_ge(x_stat, 2)
            rstd("mix", [(rs[:, 0:T], bank(6, T), D)], 1e-6)

            for i in range(KT // 2 + 1):
                if i >= 2:
                    ve.wait_ge(ln_lo, KT + i - 1)
                if i < KT // 2:
                    normed(i).then_inc(mix_norm, 1)
                if i:
                    ve.wait_ge(mix_norm, i)
                    for m in (2 * i - 2, 2 * i - 1):
                        ve.wait_ge(mix_hi, m + 1)
                        o = ve.scalar_tensor_tensor(out=a_tile(a_lo, m), in0=sc[:, (m % 4) * T:(m % 4 + 1) * T],
                                                    scalar=v("g_pre_mix", m), in1=a_tile(a_hi, m).bitcast(F32),
                                                    op0=ALU.mult, op1=ALU.subtract)
                    o.then_inc(ln_lo, 1)
            ahead = TAPS - 1 - META
            ve.wait_ge(ada_summed, 3 * DEPTH - 2)
            own.link(ve.memset(pad[:, 0:ahead], 0.0))

            def taps(j, lo, hi):
                for k in range(lo, hi):
                    w = v("w_dw", j * TAPS + k)
                    acc = mu[:, :] if k % 2 else conv_out[:, j * T:(j + 1) * T]
                    if k < 2:
                        o = ve.tensor_scalar(acc, pad[:, k:k + T], w, None, ALU.mult)
                    else:
                        o = ve.scalar_tensor_tensor(out=acc, in0=pad[:, k:k + T], scalar=w, in1=acc,
                                                    op0=ALU.mult, op1=ALU.add)
                    own.link(o, lag=1 if k < TAPS - 1 else 0)

            def pool_tile(j):
                ve.wait_ge(pl_in, j + 1)
                if j:
                    ve.wait_ge(pl_l, j)
                w = WINDOWS[j // 2]
                src, n, bufs = pool_z, 1, (pool_a, pool_b)
                while n < w:
                    to, first = bufs[0], 2 * n - 1
                    own.link(ve.tensor_tensor(to[:, first:TM], src[:, first:TM], src[:, first - n:TM - n], ALU.add))
                    src, n, bufs = to, 2 * n, bufs[::-1]
                ve.scalar_tensor_tensor(out=zs[:, :], in0=src[:, META:TM], scalar=1.0 / w, in1=pool_z[:, META:TM],
                                        op0=ALU.mult, op1=ALU.subtract).then_inc(pl_sum, 1)

            for j in range(CONV):
                g = B2_MIX + MIX * j
                if j:
                    ve.wait_ge(cv_done, j)
                after(g, g)
                ve.wait_ge(cv_tanh, j + 1)
                ve.scalar_tensor_tensor(out=pad[:, ahead:ahead + TM], in0=th[:, :], scalar=1.0, in1=bank(0, 0, TM),
                                        op0=ALU.add, op1=ALU.mult).then_inc(cv_in, 1)
                ve.wait_ge(cv_in, j + 1)
                after(g + 1, g + 1)
                taps(j, 0, 8)
                pool_tile(j)
                after(g + 2, g)
                taps(j, 8, 16)
                after(g + 3, g + 1)
                ve.wait_ge(pl_h, j + 1)
                s = slice(j * T, (j + 1) * T)
                sub_hi(y_lo[:, s], zs[:, :], y_hi[:, s]).then_inc(pl_l, 1)
                taps(j, 16, 24)
                if j < CONV - 1:
                    after(g + 4, g)
                taps(j, 24, TAPS)
                c = conv_out[:, j * T:(j + 1) * T]
                own.link(ve.tensor_tensor(c, c, mu[:, :], ALU.add))
                ve.tensor_scalar(c, c, 0.5, v("b_dw", j), ALU.mult, ALU.add).then_inc(cv_done, 1)
                if j == CONV - 1:
                    after(g + 4, g)
            for i, m in enumerate((0, 2, 4, 6, 1, 3, 5, 7)):
                ve.wait_ge(gp_h, i + 1)
                s = slice((CONV + m) * T, (CONV + m + 1) * T)
                ve.scalar_tensor_tensor(out=y_lo[:, s], in0=grp_ps(m), scalar=v("pool_scale", m),
                                        in1=y_hi[:, s].bitcast(F32), op0=ALU.mult, op1=ALU.subtract).then_inc(gp_l, 1)
            after(B2_GRP, B2_GRP)
            ve.wait_ge(cm_ps, 1)
            own.link(ve.tensor_scalar(mu[:, :], bank(6), 1.0 / (CONV * P), None, ALU.mult))
            for i in range(CONV // 2):
                s = tiles(conv_out[:, 2 * i * T:(2 * i + 2) * T], 2)
                ve.tensor_tensor(s, s, over_tokens(mu[:, :], 2), ALU.subtract).then_inc(cm_cent, 1)
                if i:
                    add_square(i - 1, rs[:, :], cm_sq, cm_sum)
            add_square(CONV // 2 - 1, rs[:, :], cm_sq, cm_sum)
            ve.wait_ge(cm_sum, CONV // 2)
            ve.tensor_tensor(zs[:, :], rs[:, 0:T], rs[:, T:2 * T], ALU.add).then_inc(cm_fold, 1)
            after(B2_GATE, B2_GATE)
            ve.wait_ge(cm_acc, 1)
            rstd("conv", [(rs[:, 0:T], bank(6, T), CONV * P)], 1e-5)
            for k in range(CONV + 2):
                if k < CONV:
                    c = conv_out[:, k * T:(k + 1) * T]
                    own.link(ve.tensor_tensor(c, c, rs[:, 0:T], ALU.mult))
                    ve.tensor_scalar(c, c, v("conv_ln_g", k), v("conv_ln_b", k), ALU.mult, ALU.add)\
                        .then_inc(cn_y, 1)
                if 1 <= k <= CONV:
                    c = conv_out[:, (k - 1) * T:k * T]
                    ve.wait_ge(cn_tanh, k)
                    ve.scalar_tensor_tensor(out=c, in0=cn_buf(k - 1), scalar=1.0, in1=c, op0=ALU.add,
                                            op1=ALU.mult).then_inc(cn_mul, 1)
                if k >= 2:
                    s = slice((k - 2) * T, (k - 1) * T)
                    ve.wait_ge(cn_h, k - 1)
                    ve.scalar_tensor_tensor(out=y_lo[:, s], in0=conv_out[:, s], scalar=0.5,
                                            in1=y_hi[:, s].bitcast(F32), op0=ALU.mult, op1=ALU.subtract)\
                        .then_inc(cn_l, 1)
                if k == 3:
                    after(B2_GATE + 1, B2_GATE + 1)

            def gate_b(i):
                for b in range(2):
                    after(B2_GATE + 4 * i + b, B2_GATE + b)

            def branches(i, b):
                g, g0 = B2_GATE + 4 * i + 2 + b, B2_GATE + b
                w = wide[:, bass.ds((2 * i + b) * T, T)]
                gb = sc[:, (2 + b) * T:(3 + b) * T]
                ve.wait_ge(gt_tanh, KT + 2)
                ve.wait_ge(weights_used, g + 1)
                ve.scalar_tensor_tensor(out=w, in0=w, scalar=1.0, in1=bank((0, 2)[b]), op0=ALU.add, op1=ALU.mult)
                own.link(ve.scalar_tensor_tensor(out=gb, in0=sc[:, b * T:(b + 1) * T], scalar=1.0,
                                                 in1=bank((1, 5)[b]), op0=ALU.add, op1=ALU.mult))
                ve.tensor_tensor(w, w, gb, ALU.add).then_inc(gt_done, 1)
                after(g, g0)

            branches(0, 0)
            branches(0, 1)
            with own.loop(1, KT // 2 - 1, 2) as i:
                gate_b(i)
                branches(i, 0)
                branches(i, 1)
            last = KT // 2 - 1
            gate_b(last)
            for i in range(KT // 2):
                if i == 3:
                    branches(last, 0)
                if i == last:
                    branches(last, 1)
                ve.wait_ge(mm_h, i + 1)
                to, hi = (t[:, i * 2 * TM:(i + 1) * 2 * TM].rearrange("p (k t) -> p k t", k=2)[:, :, META:TM]
                          for t in (a_lo, a_hi))
                ve.scalar_tensor_tensor(out=to, in0=tiles(wide[:, i * 2 * T:(i + 1) * 2 * T], 2), scalar=0.5,
                                        in1=hi.bitcast(F32), op0=ALU.mult, op1=ALU.subtract).then_inc(mm_l, 1)

            def wo_tile(i, b, first):
                m = 2 * i + b
                ve.wait_ge(wo_sq, m + 1)
                s = sc[:, b * T:(b + 1) * T]
                if first and b == 0:
                    ve.tensor_copy(mu[:, :], s).then_inc(wo_acc, 1)
                else:
                    ve.wait_ge(wo_acc, m)
                    ve.tensor_tensor(mu[:, :], mu[:, :], s, ALU.add).then_inc(wo_acc, 1)
                after(m + B2_WO, B2_WO + b)

            for b in range(2):
                wo_tile(0, b, True)
            with ve.Fori(1, KT // 2) as i:
                for b in range(2):
                    wo_tile(i, b, False)
            ve.wait_ge(wo_stat, 1)
            ve.wait_ge(wo_out, KT)
            rstd("wo", [(rs[:, 0:T], bank(6), D)], 1e-6)

            for i in range(KT // 2 + 1):
                if i < KT // 2:
                    xs, ws = (t[:, 2 * i * T:(2 * i + 2) * T] for t in (X, wide))
                    own.link(ve.tensor_tensor(tiles(ws, 2), tiles(ws, 2), over_tokens(rs[:, 0:T], 2), ALU.mult))
                    ve.tensor_tensor(xs, xs, ws, ALU.add).then_inc(h_new, 1)
                if i:
                    for m in (2 * i - 2, 2 * i - 1):
                        ve.wait_ge(h_hi, m + 1)
                        ve.wait_ge(h_new, m // 2 + 1)
                        ve.scalar_tensor_tensor(out=a_tile(a_lo, m), in0=X[:, m * T:(m + 1) * T],
                                                scalar=v("g_pre_mlp", m), in1=a_tile(a_hi, m).bitcast(F32),
                                                op0=ALU.mult, op1=ALU.subtract).then_inc(h_lo, 1)

            def up(f, i, b):
                m = 16 * f + 2 * i + b
                g = B2_FF + 32 * f + 2 * i + b
                r, s = sc[:, b * T:(b + 1) * T], sc[:, (2 + b) * T:(3 + b) * T]
                ve.wait_ge(f_relu, m + 1)
                ve.tensor_tensor(s, r, r, ALU.mult).then_inc(f_sq, 1)
                ve.wait_ge(f_sq, m + 1)
                ve.wait_ge(f_hi, m + 1)
                at = bass.ds((2 * i + b) * T, T)
                sub_hi(y_lo[:, at], s, y_hi[:, at]).then_inc(f_lo, 1)
                after(g, B2_FF + b)

            def down(f, i, b, last=False):
                m = 16 * f + 2 * i + b
                g = B2_FF + KT + 32 * f + 2 * i + b
                ve.wait_ge(weights_used, g + 1)
                o = wide[:, bass.ds((2 * i + b) * T, T)]
                if isinstance(f, int) and f == 0:
                    ve.tensor_copy(o, bank(2 + b)).then_inc(f_acc, 1)
                else:
                    ve.wait_ge(f_acc, m - 15)
                    ve.tensor_tensor(o, o, bank(2 + b), ALU.add).then_inc(f_acc, 1)
                if not last:
                    after(g, B2_FF + b)

            own.link(ve.memset(mu[:, :], 0.0))
            with own.loop(0, KT // 2, 2) as i:
                for b in range(2):
                    up(0, i, b)
                    ve.wait_ge(h_sq, 2 * i + b + 1)
                    own.link(ve.tensor_tensor(mu[:, :], mu[:, :], (zs[:, :], th[:, 0:T])[b], ALU.add))
                    ve.sem_inc(h_acc, 1)
            ve.wait_ge(h_stat, 1)
            own.link(ve.tensor_scalar(rs[:, 0:T], bank(6, T), 1.0 / D, 1e-6, ALU.mult, ALU.add))
            own.link(ve.reciprocal(rs[:, 0:T], rs[:, 0:T]))
            with ve.Fori(0, KT // 2) as i:
                for b in range(2):
                    down(0, i, b)
            with ve.Fori(1, FF_BLOCKS - 1) as f:
                with ve.Fori(0, KT // 2) as i:
                    for b in range(2):
                        up(f, i, b)
                with ve.Fori(0, KT // 2) as i:
                    for b in range(2):
                        down(f, i, b)
            f = FF_BLOCKS - 1
            with ve.Fori(0, KT // 2) as i:
                for b in range(2):
                    up(f, i, b)
            with ve.Fori(0, KT // 2 - 1) as i:
                for b in range(2):
                    down(f, i, b)
            for b in range(2):
                down(f, KT // 2 - 1, b, True)
            ve.wait_ge(f_osum, KT // 2)
            own.link(ve.tensor_tensor(mu[:, :], rs[:, 0:T], rs[:, 0:T], ALU.mult))
            own.link(ve.scalar_tensor_tensor(out=rs[:, T:2 * T], in0=bank(6), scalar=1.0 / D, in1=mu[:, :],
                                             op0=ALU.mult, op1=ALU.mult))
            ve.tensor_scalar(rs[:, T:2 * T], rs[:, T:2 * T], 1e-6, None, ALU.add).then_inc(ln_var, 1)
            ve.wait_ge(ln_std, NORM["out"] + 1)
            own.link(ve.reciprocal(rs[:, T:2 * T], rs[:, T:2 * T]))
            own.link(ve.tensor_tensor(rs[:, 0:T], rs[:, 0:T], rs[:, T:2 * T], ALU.mult))
            ve.wait_ge(f_acc, 16 * FF_BLOCKS)
            for m in range(KT):
                s = slice(m * T, (m + 1) * T)
                t = sc[:, (m % 4) * T:(m % 4 + 1) * T]
                own.link(ve.scalar_tensor_tensor(out=t, in0=wide[:, s], scalar=v("g_post_mlp", m),
                                                 in1=rs[:, 0:T], op0=ALU.mult, op1=ALU.mult))
                ve.tensor_tensor(X[:, s], X[:, s], t, ALU.add).then_inc(y_out, 1)


def by_tile(w):
    k, n = w.shape
    return w.reshape(k // P, P, n // P, P).transpose(2, 1, 0, 3).reshape(n // P, P, k)


def padded(chunks):
    out = np.zeros((chunks.shape[0], P, CH), np.float32)
    out[:, :, :chunks.shape[2]] = chunks
    return out


def columns(a):
    return np.asarray(a).reshape(-1, P).T


def swap_halves(w):
    h = ROPE // 2
    return np.concatenate([w[..., h:], w[..., :h]], axis=-1)


def dft(n):
    k = np.outer(np.arange(n), np.arange(n)) % n
    return (np.cos(2 * np.pi * k / n) / np.sqrt(n)), (np.sin(2 * np.pi * k / n) / np.sqrt(n))


def weight_stream(i):
    parts = []
    cos_s, sin_s = dft(T)
    cos_c, sin_c = dft(P)
    seq = np.concatenate([t.reshape(2, P, T).transpose(1, 0, 2).reshape(P, 2 * T) for t in (cos_s, -sin_s)], axis=1)
    seq = seq.astype(np.float32)
    chan = np.concatenate([cos_c, sin_c], axis=1).astype(np.float32)
    for l in range(DEPTH):
        w = np.asarray(i["w_in"][l])
        u, z, cq, ckv, kr, za = np.split(w, np.cumsum([1024, 1024, 512, 256, ROPE]), axis=1)
        parts.append(by_tile(np.concatenate([cq, ckv, kr, swap_halves(kr)], axis=1)))
        parts.append(padded(seq[None]))
        fm = np.asarray(i["w_fmix"][l]).transpose(1, 0, 2).reshape(P, GROUPS * P)
        parts.append(padded(np.concatenate([fm, chan], axis=1)[None]))
        parts.append(np.stack([by_tile(u), by_tile(z)], axis=1).reshape(2 * GROUPS, P, CH))
        wq = np.asarray(i["w_q_b"][l]).reshape(QT, P, HEADS, P + ROPE)
        wkv = np.asarray(i["w_kv_b"][l]).reshape(CT, P, HEADS, 2, P)
        nope, rp = wq[..., :P], wq[..., P:]
        rp = np.concatenate([rp, swap_halves(rp)], axis=-1)
        head = np.concatenate([nope, rp, wkv[:, :, :, 0], wkv[:, :, :, 1]], axis=0)
        head = head.transpose(2, 1, 0, 3).reshape(HEADS, P, 12 * P)
        parts.append(np.stack([padded(head), by_tile(za)], axis=1).reshape(2 * HEADS, P, CH))
        parts.append(by_tile(np.asarray(i["w_out"][l])))
    w = by_tile(np.asarray(i["w_in_2"][0]))
    z, val, gat, ga, gb = np.split(w, np.cumsum([CONV, CONV, CONV, KT]), axis=0)
    mix = np.concatenate([np.stack([val, gat, z], axis=1), ga.reshape(CONV, 2, P, CH)], axis=1)
    parts.append(mix.reshape(MIX * CONV, P, CH))
    grp = np.asarray(i["w_pool_grp_2"][0]).reshape(4, 2, P, 2, P)
    parts.append(grp.transpose(2, 0, 3, 1, 4).reshape(1, P, CH))
    po, co = (np.asarray(i[n][0]).reshape(CONV, P, KT, P).transpose(2, 1, 0, 3).reshape(KT, P, HALF)
              for n in ("w_pool_out_2", "w_conv_out_2"))
    branch = np.concatenate([po, co], axis=2).reshape(KT // 2, 2, P, CH)
    parts.append(np.concatenate([gb.reshape(KT // 2, 2, P, CH), branch], axis=1).reshape(2 * KT, P, CH))
    parts.append(by_tile(np.asarray(i["w_o_2"][0])))
    up = by_tile(np.asarray(i["w_up_2"][0])).reshape(FF_BLOCKS, KT, P, CH)
    down = np.asarray(i["w_down_2"][0]).reshape(FF_BLOCKS, KT, P, KT, P).transpose(0, 3, 2, 1, 4)
    parts.append(np.concatenate([up, down.reshape(FF_BLOCKS, KT, P, CH)], axis=1).reshape(-1, P, CH))
    return np.concatenate(parts, axis=0)


def kernel(**i):
    import concourse.bacc as bacc
    from concourse.bass_utils import run_bass_kernel_spmd

    def f32(name):
        return np.asarray(i[name])

    stream = weight_stream(i)
    assert stream.shape == (CHUNKS, P, CH), stream.shape
    ada = f32("w_ada").reshape(DEPTH, KT, P, 3, D).transpose(0, 3, 1, 2, 4).reshape(ADA, P, D)[ADA0:]
    ada0 = f32("w_ada")[0].reshape(4, 4, P, 3, 4, 512)[:, :, :, :2].transpose(4, 3, 0, 2, 1, 5)
    ada0 = ada0.reshape(ADA0, P, CH)
    taps = f32("w_dw_2")[0].reshape(TAPS, CONV, P).transpose(1, 0, 2)
    named = {"c": f32("c"), "b_ada": f32("b_ada"), "q_norm": f32("q_norm"), "kv_norm": f32("kv_norm"),
             "ln_g": f32("ln_g"), "ln_b": f32("ln_b"), "g_pre_mix": f32("g_pre_mix_2"),
             "pool_scale": f32("pool_scale_2"), "w_dw": taps, "b_dw": f32("b_dw_2"),
             "conv_ln_g": f32("conv_ln_g_2"), "conv_ln_b": f32("conv_ln_b_2"),
             "g_post_mix": f32("g_post_mix_2"), "g_pre_mlp": f32("g_pre_mlp_2"), "g_post_mlp": f32("g_post_mlp_2")}
    vectors = np.concatenate([columns(named[n]) for n, _ in VECTORS], axis=1)
    p = np.arange(P)
    freq = np.float32(10000.0) ** (-np.arange(0, ROPE, 2, dtype=np.float32) / np.float32(ROPE))
    consts = np.concatenate([
        np.eye(P), (p[:, None] % ROPE == p[None] % ROPE), freq[p % (ROPE // 2)][:, None],
        np.where(p < ROPE, np.pi / 2, 0.0)[:, None],
        np.where((p >= ROPE) & (p < ROPE + ROPE // 2), -1.0, 1.0)[:, None]], axis=1).astype(np.float32)
    positions = np.ascontiguousarray(np.broadcast_to(np.asarray(i["positions"]).astype(np.int32), (P, T)))
    x = f32("x")[0].reshape(T, KT, P).transpose(2, 1, 0).reshape(P, KT * T)
    meta = f32("meta_2").reshape(META, KT, P).transpose(2, 1, 0).reshape(P, KT * META)
    arrays = {"stream": stream, "ada0": ada0, "ada": ada, "vectors": vectors, "consts": consts, "positions": positions,
              "x": x, "meta": meta}
    nc = bacc.Bacc("TRN2", target_bir_lowering=False, num_devices=1)
    aps = {}
    for name, a in arrays.items():
        arrays[name] = a = np.ascontiguousarray(a)
        aps[name] = nc.dram_tensor(f"in_{name}", a.shape, mybir.dt.from_np(a.dtype), kind="ExternalInput").ap()
    out = nc.dram_tensor("out", (P, KT * T), F32, kind="ExternalOutput").ap()
    build(nc, **aps, out=out)
    r = run_bass_kernel_spmd(nc, [{f"in_{n}": a for n, a in arrays.items()}], core_ids=[0])
    y = np.asarray(r.results[0]["out"])
    return y.reshape(P, KT, T).transpose(2, 1, 0).reshape(1, T, D)
```
